# Optimizing a Trainium2 kernel written in Bass

```python
import math
import jax, jax.numpy as jnp
from jax import lax
import numpy as np

D_MODEL = 1024
BATCH = 1
SEQ = 256
DEPTH = 1
DEC_BATCH = 8
DEC_SEQ = 8
PAST_LEN = 1024
PAGE_SIZE = 128

HEAD_DIM = 64
N_FOX_HEADS = 8
N_MOBA_HEADS = 8
FOX_WIDTH = N_FOX_HEADS * HEAD_DIM
MOBA_WIDTH = N_MOBA_HEADS * HEAD_DIM
IN_WIDTH = 3 * FOX_WIDTH + N_FOX_HEADS + 3 * MOBA_WIDTH
FOX_QBLOCK = 128
MOBA_BLOCK = 256
MOBA_TOPK = 3
MOBA_QCHUNK = 16
T5_BUCKETS = 32
T5_MAX_DIST = 128
N_GROUPS = 4
EXPERTS_PER_GROUP = 8
N_EXPERTS = N_GROUPS * EXPERTS_PER_GROUP
TOPK_IN_GROUP = 2
D_EXPERT = D_MODEL // 4
MOE_ROW_BLOCK = 128
RMS_EPS = 1e-6

kernel_name = 'hymba_fox_moba_hmoe_decode_step'

def rmsnorm(x, g):
    xf = x.astype(jnp.float32)
    y = xf * lax.rsqrt(jnp.mean(xf * xf, axis=-1, keepdims=True) + RMS_EPS)
    return (y * g.astype(jnp.float32)).astype(x.dtype)

def ada_modulation(c, w_ada, b_ada):
    m = jnp.einsum('bd,de->be', jax.nn.silu(c), w_ada) + b_ada
    return jnp.split(m[:, None, :], 6, axis=-1)

def modulate(h, shift, scale):
    return h * (1.0 + scale) + shift

def masked_softmax(s, mask):
    return jax.nn.softmax(jnp.where(mask, s.astype(jnp.float32), -jnp.inf), axis=-1)

def t5_bucket(rel):
    max_exact = T5_BUCKETS // 2
    rel = jnp.maximum(rel, 0)
    relf = jnp.maximum(rel, 1).astype(jnp.float32)
    large = max_exact + (jnp.log(relf / max_exact) / math.log(T5_MAX_DIST / max_exact)
                         * (T5_BUCKETS - max_exact)).astype(jnp.int32)
    large = jnp.minimum(large, T5_BUCKETS - 1)
    return jnp.where(rel < max_exact, rel, large)

def project(h, w_in, b_forget):
    B, S, _ = h.shape
    z = jnp.einsum('bsd,de->bse', h, w_in)
    widths = [FOX_WIDTH] * 3 + [N_FOX_HEADS] + [MOBA_WIDTH] * 3
    cuts = [int(c) for c in np.cumsum(widths)[:-1]]
    fq, fk, fv, fg, mq, mk, mv = jnp.split(z, cuts, axis=-1)
    logf = jax.nn.log_sigmoid(fg.astype(jnp.float32) + b_forget.astype(jnp.float32))
    hf = lambda t: t.reshape(B, S, N_FOX_HEADS, HEAD_DIM)
    hm = lambda t: t.reshape(B, S, N_MOBA_HEADS, HEAD_DIM)
    return hf(fq), hf(fk), hf(fv), logf, hm(mq), hm(mk), hm(mv)

def fox_attend(q, k, v, fq, fk, q_pos, k_pos):
    s = jnp.einsum('bqhd,bthd->bhqt', q, k).astype(jnp.float32) * HEAD_DIM ** -0.5
    s = s + fq[..., :, None] - fk[..., None, :]
    p = masked_softmax(s, k_pos[None, :] <= q_pos[:, None])
    return jnp.einsum('bhqt,bthd->bqhd', p.astype(v.dtype), v)

def fox_prompt(q, k, v, logf):
    B, S, H, Dh = q.shape
    F = jnp.cumsum(logf, axis=1).transpose(0, 2, 1)
    pos = jnp.arange(S, dtype=jnp.int32)
    nqb = S // FOX_QBLOCK
    q_blk = q.reshape(B, nqb, FOX_QBLOCK, H, Dh).transpose(1, 0, 2, 3, 4)
    f_blk = F.reshape(B, H, nqb, FOX_QBLOCK).transpose(2, 0, 1, 3)
    p_blk = pos.reshape(nqb, FOX_QBLOCK)
    out = lax.map(lambda a: fox_attend(a[0], k, v, a[1], F, a[2], pos), (q_blk, f_blk, p_blk))
    return out.transpose(1, 0, 2, 3, 4).reshape(B, S, H * Dh)

def fox_sample(q, k, v, logf, cache_k, cache_v, cache_logf, page_table):
    DB, DS, H, Dh = q.shape
    past_k = cache_k[page_table].reshape(DB, -1, H, Dh)
    past_v = cache_v[page_table].reshape(DB, -1, H, Dh)
    past_l = cache_logf[page_table].reshape(DB, -1, H)
    past_len = past_k.shape[1]
    k_all = jnp.concatenate([past_k, k], axis=1)
    v_all = jnp.concatenate([past_v, v], axis=1)
    F = jnp.cumsum(jnp.concatenate([past_l.astype(jnp.float32), logf], axis=1), axis=1).transpose(0, 2, 1)
    k_pos = jnp.arange(past_len + DS, dtype=jnp.int32)
    q_pos = k_pos[past_len:]
    out = fox_attend(q, k_all, v_all, F[..., past_len:], F, q_pos, k_pos)
    return out.reshape(DB, DS, H * Dh)

def pad_to_blocks(t, n_blocks):
    pad = n_blocks * MOBA_BLOCK - t.shape[1]
    return jnp.pad(t, ((0, 0), (0, pad), (0, 0), (0, 0)))

def block_means(k_pad):
    B, T, H, Dh = k_pad.shape
    kb = k_pad.reshape(B, T // MOBA_BLOCK, MOBA_BLOCK, H, Dh).astype(jnp.float32)
    return kb.mean(axis=2).astype(k_pad.dtype)

def moba_attend(q, q_pos, k_pad, v_pad, k_mean, t5_bias):
    B, Q, H, Dh = q.shape
    NB = k_mean.shape[1]
    n_sel = min(MOBA_TOPK, NB)
    own = (q_pos // MOBA_BLOCK).astype(jnp.int32)
    gate = jnp.einsum('bqhd,bnhd->bhqn', q, k_mean).astype(jnp.float32)
    gate = jnp.where(jnp.arange(NB)[None, :] < own[:, None], gate, -jnp.inf)
    _, sel = lax.top_k(gate, n_sel)
    sel_ok = jnp.arange(n_sel)[None, :] < own[:, None]
    blk = jnp.concatenate([sel.astype(jnp.int32),
                           jnp.broadcast_to(own[:, None], (B, H, Q, 1))], axis=-1)
    blk_ok = jnp.concatenate([jnp.broadcast_to(sel_ok, (B, H, Q, n_sel)),
                              jnp.ones((B, H, Q, 1), dtype=bool)], axis=-1)
    ns = blk.shape[-1]
    kb = k_pad.reshape(B, NB, MOBA_BLOCK, H, Dh)
    vb = v_pad.reshape(B, NB, MOBA_BLOCK, H, Dh)
    bi = jnp.arange(B)[:, None, None, None]
    hi = jnp.arange(H)[None, :, None, None]
    kg = kb[bi, blk, :, hi]
    vg = vb[bi, blk, :, hi]
    key_pos = blk[..., None] * MOBA_BLOCK + jnp.arange(MOBA_BLOCK, dtype=jnp.int32)
    rel = q_pos[:, None, None] - key_pos
    mask = blk_ok[..., None] & (rel >= 0)
    bias = t5_bias.T[hi[..., None], t5_bucket(rel)].astype(jnp.float32)
    s = jnp.einsum('bqhd,bhqnkd->bhqnk', q, kg).astype(jnp.float32) * HEAD_DIM ** -0.5 + bias
    p = masked_softmax(s.reshape(B, H, Q, ns * MOBA_BLOCK), mask.reshape(B, H, Q, ns * MOBA_BLOCK))
    return jnp.einsum('bhqm,bhqmd->bqhd', p.astype(vg.dtype),
                      vg.reshape(B, H, Q, ns * MOBA_BLOCK, Dh))

def moba_prompt(q, k, v, t5_bias):
    B, S, H, Dh = q.shape
    nb = -(-S // MOBA_BLOCK)
    k_pad = pad_to_blocks(k, nb)
    v_pad = pad_to_blocks(v, nb)
    k_mean = block_means(k_pad)
    nqc = S // MOBA_QCHUNK
    q_c = q.reshape(B, nqc, MOBA_QCHUNK, H, Dh).transpose(1, 0, 2, 3, 4)
    p_c = jnp.arange(S, dtype=jnp.int32).reshape(nqc, MOBA_QCHUNK)
    out = lax.map(lambda a: moba_attend(a[0], a[1], k_pad, v_pad, k_mean, t5_bias), (q_c, p_c))
    return out.transpose(1, 0, 2, 3, 4).reshape(B, S, H * Dh)

def moba_sample(q, k, v, cache_k, cache_v, page_table, t5_bias):
    DB, DS, H, Dh = q.shape
    past_k = cache_k[page_table].reshape(DB, -1, H, Dh)
    past_v = cache_v[page_table].reshape(DB, -1, H, Dh)
    past_len = past_k.shape[1]
    nb = -(-(past_len + DS) // MOBA_BLOCK)
    k_pad = pad_to_blocks(jnp.concatenate([past_k, k], axis=1), nb)
    v_pad = pad_to_blocks(jnp.concatenate([past_v, v], axis=1), nb)
    q_pos = past_len + jnp.arange(DS, dtype=jnp.int32)
    out = moba_attend(q, q_pos, k_pad, v_pad, block_means(k_pad), t5_bias)
    return out.reshape(DB, DS, H * Dh)

def merge_groups(o_fox, o_moba, g_fox, g_moba, w_out):
    o = jnp.concatenate([rmsnorm(o_fox, g_fox), rmsnorm(o_moba, g_moba)], axis=-1)
    return jnp.einsum('bse,ed->bsd', o, w_out)

def grouped_expert_mlp(h, expert_id, weight, w1, w3, w2):
    N, D = h.shape
    A = N * TOPK_IN_GROUP
    flat_e = expert_id.reshape(A).astype(jnp.int32)
    flat_tok = jnp.arange(A, dtype=jnp.int32) // TOPK_IN_GROUP
    flat_w = weight.reshape(A)
    order = jnp.argsort(flat_e)
    e_sorted = flat_e[order]
    tok_sorted = flat_tok[order]
    counts = jnp.bincount(flat_e, length=N_EXPERTS)
    start = jnp.cumsum(counts) - counts
    padded = (counts + MOE_ROW_BLOCK - 1) // MOE_ROW_BLOCK * MOE_ROW_BLOCK
    pend = jnp.cumsum(padded)
    pstart = pend - padded
    dest = pstart[e_sorted] + (jnp.arange(A, dtype=jnp.int32) - start[e_sorted])
    n_blocks = -(-(A + N_EXPERTS * (MOE_ROW_BLOCK - 1)) // MOE_ROW_BLOCK)
    rows = jnp.zeros((n_blocks * MOE_ROW_BLOCK, D), h.dtype).at[dest].set(h[tok_sorted])
    block_e = jnp.clip(jnp.searchsorted(pend, jnp.arange(n_blocks) * MOE_ROW_BLOCK, side='right'),
                       0, N_EXPERTS - 1)

    def block_mlp(a):
        xb, e = a
        return (jax.nn.silu(xb @ w1[e]) * (xb @ w3[e])) @ w2[e]

    y = lax.map(block_mlp, (rows.reshape(n_blocks, MOE_ROW_BLOCK, D), block_e)).reshape(-1, D)
    contrib = y[dest] * flat_w[order][:, None].astype(y.dtype)
    return jnp.zeros((N, D), y.dtype).at[tok_sorted].add(contrib)

def hier_moe(h, w_rg, b_rg, w_re, b_re, w1, w3, w2):
    N = h.shape[0]
    hf = h.astype(jnp.float32)
    g_logits = jnp.einsum('nd,dg->ng', hf, w_rg.astype(jnp.float32)) + b_rg.astype(jnp.float32)
    g_prob = jax.nn.softmax(g_logits, axis=-1)
    g_idx = jnp.argmax(g_logits, axis=-1)
    g_w = jnp.take_along_axis(g_prob, g_idx[:, None], axis=-1)
    e_logits = (jnp.einsum('nd,de->ne', hf, w_re.astype(jnp.float32)) + b_re.astype(jnp.float32))
    e_logits = jnp.take_along_axis(e_logits.reshape(N, N_GROUPS, EXPERTS_PER_GROUP),
                                   g_idx[:, None, None], axis=1)[:, 0]
    top_p, top_i = lax.top_k(jax.nn.softmax(e_logits, axis=-1), TOPK_IN_GROUP)
    top_p = top_p / jnp.sum(top_p, axis=-1, keepdims=True)
    expert_id = g_idx[:, None].astype(jnp.int32) * EXPERTS_PER_GROUP + top_i
    return grouped_expert_mlp(h, expert_id, g_w * top_p, w1, w3, w2)

def ffn_sublayer(x, shift, scale, gate, g, w_rg, b_rg, w_re, b_re, w1, w3, w2):
    B, S, D = x.shape
    h = modulate(rmsnorm(x, g), shift, scale)
    y = hier_moe(h.reshape(B * S, D), w_rg, b_rg, w_re, b_re, w1, w3, w2).reshape(B, S, D)
    return x + gate * y

def setup_inputs(seed: int = 0) -> dict:
    key = jax.random.key(seed)
    ks = jax.random.split(key, 32)
    D = D_MODEL
    n_pages = PAST_LEN // PAGE_SIZE
    n_used = DEC_BATCH * n_pages
    n_phys = (5 * n_used + 3) // 4
    nrm = lambda k, shape, s=1.0: s * jax.random.normal(k, shape, jnp.float32)
    page_table = jax.random.permutation(ks[7], n_phys)[:n_used].reshape(DEC_BATCH, n_pages).astype(jnp.int32)
    b_forget = jnp.broadcast_to(jnp.linspace(1.0, 5.0, N_FOX_HEADS), (DEPTH, N_FOX_HEADS)) \
        + nrm(ks[14], (DEPTH, N_FOX_HEADS), 0.1)
    return {
        'x_prompt': nrm(ks[0], (BATCH, SEQ, D)),
        'x_sample': nrm(ks[1], (DEC_BATCH, DEC_SEQ, D)),
        'cache_fox_k': nrm(ks[2], (DEPTH, n_phys, PAGE_SIZE, N_FOX_HEADS, HEAD_DIM)),
        'cache_fox_v': nrm(ks[3], (DEPTH, n_phys, PAGE_SIZE, N_FOX_HEADS, HEAD_DIM)),
        'cache_fox_logf': jax.nn.log_sigmoid(3.0 + nrm(ks[4], (DEPTH, n_phys, PAGE_SIZE, N_FOX_HEADS))),
        'cache_moba_k': nrm(ks[5], (DEPTH, n_phys, PAGE_SIZE, N_MOBA_HEADS, HEAD_DIM)),
        'cache_moba_v': nrm(ks[6], (DEPTH, n_phys, PAGE_SIZE, N_MOBA_HEADS, HEAD_DIM)),
        'page_table': page_table,
        'c_prompt': nrm(ks[8], (BATCH, D)),
        'c_sample': nrm(ks[9], (DEC_BATCH, D)),
        'w_ada': nrm(ks[10], (DEPTH, D, 6 * D), 0.5 * D ** -0.5),
        'b_ada': nrm(ks[11], (DEPTH, 6 * D), 0.02),
        'g_attn': 1.0 + nrm(ks[12], (DEPTH, D), 0.02),
        'w_in': nrm(ks[13], (DEPTH, D, IN_WIDTH), D ** -0.5),
        'b_forget': b_forget,
        'g_out_fox': 1.0 + nrm(ks[15], (DEPTH, FOX_WIDTH), 0.02),
        'g_out_moba': 1.0 + nrm(ks[16], (DEPTH, MOBA_WIDTH), 0.02),
        't5_bias': nrm(ks[17], (T5_BUCKETS, N_MOBA_HEADS), 0.3),
        'w_out': nrm(ks[18], (DEPTH, D, D), D ** -0.5),
        'g_ffn': 1.0 + nrm(ks[19], (DEPTH, D), 0.02),
        'w_router_group': nrm(ks[20], (DEPTH, D, N_GROUPS), D ** -0.5),
        'b_router_group': nrm(ks[21], (DEPTH, N_GROUPS), 0.01),
        'w_router_expert': nrm(ks[22], (DEPTH, D, N_EXPERTS), D ** -0.5),
        'b_router_expert': nrm(ks[23], (DEPTH, N_EXPERTS), 0.01),
        'w1': nrm(ks[24], (DEPTH, N_EXPERTS, D, D_EXPERT), D ** -0.5),
        'w3': nrm(ks[25], (DEPTH, N_EXPERTS, D, D_EXPERT), D ** -0.5),
        'w2': nrm(ks[26], (DEPTH, N_EXPERTS, D_EXPERT, D), D_EXPERT ** -0.5),
        'g_final': 1.0 + nrm(ks[27], (D,), 0.02),
    }

def reference(x_prompt, x_sample, cache_fox_k, cache_fox_v, cache_fox_logf, cache_moba_k, cache_moba_v,
              page_table, c_prompt, c_sample, w_ada, b_ada, g_attn, w_in, b_forget, g_out_fox, g_out_moba,
              t5_bias, w_out, g_ffn, w_router_group, b_router_group, w_router_expert, b_router_expert,
              w1, w3, w2, g_final):
    xp, xs = x_prompt, x_sample
    p_fk, p_fv, p_fl, p_mk, p_mv = [], [], [], [], []
    s_fk, s_fv, s_fl, s_mk, s_mv = [], [], [], [], []
    for l in range(DEPTH):
        mp = ada_modulation(c_prompt, w_ada[l], b_ada[l])
        ms = ada_modulation(c_sample, w_ada[l], b_ada[l])
        hp = modulate(rmsnorm(xp, g_attn[l]), mp[0], mp[1])
        fq, fk, fv, fl, mq, mk, mv = project(hp, w_in[l], b_forget[l])
        o = merge_groups(fox_prompt(fq, fk, fv, fl), moba_prompt(mq, mk, mv, t5_bias),
                         g_out_fox[l], g_out_moba[l], w_out[l])
        xp = xp + mp[2] * o
        p_fk.append(fk); p_fv.append(fv); p_fl.append(fl); p_mk.append(mk); p_mv.append(mv)
        hs = modulate(rmsnorm(xs, g_attn[l]), ms[0], ms[1])
        fq, fk, fv, fl, mq, mk, mv = project(hs, w_in[l], b_forget[l])
        o_fox = fox_sample(fq, fk, fv, fl, cache_fox_k[l], cache_fox_v[l], cache_fox_logf[l], page_table)
        o_moba = moba_sample(mq, mk, mv, cache_moba_k[l], cache_moba_v[l], page_table, t5_bias)
        xs = xs + ms[2] * merge_groups(o_fox, o_moba, g_out_fox[l], g_out_moba[l], w_out[l])
        s_fk.append(fk); s_fv.append(fv); s_fl.append(fl); s_mk.append(mk); s_mv.append(mv)
        xp = ffn_sublayer(xp, mp[3], mp[4], mp[5], g_ffn[l], w_router_group[l], b_router_group[l],
                          w_router_expert[l], b_router_expert[l], w1[l], w3[l], w2[l])
        xs = ffn_sublayer(xs, ms[3], ms[4], ms[5], g_ffn[l], w_router_group[l], b_router_group[l],
                          w_router_expert[l], b_router_expert[l], w1[l], w3[l], w2[l])
    y_prompt = rmsnorm(xp, g_final)
    y_sample = rmsnorm(xs, g_final)
    new_fox_k_prompt = jnp.stack(p_fk)
    new_fox_v_prompt = jnp.stack(p_fv)
    new_fox_logf_prompt = jnp.stack(p_fl)
    new_moba_k_prompt = jnp.stack(p_mk)
    new_moba_v_prompt = jnp.stack(p_mv)
    new_fox_k_sample = jnp.stack(s_fk)
    new_fox_v_sample = jnp.stack(s_fv)
    new_fox_logf_sample = jnp.stack(s_fl)
    new_moba_k_sample = jnp.stack(s_mk)
    new_moba_v_sample = jnp.stack(s_mv)
    return (y_prompt, y_sample, new_fox_k_prompt, new_fox_v_prompt, new_fox_logf_prompt,
            new_moba_k_prompt, new_moba_v_prompt, new_fox_k_sample, new_fox_v_sample,
            new_fox_logf_sample, new_moba_k_sample, new_moba_v_sample)


_drawn_inputs = setup_inputs


def setup_inputs(seed=0):
    import zlib

    import numpy as np

    out = dict(_drawn_inputs(seed))
    spreads = {}
    factors = {'g_attn': 2.99,
     'g_out_fox': 8.0,
     'g_out_moba': 8.0,
     'g_ffn': 4.374,
     'b_router_group': 8.0,
     'b_router_expert': 6.949,
     'g_final': 3.087}
    for name, (base, spread) in spreads.items():
        noise = np.random.default_rng([zlib.crc32(name.encode()), seed]).standard_normal(out[name].shape)
        drawn = base * np.exp(spread * noise) if base else spread * noise
        out[name] = __import__('jax').numpy.asarray(drawn.astype(out[name].dtype))
    for name, factor in factors.items():
        out[name] = (out[name] * factor).astype(out[name].dtype)
    return out
```

```python
from contextlib import ExitStack

import numpy as np

import concourse.bass as bass
from concourse import mybir

F32 = mybir.dt.float32
I32 = mybir.dt.int32
U32 = mybir.dt.uint32
ALU = mybir.AluOpType
ACT = mybir.ActivationFunctionType
AX = mybir.AxisListType

P = 128
D = 1024
KC = D // P
NP = 256
NB = 8
NQ = 8
NS = NB * NQ
NT = NP + NS
TILES = [(0, P), (P, P), (2 * P, NS)]
H = 8
HD = 64
W = H * HD
PC = W // P
PAGES = 8
PAGE = 128
NSEQ = NB + 1
NEG = -1.0e30
EPS = 1e-6
NG, EPG = 4, 8
NE = NG * EPG
DE = 256
FC = DE // P
BLK = 64
ASSIGN = 2 * NT
SORTED = ASSIGN + BLK
MAXOV = (ASSIGN - 1) // BLK
BUCKETS = 32
MOD_SHIFT1, MOD_SCALE1, MOD_GATE1, MOD_SHIFT2, MOD_SCALE2, MOD_GATE2 = range(6)

CONST = {}
_at = 0
for _n, _w in [("ident", P), ("ones", P), ("half0", P), ("half1", P), ("causal", 2 * P), ("before", P),
               ("block_id", 2), ("block_no", 4), ("iota32", NE), ("iota_ov", MAXOV),
               ("suf_lo", P), ("suf_same", P), ("suf_page", P), ("own_mask", NS), ("neg_prefix", NS)]:
    if _n == "suf_lo":
        NCONST = _at
    CONST[_n] = (_at, _at + _w)
    _at += _w
NEARLY = _at - NCONST
REV = 256
FWD = 144
WROW = 384 + NQ + FWD


def make_constants():
    c = np.zeros((P, NCONST + NEARLY), np.float32)
    k, m = np.arange(P)[:, None], np.arange(P)[None, :]

    def put(name, v):
        a, b = CONST[name]
        c[:, a:b] = v

    put("ident", k == m)
    put("ones", 1.0)
    put("suf_lo", (k // 32 == m // 32) & (k > m))
    put("suf_same", k // 32 == m // 32)
    put("suf_page", k // 32 > m // 32)
    put("half0", (k < 64) & (m >= 0))
    put("half1", (k >= 64) & (m >= 0))
    put("causal", np.where(np.arange(2 * P)[None, :] <= P + k, 0.0, NEG))
    j, q = np.arange(P)[:, None], np.arange(NS)[None, :]
    put("own_mask", np.where((j // NQ == q // NQ) & (j <= q), 0.0, NEG))
    put("neg_prefix", np.where((j // NQ == q // NQ) & (j <= q), -1.0, 0.0))
    put("before", k < m)
    put("block_id", 2 * np.arange(2)[None, :] + k // 64 + 1)
    put("block_no", np.array([[1, 3, 2, 4]]))
    put("iota32", np.arange(NE)[None, :])
    put("iota_ov", np.arange(MAXOV)[None, :])
    return c


def make_distance_onehot():
    dist = np.concatenate([REV - 1 - np.arange(REV), np.arange(FWD)])
    half = BUCKETS // 2
    large = half + (np.log(np.maximum(dist, 1).astype(np.float32) / half) / np.float32(np.log(P / half))
                    * half).astype(np.int32)
    bucket = np.where(dist < half, dist, np.minimum(large, BUCKETS - 1))
    return (np.arange(BUCKETS)[:, None] == bucket[None, :]).astype(np.float32)


def make_sequence_onehot():
    seq = np.concatenate([np.zeros(NP, int), 1 + np.arange(NS) // NQ])
    return (np.arange(NSEQ)[:, None] == seq[None, :]).astype(np.float32)


def trunk_kernel(nc, ins, outs):
    (x_prompt, x_sample, cache_fox_k, cache_fox_v, cache_fox_logf, cache_moba_k, cache_moba_v, page_table,
     c_prompt, c_sample, w_ada, b_ada, g_attn, w_in, b_forget, g_out_fox, g_out_moba, t5_bias, w_out, g_ffn,
     w_rg, b_rg, w_re, b_re, w1, w3, w2, g_final, consts, dist_onehot, seq_onehot) = ins
    (y_prompt, y_sample, o_fk_p, o_fv_p, o_fl_p, o_mk_p, o_mv_p, o_fk_s, o_fv_s, o_fl_s, o_mk_s, o_mv_s) = outs
    n_phys = cache_fox_k.shape[1]
    cache_k, cache_v = [cache_fox_k, cache_moba_k], [cache_fox_v, cache_moba_v]

    scr_f = nc.dram_tensor("scr_f", (H, NP), F32).ap()
    scr_w = nc.dram_tensor("scr_w", (H, P, WROW), F32).ap()
    scr_y = nc.dram_tensor("scr_y", ((NE + MAXOV) * BLK, D), F32).ap()

    with ExitStack() as ctx:
        def sb(name, shape, dt=F32):
            return ctx.enter_context(nc.sbuf_tensor(name, shape, dt))

        def sem(name):
            return ctx.enter_context(nc.semaphore(name))

        RS = 3
        SLOT = 8 * D
        ES = 4
        ESLOT = 2 * KC * DE + FC * D
        ring = sb("ring", [P, RS * SLOT])
        slot = [ring[:, i * SLOT:(i + 1) * SLOT] for i in range(RS)]
        eplace = [0, 3, 1, 2]
        eslot = [ring[:, i * ESLOT:(i + 1) * ESLOT] for i in eplace]
        w13_of = [s[:, 0:2 * KC * DE].rearrange("p (k n) -> p k n", k=KC) for s in eslot]
        w2_of = [s[:, 2 * KC * DE:].rearrange("p (k n) -> p k n", k=FC) for s in eslot]

        work = sb("work", [P, 19456])
        early = work[:, 13824:13824 + NEARLY]
        xh = sb("xh", [P, 2 * KC * NT])
        xT = xh[:, 0:KC * NT].rearrange("p (k t) -> p k t", k=KC)
        hT = xh[:, KC * NT:].rearrange("p (k t) -> p k t", k=KC)
        oT = hT
        cst = sb("cst", [P, NCONST])

        def const(name, rows=P):
            a, b = CONST[name]
            return cst[0:rows, a:b] if a < NCONST else early[0:rows, a - NCONST:b - NCONST]

        ident, ones = const("ident"), const("ones")
        modT = sb("modT", [P, 6 * KC, NSEQ])
        parT = sb("parT", [P, 72])
        wfg = sb("wfg", [P, KC, H])
        wr = sb("wr", [P, KC, NG + NE])
        brow = sb("brow", [P, NG + NE])
        bfg = sb("bfg", [H, 1])
        t5 = sb("t5", [BUCKETS, H])
        t5_far = sb("t5_far", [P, H])
        rstd = sb("rstd", [P, NT])
        lfT = sb("lfT", [H, NT])
        lft = sb("lft", [P, 3, H])
        table = sb("table", [1, NB * PAGES], I32)

        def region(a, n):
            return work[:, a:a + n]

        qkT = region(0, 16 * NT).rearrange("p (c t) -> p c t", c=16)
        v_tok = region(5120, 6 * W).rearrange("p (g t n) -> p g t n", g=2, t=3)
        q_rep = region(8192, 2 * D).rearrange("p (g b h e i) -> p g b h e i", g=2, b=NB, h=H, e=2)
        kt = [region(at, 4096).rearrange("p (q n) -> p q n", q=2) for at in (10240, 1024)]
        s_nat = region(0, 512)
        o_nat = region(512, P)
        k_out = region(10240, 6 * W).rearrange("p (g t n) -> p g t n", g=2, t=3)
        fox_tab = region(10240, H * NP).rearrange("p (h t) -> p h t", h=H)
        pr_s = region(12288, 2 * 384).rearrange("p (a n) -> p a n", a=2)
        pr_pt = region(13056, 2 * 384).rearrange("p (a n) -> p a n", a=2)
        moba_tab = region(14336, H * NP).rearrange("p (h t) -> p h t", h=H)
        s_tile = region(14336, 512)
        p_tile = region(14912, 2 * 576).rearrange("p (a n) -> p a n", a=2)
        q_cur = region(16384, 2 * 512).rearrange("p (g c n) -> p g c n", g=2, c=16)
        fox_tab0 = region(16384, H * P).rearrange("p (h t) -> p h t", h=H)
        logf_raw = region(16384, 512)
        logf_tb = region(16896, 512)
        suffix = region(17408, 512)
        far_tab = region(17920, 512)
        own = region(18432, 1024).rearrange("p (g h t) -> p g h t", g=2, h=H)
        x_tok = region(10240, 3 * D).rearrange("p (t d) -> p t d", t=3)
        ada_row = [work[0:NSEQ, 4096:4096 + D].rearrange("p (a n) -> p a n", a=2),
                   xh[0:NSEQ, KC * NT:KC * NT + D].rearrange("p (a n) -> p a n", a=2)]
        c_row, c_sig = work[0:NSEQ, 0:D], work[0:NSEQ, D:2 * D]
        par_row = work[0:72, 2 * D:2 * D + P]
        dist_oh = work[0:BUCKETS, 3 * D:3 * D + REV + FWD]
        sq1 = region(0, KC * NT).rearrange("p (k t) -> p k t", k=KC)
        sq = region(14336, KC * NT).rearrange("p (k t) -> p k t", k=KC)
        h_sort = region(0, KC * SORTED).rearrange("p (k t) -> p k t", k=KC)
        h_tok = region(5632, 3 * D).rearrange("p (t d) -> p t d", t=3)
        place1 = region(8704, 3 * ASSIGN).rearrange("p (t n) -> p t n", t=3)
        iota_s = region(10624, ASSIGN)
        x_tok2 = region(11264, 3 * D).rearrange("p (t d) -> p t d", t=3)
        y_st = region(14336, 2 * D).rearrange("p (a d) -> p a d", a=2)
        h_cur = region(16384, 2 * KC * BLK).rearrange("p (a k t) -> p a k t", a=2, k=KC)
        g_tok = xh[:, 0:3 * D].rearrange("p (t d) -> p t d", t=3)
        g2_row = work[0:NSEQ, 17408:17408 + D]
        seq_oh = work[0:NSEQ, 18432:18432 + NT]
        gfin = region(8704, D)
        y_a = region(0, 3 * D).rearrange("p (t d) -> p t d", t=3)
        y_b = region(3 * D, 2 * D + D // 2)
        y_b3 = [region(3072, D), region(4096, D), region(17408, D)]

        small = sb("small", [P, 640])
        silu_cT = small[:, 560:560 + KC * NSEQ].rearrange("p (k s) -> p k s", k=KC)
        gt_sum = small[:, 0:128]
        eq4 = small[:, 128:384]
        mx_a = region(16064, 256)
        mx_b = sb("mx_b", [P, P])
        mx_col = sb("mx_col", [64, 1])
        mx_diag = work[0:64, 14848:14912]
        drop = small[:, 384:448]
        pen = small[:, 448:576].rearrange("p (q n) -> p q n", q=2)
        rsum = small[:, 576:640]
        p_half = sb("p_half", [P, 256])
        l_part = p_half[:, 0:128].rearrange("p (a n) -> p a n", a=2)
        pr_m = sb("pr_m", [P, 2, 2])
        pr_l = sb("pr_l", [P, 2, 2])

        lg = small[:, 0:108].rearrange("p (t n) -> p t n", t=3)
        rt = sb("rt", [P, 280])
        g8 = rt[:, 0:24].rearrange("p (t n) -> p t n", t=3)
        gm8 = rt[:, 24:48].rearrange("p (t n) -> p t n", t=3)
        e8 = rt[:, 48:72].rearrange("p (t n) -> p t n", t=3)
        em8 = rt[:, 72:96].rearrange("p (t n) -> p t n", t=3)
        gidf = rt[:, 96:120].rearrange("p (t n) -> p t n", t=3)
        eidf = rt[:, 120:144].rearrange("p (t n) -> p t n", t=3)
        goh = rt[:, 144:156].rearrange("p (t n) -> p t n", t=3)
        gex = rt[:, 156:168].rearrange("p (t n) -> p t n", t=3)
        gsum = rt[:, 168:171]
        tex = rt[:, 171:174]
        wt = rt[:, 174:180].rearrange("p (a t) -> p a t", a=2)
        ids = rt[:, 180:186].rearrange("p (a t) -> p a t", a=2)
        slots = rt[:, 186:192].rearrange("p (a t) -> p a t", a=2)
        poss = rt[:, 192:198].rearrange("p (a t) -> p a t", a=2)
        ss_f = rt[:, 198:201]
        gi8 = sb("gi8", [P, 3, 8], U32)
        ei8 = sb("ei8", [P, 3, 8], U32)
        posu = sb("posu", [P, 6], U32)
        sel_e = eq_e = small[:, 108:204].rearrange("p (t n) -> p t n", t=3)
        A = mx_a[:, 0:192].rearrange("p (a t n) -> p a t n", a=2, t=3)
        Asum = small[:, 204:300].rearrange("p (t n) -> p t n", t=3)
        rank = small[:, 300:396].rearrange("p (t n) -> p t n", t=3)
        tmp3 = small[:, 396:492].rearrange("p (t n) -> p t n", t=3)
        place_m = small[:, 492:588].rearrange("p (t n) -> p t n", t=3)
        cnt = p_half[:, 0:32]
        start = p_half[:, 32:64]
        extra = p_half[:, 64:96]
        ovb = p_half[:, 96:128]
        base64 = p_half[:, 128:160]
        ov_off = p_half[:, 160:192]
        ones32 = p_half[:, 192:224]
        ov_hi = rt[0:1, 202:234]
        ov_tab = rt[0:1, 234:252].rearrange("p (a n) -> p a n", a=2)
        ov_a = work[0:1, 8704:8704 + 9 * 32].rearrange("p (j n) -> p j n", j=9)
        ov_b = work[0:1, 8704 + 288:8704 + 576].rearrange("p (j n) -> p j n", j=9)
        mr = [rstd[:], region(16896, NT)]
        e_sig = work[0:BLK, 17408:17408 + 2 * DE].rearrange("p (a n) -> p a n", a=2)
        hid = region(17408 + 2 * DE, 2 * DE).rearrange("p (a n) -> p a n", a=2)
        hid_t = region(18752, 2 * FC * BLK).rearrange("p (a f t) -> p a f t", a=2, f=FC)
        ov_st = rt[0:1, 252:253]
        start_i = sb("start_i", [1, NE], I32)
        ov_i = sb("ov_i", [1, 2 * MAXOV], I32)
        nov_i = sb("nov_i", [1, 1], I32)
        assert MAXOV == 9

        ps = [ctx.enter_context(nc.psum_tensor(f"ps{i}", [P, 512], F32)) for i in range(8)]

        ring_in = [sem(f"ring_in{i}") for i in range(RS)]
        pages_v_in = [sem(f"pages_v_in{i}") for i in range(RS)]
        ring_free = [sem(f"ring_free{i}") for i in range(RS)]
        exp_in = [sem(f"exp_in{i}") for i in range(ES)]
        exp_free = [sem(f"exp_free{i}") for i in range(ES)]
        table_in, cst_in, c_in, par_in, x_in, small_in = [sem(n) for n in (
            "table_in", "cst_in", "c_in", "par_in", "x_in", "small_in")]
        names = """c_exp c_silu ada_half ada_mm ada_row mod_tp head_tp head_ev x_tp x_ev_a x_ev_v sq_done ssq_done
            var_done sqrt_done mod_ev h_done fg_mm fg_v fg_a proj_mm proj_a proj_v ktok_tp ktok_ev out_dma
            lf_tp lf_ev f_ready f_dma t5_mm t5_ev w_dma tab_dma own_init own_dma own_mm own_done logf_in
            logf_pre suf_mm suf_done pr_smm pr_max pr_exp pr_norm pr_tp pr_pt pr_pv pr_out qrep_a qrep_p
            qcur_init qcur scores kt_ready s_added s_copied s_turned o_copied o_turned o_init gt_ready
            gate_mm max_part max_t diag max_bc p_sub p_exp p_add lsum pv o_done vl vlc vlp hx osq ossq
            on_done wo_mm wo_done sq2 ssq2 h2_done r_mm lg_ready sel_rdy rank_mm tabs onehot iota_done
            htok_tp htok_ev g2_tp g2_ev gt_mm gt_ev sort_mm sort_a sort_v h_mm h_exp hid hid_tp hid_t y_mm
            y_ev_a y_ev_v y_dma0 y_dma1 v_moe ov_in ov_hx ov_h ov_exp ov_hid ov_y gather_a gather_b gf_in
            zero_set zero_dma fin_sq fin_sqrt fin_v fin_out seq_in pad_done r_a""".split()
        S = {n: sem(n) for n in names}

        block = ctx.enter_context(nc.Block())

        class Unit:

            def __init__(self, c, turn=None):
                self.c, self.turn = c, turn
                self.u = c if turn is None else turn * 6 + c
                self.b = c // 2 if turn is None else turn * 3 + c // 2
                self.g = self.par = c % 2
                self.slot = c % RS

            def step(self, n):
                return Unit(self.c + n, self.turn)

            def count(self, fox, moba):
                v = (self.c // 2) * (fox + moba) + (self.c % 2) * fox
                return v if self.turn is None else self.turn * 3 * (fox + moba) + v

            def times(self, n, more=0):
                return self.u * n + more

            def in_slot(self, more):
                n = self.c // RS + more
                return n if self.turn is None else self.turn * 2 + n

        NU = 2 * NB

        PROJ = ([(True, 2, j * P, j) for j in range(8)]
                + [(False, 3, 0, (0, t)) for t in range(3)] + [(True, 3, W + j * P, 8 + j) for j in range(4)]
                + [(True, 4, j * P, 12 + j) for j in range(4)] + [(False, 4, W, (1, t)) for t in range(3)])

        def proj_evac(r):
            transposed, _, _, d = PROJ[r]
            if transposed:
                return qkT[:, d, :], ps[r % 4][:, 0:NT], HD ** -0.5 if d // 4 % 2 == 0 else 1.0
            g, t = d
            n = TILES[t][1]
            return v_tok[0:n, g, t, :], ps[r % 4][0:n, :], 1.0

        def tok_evac(r):
            t, hf = r % 6 // 2, r % 2
            n = TILES[t][1]
            return (x_tok2, h_tok)[r // 6][0:n, t, 512 * hf:512 * hf + 512], ps[4 + r % 4][0:n, :]

        ADA_AT = [0, 1, 5, 6, 7, 8]
        WIN_AT = {2: [(0, 1024)], 3: [(1024, 512), (1544, 512)], 4: [(2056, 1024)]}
        WLOADS = [4, 3, 3]

        def key_loads(u):
            n = 16 * (WLOADS[u.slot] + PAGES * (u.c // RS + 1))
            return n if u.turn is None else u.turn * (2 * 16 * PAGES) + n

        def ada_full(r):
            n = ADA_AT[r // 2]
            return (S["ada_mm"], r // 2 + 1) if r % 2 == 0 else (ring_free[n % RS], n // RS + 1)

        @block.sync
        def _(sp):
            sp.dma_start(c_row[0:1, :], c_prompt).then_inc(c_in, 16)
            sp.dma_start(c_row[1:NSEQ, :], c_sample).then_inc(c_in, 16)
            sp.dma_start(cst[:], consts[:, 0:NCONST]).then_inc(cst_in, 16)
            ada = w_ada[0].rearrange("(k p) e -> p k e", p=P)
            win = w_in[0].rearrange("(k p) e -> p k e", p=P)
            for n in range(9):
                if n >= RS:
                    sp.wait_ge(ring_free[n % RS], n // RS)
                sv = slot[n % RS].rearrange("p (k e) -> p k e", k=KC)
                if n in WIN_AT:
                    at = 0
                    for c0, w in WIN_AT[n]:
                        sp.dma_start(sv[:, :, at:at + w], win[:, :, c0:c0 + w]).then_inc(ring_in[n % RS], 16)
                        at += w
                elif n == 0:
                    sp.dma_start(sv[:, :, 0:512], ada[:, :, 0:512]).then_inc(S["ada_half"], 16)
                    sp.dma_start(sv[:, :, 512:], ada[:, :, 512:D]).then_inc(ring_in[0], 16)
                else:
                    m = ADA_AT.index(n)
                    sp.dma_start(sv, ada[:, :, m * D:(m + 1) * D]).then_inc(ring_in[n % RS], 16)
            sp.wait_ge(table_in, 16)

            def pages(u):
                for a in range(PAGES):
                    yield a, sp.value_load(table[0:1, bass.ds(u.b * PAGES + a, 1)], min_val=0, max_val=n_phys - 1)

            def load_keys(u, first):
                kd = slot[u.slot][:, 0:4096].rearrange("p (a n) -> p a n", a=PAGES)
                for a, page in pages(u):
                    if a == 0:
                        if first:
                            sp.wait_ge(ring_free[u.slot], 3)
                        else:
                            sp.wait_ge(S["kt_ready"], u.times(2, -4))
                    sp.dma_start(kd[:, a, :], cache_k[u.g][0, bass.ds(page, 1)].rearrange("r t h d -> (r t) (h d)")
                                 ).then_inc(ring_in[u.slot], 16)

            def load_values(u):
                vd = slot[u.slot][:, 4096:].rearrange("p (q t n) -> p q t n", q=2, t=4)
                for a, page in pages(u):
                    if a == 0:
                        sp.wait_ge(ring_free[u.slot], u.in_slot(3))
                    sp.dma_start(vd[32 * (a % 4):32 * (a % 4) + 32, a // 4, :, :],
                                 cache_v[u.g][0, bass.ds(page, 1)].rearrange("r (t l) h d -> (r l) t (h d)", t=4)
                                 ).then_inc(pages_v_in[u.slot], 16)

            load_keys(Unit(0), True)
            for c in range(2):
                load_keys(Unit(c + 1), True)
                load_values(Unit(c))
            with sp.Fori(0, 2) as turn:
                for j in range(6):
                    u = Unit(2 + j, turn)
                    load_keys(u.step(1), False)
                    load_values(u)
            load_keys(Unit(15), False)
            load_values(Unit(14))
            load_values(Unit(15))
            sp.wait_ge(ring_free[1], 8)
            sp.dma_start(slot[1].rearrange("p (k e) -> p k e", k=KC),
                         w_out[0].rearrange("(k p) e -> p k e", p=P)).then_inc(ring_in[1], 16)

            def load_expert(e, k, s, inc):
                sp.dma_start(w13_of[k][:, :, 0:DE], w1[0, e].rearrange("(k p) n -> p k n", p=P)).then_inc(inc, 16)
                sp.dma_start(w13_of[k][:, :, DE:], w3[0, e].rearrange("(k p) n -> p k n", p=P)).then_inc(inc, 16)
                sp.dma_start(w2_of[k], w2[0, e].rearrange("(k p) n -> p k n", p=P)).then_inc(inc, 16)

            for e, need in ((0, [(0, 9)]), (1, [(2, 8)]), (2, [(0, 9), (1, 9)]), (3, [(1, 9), (2, 8)])):
                for s, n in need:
                    sp.wait_ge(ring_free[s], n)
                load_expert(e, e, None, exp_in[e])

            def expert_at(w, e, pat):
                return w[0, bass.ds(e, 1)].rearrange(pat, p=P)

            def load_expert_dyn(e, k, inc):
                sp.dma_start(w13_of[k][:, :, 0:DE], expert_at(w1, e, "o (k p) n -> p (o k) n")).then_inc(inc, 16)
                sp.dma_start(w13_of[k][:, :, DE:], expert_at(w3, e, "o (k p) n -> p (o k) n")).then_inc(inc, 16)
                sp.dma_start(w2_of[k], expert_at(w2, e, "o (k p) n -> p (o k) n")).then_inc(inc, 16)

            with sp.Fori(0, NE // ES - 1) as turn:
                for k in range(ES):
                    sp.wait_ge(exp_free[k], turn + 1)
                    load_expert_dyn(turn * ES + ES + k, k, exp_in[k])
            sp.wait_ge(S["tabs"], 1)
            nov = sp.value_load(nov_i[0:1, 0:1], min_val=0, max_val=MAXOV)
            with sp.If(nov > 0):
                with sp.Fori(0, nov) as i:
                    e = sp.value_load(ov_i[0:1, bass.ds(i + MAXOV, 1)], min_val=0, max_val=NE - 1)
                    sp.wait_ge(exp_free[0], i + NE // ES)
                    load_expert_dyn(e, 0, S["ov_in"])
            sp.wait_ge(S["out_dma"], 16 * 14)
            sp.wait_ge(S["fin_out"], 16 * 3)

        @block.gpsimd
        def _(pool):
            pool.dma_start(table[:], page_table.rearrange("(o b) p -> o (b p)", o=1)).then_inc(table_in, 16)
            pool.wait_ge(table_in, 16)
            lr = logf_raw.rearrange("p (b q t h) -> p b q (t h)", b=NB, q=2, t=4)
            with pool.Fori(0, NB) as b:
                for a in range(PAGES):
                    r = pool.value_load(table[0:1, bass.ds(b * PAGES + a, 1)], min_val=0, max_val=n_phys - 1)
                    pool.dma_start(
                        lr[32 * (a % 4):32 * (a % 4) + 32, bass.ds(b, 1), a // 4, :]
                        .rearrange("p o (t h) -> p (o t) h", t=4),
                        cache_fox_logf[0, bass.ds(r, 1)].rearrange("r (t l) h -> (r l) t h", t=4)
                    ).then_inc(S["logf_in"], 16)
            zeros = work[0:BLK, 10240:10240 + D]
            pool.wait_ge(S["x_tp"], KC)
            nc.gpsimd.memset(zeros, 0.0).then_inc(S["zero_set"], 1)
            pool.wait_ge(S["zero_set"], 1)
            pool.dma_start(scr_y[NE * BLK:, :].rearrange("(j p) d -> p j d", p=BLK),
                           zeros.unsqueeze(1).broadcast_to([BLK, MAXOV, D])).then_inc(S["zero_dma"], 16)
            pool.wait_ge(S["proj_a"], 11)
            pool.wait_ge(S["proj_v"], 11)

            n = 0
            for r in range(2):
                for e in range(2):
                    src = qkT[64 * r + 32 * e:64 * r + 32 * e + 32, 8:12, NP:NT] \
                        .rearrange("p c (b i) -> p b c i", b=NB)
                    for tb in range(4):
                        nc.gpsimd.tensor_copy(q_rep[32 * tb:32 * tb + 32, 1, :, r::2, e, :], src
                                              ).then_inc(S["qrep_p"], 1)
                        n += 1
                        pool.wait_ge(S["qrep_p"], n)
            pool.wait_ge(S["pr_max"], 3 * H)
            nc.gpsimd.memset(q_cur, 0.0).then_inc(S["qcur_init"], 1)
            pool.wait_ge(S["qcur_init"], 1)
            pool.wait_ge(S["qrep_a"], 1)

            qr = q_rep.rearrange("p g b h e i -> p g b (h e) i")

            def unit_query(u):
                if u.c >= 2:
                    pool.wait_ge(S["scores"], u.times(1, -1))
                for tb in range(4):
                    last = nc.gpsimd.tensor_copy(
                        q_cur[32 * tb:32 * tb + 32, u.g, :, 8 * tb:8 * tb + 8],
                        qr[32 * tb:32 * tb + 32, u.g, bass.ds(u.b, 1), :, :].rearrange("p o c i -> p (o c) i"))
                last.then_inc(S["qcur"], 1)

            for c in range(2):
                unit_query(Unit(c))
            with pool.Fori(0, 2) as turn:
                for j in range(6):
                    unit_query(Unit(2 + j, turn))
            for c in range(14, NU):
                unit_query(Unit(c))

            pool.wait_ge(S["wo_done"], 1)
            nc.gpsimd.iota(iota_s, pattern=[[1, ASSIGN]], base=0, channel_multiplier=0,
                           allow_small_or_imprecise_dtypes=True).then_inc(S["iota_done"], 1)
            pool.wait_ge(S["sort_a"], 8)
            pool.wait_ge(S["sort_v"], 8)
            pool.wait_ge(S["pad_done"], 1)
            pool.wait_ge(S["tabs"], 1)

            def block_columns(e, par, first):
                r = pool.value_load(start_i[0:1, bass.ds(e, 1)], min_val=0, max_val=ASSIGN)
                if not first:
                    pool.wait_ge(S["h_mm"], e - 1)
                nc.gpsimd.tensor_copy(h_cur[:, par], h_sort[:, :, bass.ds(r, BLK)]).then_inc(S["hx"], 1)

            for e in range(4):
                block_columns(e, e % 2, e < 2)
            with pool.Fori(0, NE // ES - 1) as turn:
                for k in range(ES):
                    block_columns(turn * ES + ES + k, k % 2, False)
            for par in range(2):
                pool.wait_ge(S[f"y_dma{par}"], 16 * NE // 2)
            nov = pool.value_load(nov_i[0:1, 0:1], min_val=0, max_val=MAXOV)
            with pool.If(nov > 0):
                with pool.Fori(0, nov) as i:
                    r = pool.value_load(ov_i[0:1, bass.ds(i, 1)], min_val=0, max_val=ASSIGN)
                    nc.gpsimd.tensor_copy(h_cur[:, 0], h_sort[:, :, bass.ds(r, BLK)]).then_inc(S["ov_hx"], 1)
                    pool.wait_ge(S["y_dma0"], i * 16 + 16 * (NE // 2 + 1))
            for t, (_, n) in enumerate(TILES):
                pool.indirect_dma_start(y_a[0:n, t, :], None, scr_y,
                                        bass.IndirectOffsetOnAxis(posu[0:n, t:t + 1], 0)
                                        ).then_inc(S["gather_a"], 16)
                pool.indirect_dma_start(y_b3[t][0:n, :], None, scr_y,
                                        bass.IndirectOffsetOnAxis(posu[0:n, 3 + t:4 + t], 0)
                                        ).then_inc(S["gather_b"], 16)

        @block.scalar
        def _(act):
            at = 0
            for v, n in ((b_ada, 48), (g_attn, 8), (g_ffn, 8), (g_out_fox, 4), (g_out_moba, 4)):
                act.dma_start(par_row[at:at + n, :], v[0].rearrange("(a p) -> a p", p=P)).then_inc(par_in, 16)
                at += n
            act.dma_start(x_tok[:, 0:2, :], x_prompt[0].rearrange("(t p) d -> p t d", p=P)).then_inc(x_in, 16)
            act.dma_start(x_tok[0:NS, 2, :], x_sample.rearrange("b i d -> (b i) d")).then_inc(x_in, 16)
            act.dma_start(wfg[:], w_in[0].rearrange("(k p) e -> p k e", p=P)[:, :, 3 * W:3 * W + H]
                          ).then_inc(small_in, 16)
            act.dma_start(wr[:, :, 0:NG], w_rg[0].rearrange("(k p) e -> p k e", p=P)).then_inc(small_in, 16)
            act.dma_start(wr[:, :, NG:], w_re[0].rearrange("(k p) e -> p k e", p=P)).then_inc(small_in, 16)
            act.dma_start(brow[:, 0:NG], b_rg.partition_broadcast(P).rearrange("p o n -> p (o n)")
                          ).then_inc(small_in, 16)
            act.dma_start(brow[:, NG:], b_re.partition_broadcast(P).rearrange("p o n -> p (o n)")
                          ).then_inc(small_in, 16)
            act.dma_start(bfg[:], b_forget.rearrange("o h -> h o")).then_inc(small_in, 16)
            act.dma_start(t5[:], t5_bias).then_inc(small_in, 16)
            act.dma_start(t5_far[:], t5_bias[BUCKETS - 1:BUCKETS, :].partition_broadcast(P)
                          .rearrange("p o n -> p (o n)")).then_inc(small_in, 16)
            act.dma_start(dist_oh, dist_onehot).then_inc(small_in, 16)
            act.dma_start(early, consts[:, NCONST:]).then_inc(small_in, 16)
            act.wait_ge(c_in, 32)
            nc.scalar.activation(c_sig, c_row, ACT.Exp, scale=-1.0).then_inc(S["c_exp"], 1)
            for k in range(0, KC, 2):
                act.wait_ge(S["x_tp"], k + 1)
                nc.scalar.copy(xT[:, k, :], ps[k % 4][:, 0:NT]).then_inc(S["x_ev_a"], 1)
            for k in range(KC):
                act.wait_ge(*((S["x_ev_a"], k // 2 + 1) if k % 2 == 0 else (S["x_ev_v"], k // 2 + 1)))
                if k == 0:
                    act.wait_ge(S["head_ev"], 2)
                nc.scalar.activation(sq1[:, k, :], xT[:, k, :], ACT.Square).then_inc(S["sq_done"], 1)
            def ada_evac(r):
                act.wait_ge(*ada_full(r))
                nc.scalar.copy(ada_row[r // 4 > 0][:, r % 2, :], ps[6 + r % 2][0:NSEQ, :]).then_inc(S["ada_row"], 1)

            ada_evac(0)
            act.wait_ge(S["var_done"], 1)
            nc.scalar.activation(rstd[:], rstd[:], ACT.Sqrt).then_inc(S["sqrt_done"], 1)
            for r in range(1, 4):
                ada_evac(r)
            act.wait_ge(S["fg_v"], 2)
            nc.scalar.activation(work[0:H, 16000:16000 + NT], work[0:H, 15500:15500 + NT], ACT.Exp, scale=-1.0
                                 ).then_inc(S["fg_a"], 1)
            act.wait_ge(S["fg_v"], 3)
            nc.scalar.activation(work[0:H, 16000:16000 + NT], work[0:H, 16000:16000 + NT], ACT.Ln
                                 ).then_inc(S["fg_a"], 1)
            for r in range(0, 22, 2):
                act.wait_ge(S["proj_mm"], r + 1)
                dst, src, scale = proj_evac(r)
                nc.scalar.activation(dst, src, ACT.Copy, scale=scale).then_inc(S["proj_a"], 1)
            act.wait_ge(S["proj_a"], 11)
            act.wait_ge(S["proj_v"], 11)
            for r in range(2):
                for e in range(2):
                    src = qkT[64 * r + 32 * e:64 * r + 32 * e + 32, 0:4, NP:NT] \
                        .rearrange("p c (b i) -> p b c i", b=NB)
                    for tb in range(4):
                        last = nc.scalar.copy(q_rep[32 * tb:32 * tb + 32, 0, :, r::2, e, :], src)
            last.then_inc(S["qrep_a"], 1)
            for g, (kp, ks_, vp, vs) in enumerate(((o_fk_p, o_fk_s, o_fv_p, o_fv_s),
                                                   (o_mk_p, o_mk_s, o_mv_p, o_mv_s))):
                kpv = kp[0, 0].rearrange("(t p) h d -> p t (h d)", p=P)
                vpv = vp[0, 0].rearrange("(t p) h d -> p t (h d)", p=P)
                for t in range(2):
                    act.dma_start(vpv[:, t, :], v_tok[:, g, t, :]).then_inc(S["out_dma"], 16)
                act.dma_start(vs[0].rearrange("b i h d -> (b i) (h d)"), v_tok[0:NS, g, 2, :]
                              ).then_inc(S["out_dma"], 16)
                for t in range(2):
                    act.wait_ge(S["ktok_ev"], 3 * g + t + 1)
                    act.dma_start(kpv[:, t, :], k_out[:, g, t, :]).then_inc(S["out_dma"], 16)
                act.wait_ge(S["ktok_ev"], 3 * g + 3)
                act.dma_start(ks_[0].rearrange("b i h d -> (b i) (h d)"), k_out[0:NS, g, 2, :]
                              ).then_inc(S["out_dma"], 16)
            act.wait_ge(S["lf_ev"], 1)
            act.dma_start(o_fl_p[0, 0].rearrange("(t p) h -> p t h", p=P), lft[:, 0:2, :]).then_inc(S["out_dma"], 16)
            act.dma_start(o_fl_s[0].rearrange("b i h -> (b i) h"), lft[0:NS, 2, :]).then_inc(S["out_dma"], 16)
            act.wait_ge(S["f_ready"], 2)
            act.dma_start(scr_f, work[0:H, 15500:15500 + NP]).then_inc(S["f_dma"], 16)
            act.wait_ge(S["t5_ev"], 3)
            act.dma_start(scr_w, work[0:H, 17408:17408 + WROW].unsqueeze(1).broadcast_to([H, P, WROW])).then_inc(S["w_dma"], 16)
            for r in range(4, 8):
                ada_evac(r)
            act.wait_ge(S["f_dma"], 16)
            act.wait_ge(S["out_dma"], 16 * 14)
            act.dma_start(fox_tab, scr_f.partition_broadcast(P)).then_inc(S["tab_dma"], 16)
            act.wait_ge(S["w_dma"], 16)

            def shifted(offset, n, width):
                return bass.AP(scr_w.tensor, offset, [[WROW - 1, n], [P * WROW, H], [1, width]])

            act.dma_start(moba_tab, shifted(P - 1, P, NP)
                          ).then_inc(S["w_dma"], 16)
            act.wait_ge(S["own_init"], 2)
            ft = far_tab.rearrange("p (q h t i) -> p q h t i", q=2, h=H, t=4)
            for t in range(4):
                act.dma_start(ft[96:128, 1, :, t, :], shifted(384 + NQ + P - 32 * t, 32, NQ)
                              ).then_inc(S["own_dma"], 16)
            for b in range(NB):
                act.dma_start(own[NQ * b:NQ * b + NQ, 1, :, NQ * b:NQ * b + NQ],
                              shifted(384 + NQ, NQ, NQ)
                              ).then_inc(S["own_dma"], 16)
            for r in range(8, 12):
                ada_evac(r)
            for n in range(16):
                act.wait_ge(S["pr_max"], 3 * (n + 1))
                for j in range(2):
                    a, b = (0, P) if j == 0 else (P, 3 * P)
                    last = nc.scalar.activation(pr_s[:, n % 2, a:b], pr_s[:, n % 2, a:b], ACT.Exp,
                                                bias=pr_m[:, n % 2, j:j + 1], accum_out=pr_l[:, n % 2, j:j + 1])
                    last.then_inc(S["pr_exp"], 1)
                act.wait_ge(S["pr_tp"], n + 1)
                nc.scalar.copy(pr_pt[:, n % 2, :], ps[2 + n % 2][:, 0:384]).then_inc(S["pr_pt"], 1)

            def copy_scores(u):
                act.wait_ge(S["scores"], u.times(1, 1))
                nc.scalar.copy(s_nat, ps[0][:, :]).then_inc(S["s_copied"], 1)

            def unit_exp(u):
                act.wait_ge(S["p_sub"], u.times(3, 3))
                nc.scalar.activation(p_tile[:, u.par, :], p_tile[:, u.par, :], ACT.Exp).then_inc(S["p_exp"], 1)

            def copy_output(u):
                act.wait_ge(S["pv"], u.times(1, 1))
                nc.scalar.copy(o_nat, ps[6][:, 0:P]).then_inc(S["o_copied"], 1)

            copy_scores(Unit(0))
            for c in range(2):
                copy_scores(Unit(c + 1))
                unit_exp(Unit(c))
                if c:
                    copy_output(Unit(0))
            with act.Fori(0, 2) as turn:
                for j in range(6):
                    u = Unit(2 + j, turn)
                    copy_scores(u.step(1))
                    unit_exp(u)
                    copy_output(u.step(-1))
            for c in range(14, NU):
                if c + 1 < NU:
                    copy_scores(Unit(c + 1))
                unit_exp(Unit(c))
                copy_output(Unit(c - 1))
            copy_output(Unit(NU - 1))
            act.wait_ge(S["o_done"], 2 * NU)
            act.wait_ge(S["pr_out"], 16)
            for k in range(KC):
                nc.scalar.activation(sq[:, k, :], oT[:, k, :], ACT.Square).then_inc(S["osq"], 1)
            for g in range(2):
                act.wait_ge(S["var_done"], 2 + g)
                nc.scalar.activation(mr[g], mr[g], ACT.Sqrt).then_inc(S["sqrt_done"], 1)
            for k in range(KC):
                act.wait_ge(S["wo_done"], k + 1)
                nc.scalar.activation(sq[:, k, :], xT[:, k, :], ACT.Square).then_inc(S["sq2"], 1)
            act.wait_ge(S["var_done"], 4)
            nc.scalar.activation(rstd[:], rstd[:], ACT.Sqrt).then_inc(S["sqrt_done"], 1)
            act.dma_start(seq_oh, seq_onehot).then_inc(S["seq_in"], 16)
            act.wait_ge(S["lg_ready"], 1)
            nc.scalar.activation(gex, gex, ACT.Exp).then_inc(S["r_a"], 1)
            act.wait_ge(S["lg_ready"], 2)
            nc.scalar.activation(tex, tex, ACT.Exp).then_inc(S["r_a"], 1)
            for r in range(0, 12, 2):
                act.wait_ge(S["htok_tp"], r + 1)
                dst, src = tok_evac(r)
                nc.scalar.copy(dst, src).then_inc(S["htok_ev"], 1)
            for k in range(KC):
                act.wait_ge(S["sort_mm"], k + 1)
                nc.scalar.copy(h_sort[:, k, 0:512], ps[2 * (k % 2)][:, 0:512]).then_inc(S["sort_a"], 1)
            for r in range(6):
                act.wait_ge(S["gt_mm"], r + 1)
                t, hf = r // 2, r % 2
                n = TILES[t][1]
                nc.scalar.copy(g_tok[0:n, t, 512 * hf:512 * hf + 512], ps[4 + r % 2][0:n, :]).then_inc(S["gt_ev"], 1)
            act.wait_ge(S["onehot"], 6)
            act.wait_ge(S["sort_mm"], KC)
            act.dma_start(gfin, g_final.rearrange("(o d) -> o d", o=1).partition_broadcast(P)
                          .rearrange("p o n -> p (o n)")).then_inc(S["gf_in"], 16)

            def block_exp(e, par, hidden_full, done):
                act.wait_ge(hidden_full, e + 1)
                nc.scalar.activation(e_sig[:, par, :], ps[par][0:BLK, 0:DE], ACT.Exp, scale=-1.0).then_inc(done, 1)

            def block_turned(e, par):
                act.wait_ge(S["hid_tp"], e + 1)
                nc.scalar.copy(hid_t[:, par, :, :], ps[6][:, 0:FC * P].rearrange("p (f t) -> p f t", f=FC)[:, :, 0:BLK]
                               ).then_inc(S["hid_t"], 1)

            def block_y_act(e, par, before):
                act.wait_ge(S["y_mm"], e + 1)
                if before is not None:
                    act.wait_ge(S[f"y_dma{par}"], before * 16)
                nc.scalar.copy(y_st[0:BLK, par, 0:512], ps[2 + 2 * par][0:BLK, :]).then_inc(S["y_ev_a"], 1)

            def store_block(e, par):
                act.wait_ge(S["y_ev_a"], e + 1)
                act.wait_ge(S["y_ev_v"], e + 1)
                act.dma_start(scr_y[bass.ds(e * BLK, BLK), :], y_st[0:BLK, par, :]).then_inc(S[f"y_dma{par}"], 16)

            for e in range(4):
                block_exp(e, e % 2, S["h_mm"], S["h_exp"])
                if e >= 1:
                    block_y_act(e - 1, (e - 1) % 2, 1 if e == 3 else None)
                block_turned(e, e % 2)
                if e >= 1:
                    store_block(e - 1, (e - 1) % 2)
            with act.Fori(0, NE // ES - 1) as turn:
                for k in range(ES):
                    e = turn * ES + ES + k
                    block_exp(e, k % 2, S["h_mm"], S["h_exp"])
                    block_y_act(e - 1, (k - 1) % 2, turn * 2 + (k + 3) // 2)
                    block_turned(e, k % 2)
                    store_block(e - 1, (k - 1) % 2)
            block_y_act(NE - 1, 1, NE // 2 - 1)
            store_block(NE - 1, 1)
            nov = act.value_load(nov_i[0:1, 0:1], min_val=0, max_val=MAXOV)
            with act.If(nov > 0):
                with act.Fori(0, nov) as i:
                    block_exp(i, 0, S["ov_h"], S["ov_exp"])
                    block_turned(i + NE, 0)
                    act.wait_ge(S["y_dma0"], i * 16 + 16 * (NE // 2))
                    act.wait_ge(S["ov_y"], i + 1)
                    nc.scalar.copy(y_st[0:BLK, 0, 0:512], ps[2][0:BLK, :]).then_inc(S["y_ev_a"], 1)
                    store_block(i + NE, 0)
            for t, (_, n) in enumerate(TILES):
                act.wait_ge(S["fin_sq"], 2 * t + 2)
                nc.scalar.activation(ss_f[0:n, t:t + 1], ss_f[0:n, t:t + 1], ACT.Sqrt).then_inc(S["fin_sqrt"], 1)
            act.wait_ge(S["fin_v"], 2)
            act.dma_start(y_prompt[0].rearrange("(t p) d -> p t d", p=P)[:, 0], x_tok2[:, 0, :]
                          ).then_inc(S["fin_out"], 16)
            act.wait_ge(S["fin_v"], 4)
            act.dma_start(y_prompt[0].rearrange("(t p) d -> p t d", p=P)[:, 1], x_tok2[:, 1, :]
                          ).then_inc(S["fin_out"], 16)
            act.wait_ge(S["fin_v"], 6)
            act.dma_start(y_sample.rearrange("b i d -> (b i) d"), x_tok2[0:NS, 2, :]).then_inc(S["fin_out"], 16)

        @block.vector
        def _(v):
            chain = [0]

            def link(ins):
                chain[0] += 1
                ins.then_inc(S["vl"], 1)
                v.wait_ge(S["vl"], chain[0])

            tt, ts, stt = nc.vector.tensor_tensor, nc.vector.tensor_scalar, nc.vector.scalar_tensor_tensor

            nc.vector.memset(mx_b[:], 0.0)
            v.wait_ge(S["c_exp"], 1)
            link(ts(c_sig, c_sig, 1.0, None, ALU.add))
            link(nc.vector.reciprocal(c_sig, c_sig))
            tt(c_row, c_row, c_sig, ALU.mult).then_inc(S["c_silu"], 1)
            bias_rows = work[0:H, 17408:17408 + WROW]
            nc.vector.memset(bias_rows, NEG).then_inc(S["t5_ev"], 1)
            v.wait_ge(S["head_tp"], 2)
            nc.vector.tensor_copy(silu_cT[:], ps[4][:, 0:KC * NSEQ].rearrange("p (k s) -> p k s", k=KC)
                                  ).then_inc(S["head_ev"], 1)
            nc.vector.tensor_copy(parT[:], ps[5][:, 0:72]).then_inc(S["head_ev"], 1)
            for k in range(1, KC, 2):
                v.wait_ge(S["x_tp"], k + 1)
                nc.vector.tensor_copy(xT[:, k, :], ps[k % 4][:, 0:NT]).then_inc(S["x_ev_v"], 1)

            rms = [0]

            def inv_rms(dst, src, n):
                ts(dst, src, 1.0 / n, EPS, ALU.mult, ALU.add).then_inc(S["var_done"], 1)
                rms[0] += 1
                v.wait_ge(S["sqrt_done"], rms[0])
                link(nc.vector.reciprocal(dst, dst))

            def normed(dst, src):
                return tt(dst, src, rstd[:].unsqueeze(1).broadcast_to([P, KC, NT]), ALU.mult)

            def modulate(x, m_scale, m_shift, signal):
                sv = x[:, :, NP:].rearrange("p k (b i) -> p k b i", b=NB)
                a = modT[:, m_scale * KC:(m_scale + 1) * KC, :]
                s = modT[:, m_shift * KC:(m_shift + 1) * KC, :]
                link(tt(sv, sv, a[:, :, 1:].unsqueeze(3).broadcast_to([P, KC, NB, NQ]), ALU.mult))
                tt(sv, sv, s[:, :, 1:].unsqueeze(3).broadcast_to([P, KC, NB, NQ]), ALU.add)
                for k in range(KC):
                    ts(x[:, k, 0:NP], x[:, k, 0:NP], a[:, k, 0:1], s[:, k, 0:1], ALU.mult, ALU.add
                       ).then_inc(signal, 1)

            v.wait_ge(S["ssq_done"], 1)
            inv_rms(rstd[:], ps[5][:, 0:NT], D)
            v.wait_ge(S["x_ev_a"], 4)
            link(normed(hT, xT))
            def mod_add(r):
                v.wait_ge(S["mod_tp"], r + 1)
                tt(modT[:, 4 * r:4 * r + 4, :],
                   ps[4][:, 0:4 * NSEQ].rearrange("p (k s) -> p k s", k=4),
                   parT[:, 4 * r:4 * r + 4].unsqueeze(2).broadcast_to([P, 4, NSEQ]), ALU.add).then_inc(S["mod_ev"], 1)

            def mod_gain(m, at):
                a = modT[:, m * KC:(m + 1) * KC, :]
                link(stt(a, a, 1.0, parT[:, at:at + KC].unsqueeze(2).broadcast_to([P, KC, NSEQ]), ALU.add, ALU.mult))

            for r in range(4):
                mod_add(r)
            v.wait_ge(S["mod_ev"], 4)
            mod_gain(MOD_SCALE1, 48)
            modulate(hT, MOD_SCALE1, MOD_SHIFT1, S["h_done"])
            az, ez = work[0:H, 15500:15500 + NT], work[0:H, 16000:16000 + NT]
            v.wait_ge(S["fg_mm"], 1)
            ts(lfT[:], ps[4][0:H, 0:NT], bfg[:, 0:1], None, ALU.add).then_inc(S["fg_v"], 1)
            v.wait_ge(S["fg_v"], 1)
            stt(az, lfT[:], -1.0, lfT[:], ALU.mult, ALU.max).then_inc(S["fg_v"], 1)

            def proj_round(r):
                v.wait_ge(S["proj_mm"], r + 1)
                dst, src, scale = proj_evac(r)
                ts(dst, src, scale, None, ALU.mult).then_inc(S["proj_v"], 1)

            proj_round(1)
            v.wait_ge(S["fg_a"], 1)
            ts(ez, ez, 1.0, None, ALU.add).then_inc(S["fg_v"], 1)
            proj_round(3)
            v.wait_ge(S["fg_a"], 2)
            link(stt(lfT[:], lfT[:], 0.0, ez, ALU.min, ALU.subtract))
            f_cum = work[0:H, 15500:15500 + NP]
            nc.vector.tensor_tensor_scan(f_cum[:, 0:P], const("ones", H), lfT[:, 0:P], 0.0, ALU.mult, ALU.add
                                         ).then_inc(S["f_ready"], 1)
            v.wait_ge(S["f_ready"], 1)
            nc.vector.tensor_tensor_scan(f_cum[:, P:NP], const("ones", H), lfT[:, P:NP], f_cum[:, P - 1:P],
                                         ALU.mult, ALU.add).then_inc(S["f_ready"], 1)
            nc.vector.memset(own, NEG).then_inc(S["own_init"], 1)
            v.wait_ge(S["t5_mm"], 1)
            v.wait_ge(S["t5_ev"], 1)
            nc.vector.tensor_copy(bias_rows[:, 0:REV], ps[5][0:H, 0:REV]).then_inc(S["t5_ev"], 1)
            nc.vector.tensor_copy(bias_rows[:, 384 + NQ:], ps[5][0:H, REV:REV + FWD]).then_inc(S["t5_ev"], 1)
            for r in range(5, 22, 2):
                proj_round(r)
            v.wait_ge(S["lf_tp"], 1)
            nc.vector.tensor_copy(lft[:, 0:2, :], ps[6][:, 0:2 * H].rearrange("p (t h) -> p t h", t=2))
            nc.vector.tensor_copy(lft[0:NS, 2, :], ps[6][0:NS, 2 * H:3 * H]).then_inc(S["lf_ev"], 1)
            v.wait_ge(S["zero_dma"], 16)
            for r in range(6):
                g, t = r // 3, r % 3
                n = TILES[t][1]
                v.wait_ge(S["ktok_tp"], r + 1)
                nc.vector.tensor_copy(k_out[0:n, g, t, :], ps[4 + r % 2][0:n, :]).then_inc(S["ktok_ev"], 1)
            lv = logf_raw.rearrange("p (c t h) -> p c t h", c=16, t=4)
            uv = logf_tb.rearrange("p (c t h) -> p c t h", c=16, t=4)
            tv = small[:, 0:128].rearrange("p (c h) -> p c h", c=16)
            v.wait_ge(S["logf_in"], 16 * NB * PAGES)
            nc.vector.memset(uv[:, :, 3, :], 0.0)
            link(nc.vector.tensor_copy(uv[:, :, 2, :], lv[:, :, 3, :]))
            link(tt(uv[:, :, 1, :], uv[:, :, 2, :], lv[:, :, 2, :], ALU.add))
            link(tt(uv[:, :, 0, :], uv[:, :, 1, :], lv[:, :, 1, :], ALU.add))
            link(nc.vector.memset(small[:, 128:256], 0.0))
            link(tt(tv, uv[:, :, 0, :], lv[:, :, 0, :], ALU.add))
            nc.vector.tensor_copy(small[:, 128:256].rearrange("p (b q h) -> p b q h", b=NB, q=2)[:, :, 0],
                                  tv.rearrange("p (b q) h -> p b q h", b=NB)[:, :, 1]).then_inc(S["logf_pre"], 1)
            v.wait_ge(S["w_dma"], 16)
            nc.vector.tensor_copy(far_tab.rearrange("p (q h n) -> p q h n", q=2, h=H),
                                  t5_far[:].unsqueeze(1).unsqueeze(3).broadcast_to([P, 2, H, 32])
                                  ).then_inc(S["own_init"], 1)
            v.wait_ge(S["suf_mm"], 1)
            nc.vector.tensor_copy(suffix.rearrange("p (c h t) -> p c t h", c=16, h=H),
                                  ps[5][:, :].rearrange("p (c t h) -> p c t h", c=16, t=4)
                                  ).then_inc(S["suf_done"], 1)
            v.wait_ge(S["own_mm"], 3)
            om = const("own_mask", NS).unsqueeze(1).broadcast_to([NS, H, NS])
            link(tt(own[0:NS, 0], ps[0][0:NS, 256:256 + H].unsqueeze(2).broadcast_to([NS, H, NS]), om, ALU.add))

            def own_add(g):
                for r in range(2):
                    o = own[0:NS, g, r::2, :]
                    last = tt(o, o, ps[2 * g + r][0:NS, 0:4 * NS].rearrange("p (h t) -> p h t", h=4), ALU.add)
                last.then_inc(S["own_done"], 1)

            own_add(0)
            for r in range(4, 8):
                mod_add(r)
            v.wait_ge(S["own_dma"], 16 * (NB + 4))
            own_add(1)
            for r in range(8, 12):
                mod_add(r)
            v.wait_ge(S["mod_ev"], 12)
            mod_gain(MOD_SCALE2, 56)
            v.wait_ge(S["tab_dma"], 16)
            link(tt(fox_tab0, const("causal")[:, P:].unsqueeze(1).broadcast_to([P, H, P]), fox_tab[:, :, 0:P],
                    ALU.subtract))
            link(tt(fox_tab, const("causal").unsqueeze(1).broadcast_to([P, H, NP]), fox_tab, ALU.subtract))
            v.wait_ge(S["w_dma"], 32)

            def prompt_max(n):
                tab = (fox_tab, moba_tab)[n // H][:, n % H, :]
                tab0 = fox_tab0[:, n, :] if n < H else tab[:, P:]
                v.wait_ge(S["pr_smm"], n + 1)
                if n >= 2:
                    v.wait_ge(S["pr_tp"], n - 1)
                for j, (a, b, bias) in enumerate(((0, P, tab0), (P, 3 * P, tab))):
                    nc.vector.tensor_tensor_reduce(pr_s[:, n % 2, a:b], ps[n % 2][:, a:b], bias, 1.0, NEG,
                                                   ALU.add, ALU.max, pr_m[:, n % 2, j:j + 1]
                                                   ).then_inc(S["pr_max"], 1)
                v.wait_ge(S["pr_max"], 3 * n + 2)
                ts(pr_m[:, n % 2, :], pr_m[:, n % 2, :], -1.0, None, ALU.mult).then_inc(S["pr_max"], 1)

            def prompt_norm(n):
                v.wait_ge(S["pr_exp"], 2 * n + 2)
                link(nc.vector.reciprocal(pr_l[:, n % 2, :], pr_l[:, n % 2, :]))
                ts(pr_s[:, n % 2, 0:P], pr_s[:, n % 2, 0:P], pr_l[:, n % 2, 0:1], None, ALU.mult)
                ts(pr_s[:, n % 2, P:3 * P], pr_s[:, n % 2, P:3 * P], pr_l[:, n % 2, 1:2], None, ALU.mult
                   ).then_inc(S["pr_norm"], 1)

            def prompt_out(n):
                v.wait_ge(S["pr_pv"], n + 1)
                rows = slice(64 * (n % 2), 64 * (n % 2) + 64)
                nc.vector.tensor_copy(oT[rows, n // 2, 0:NP], ps[4 + n % 2][rows, 0:NP]).then_inc(S["pr_out"], 1)

            for n in range(16 + 2):
                if n < 16:
                    prompt_max(n)
                if 1 <= n < 17:
                    prompt_norm(n - 1)
                if n >= 2:
                    prompt_out(n - 2)

            LINKS = (2, 10)
            sv = s_tile.rearrange("p (q h t i) -> p q h t i", q=2, h=H, t=4)

            def transpose_keys(u, q):
                if q == 0:
                    v.wait_ge(ring_in[u.slot], key_loads(u))
                    if u.c >= 2:
                        v.wait_ge(S["scores"], u.times(1, -1))
                nc.vector.transpose(kt[u.par][:, q, :].rearrange("p (c a l) -> p a c l", c=16, a=4),
                                    slot[u.slot][:, 2048 * q:2048 * q + 2048]
                                    .rearrange("p (a c l) -> p a c l", c=16, a=4)).then_inc(S["kt_ready"], 1)

            def unit_softmax(u, later, old):
                moba = u.g == 1
                did = [0]

                def ulink(ins):
                    did[0] += 1
                    ins.then_inc(S["vlc"], 1)
                    v.wait_ge(S["vlc"], u.count(*LINKS) + did[0])

                bank = ps[1]
                v.wait_ge(S["s_turned"], u.times(1, 1))
                if u.c >= 1:
                    v.wait_ge(S["p_sub"], u.times(3))
                if moba:
                    nc.vector.tensor_reduce(gt_sum.rearrange("p (c i) -> p c i", c=16),
                                            bank[:, :].rearrange("p (c t i) -> p c i t", c=16, t=4),
                                            AX.X, ALU.add).then_inc(S["gt_ready"], 1)
                    tt(s_tile, bank[:, :], far_tab, ALU.add).then_inc(S["s_added"], 1)
                else:
                    d = suffix.rearrange("p (b c) -> p b c", b=NB)[:, bass.ds(u.b, 1), :] \
                        .rearrange("p o c -> p (o c)").unsqueeze(2).broadcast_to([P, 64, NQ])
                    tt(s_tile.rearrange("p (c i) -> p c i", c=64), bank[:, :].rearrange("p (c i) -> p c i", c=64),
                       d, ALU.add).then_inc(S["s_added"], 1)
                if moba and later is not None:
                    transpose_keys(later, 0)
                v.wait_ge(S["s_added"], u.times(1, 1))
                if moba:
                    v.wait_ge(S["gate_mm"], u.count(0, 1) + 1)
                    g4 = ps[2][:, 0:256].rearrange("p (n c) -> p n c", n=4)
                    e4 = eq4.rearrange("p (n c) -> p n c", n=4)
                    ulink(nc.vector.tensor_reduce(drop, ps[2][:, 0:256].rearrange("p (n c) -> p c n", n=4), AX.X,
                                                  ALU.min))
                    ulink(tt(e4, g4, drop.unsqueeze(1).broadcast_to([P, 4, 64]), ALU.is_le))
                    ulink(tt(e4, e4, const("block_no").unsqueeze(2).broadcast_to([P, 4, 64]), ALU.mult))
                    ulink(nc.vector.tensor_reduce(drop, eq4.rearrange("p (n c) -> p c n", n=4), AX.X, ALU.max))
                    for q in range(2):
                        ulink(ts(pen[:, q, :], drop, const("block_id")[:, q:q + 1], NEG, ALU.is_equal, ALU.mult))
                    for q in range(2):
                        ulink(tt(sv[:, q], sv[:, q], pen[:, q, :].rearrange("p (h i) -> p h i", h=H).unsqueeze(2)
                                 .broadcast_to([P, H, 4, NQ]), ALU.add))
                own_u = own[:, u.g, :, bass.ds(u.b * NQ, NQ)]
                mb = mx_b[:, 0:64].rearrange("p (h i) -> p h i", h=H)
                ulink(nc.vector.tensor_reduce(mb, s_tile.rearrange("p (q h t i) -> p h i q t", q=2, h=H, t=4),
                                              AX.XY, ALU.max))
                tt(mb, mb, own_u, ALU.max).then_inc(S["max_part"], 1)
                if later is not None:
                    if not moba:
                        transpose_keys(later, 0)
                    transpose_keys(later, 1)
                v.wait_ge(S["max_t"], u.times(1, 1))
                ulink(nc.vector.reduce_max(mx_col[:], ps[3][0:64, 0:P], AX.X))
                assert did[0] == LINKS[u.g]
                ts(mx_diag[:], const("ident", 64)[:, 0:64], mx_col[:, 0:1], None, ALU.mult).then_inc(S["diag"], 1)
                if old is not None:
                    unit_output(old)
                v.wait_ge(S["max_bc"], u.times(1, 1))
                m = ps[4][:, 0:64].rearrange("p (h i) -> p h i", h=H)
                pt = p_tile[:, u.par, :]
                for q in range(2):
                    tt(pt[:, 256 * q:256 * q + 256].rearrange("p (t h i) -> p h t i", h=H, t=4), sv[:, q],
                       m.unsqueeze(2).broadcast_to([P, H, 4, NQ]), ALU.subtract).then_inc(S["p_sub"], 1)
                tt(pt[:, 512:576].rearrange("p (h i) -> p h i", h=H), own_u, m, ALU.subtract).then_inc(S["p_sub"], 1)
                v.wait_ge(S["p_exp"], u.times(1, 1))
                nc.vector.tensor_reduce(l_part[:, u.par, :], pt.rearrange("p (s n) -> p n s", s=9), AX.X, ALU.add
                                        ).then_inc(S["p_add"], 1)

            def unit_output(u):
                v.wait_ge(S["lsum"], u.times(1, 1))
                nc.vector.reciprocal(rsum, ps[5][:, 0:64]).then_inc(S["vlp"], 1)
                v.wait_ge(S["vlp"], u.times(1, 1))
                v.wait_ge(S["o_turned"], u.times(1, 1))
                o = ps[7][:, 0:P].rearrange("p (c r i) -> p c r i", c=4, r=4)
                for r in range(2):
                    rows = slice(64 * r, 64 * r + 64)
                    tt(oT[rows, 4 * u.g:4 * u.g + 4, bass.ds(u.b * NQ + NP, NQ)], o[rows, :, r, :],
                       rsum[rows, :].rearrange("p (c r i) -> p c r i", c=4, r=2)[:, :, r, :], ALU.mult
                       ).then_inc(S["o_done"], 1)

            nc.vector.memset(ps[6][:, 0:P], 0.0).then_inc(S["o_init"], 1)
            v.wait_ge(S["pr_pv"], 16)
            v.wait_ge(S["qcur"], 1)
            for c in range(2):
                for q in range(2):
                    transpose_keys(Unit(c), q)
            for c in range(2):
                unit_softmax(Unit(c), Unit(c + 2), None)
            with v.Fori(0, 2) as turn:
                for j in range(6):
                    u = Unit(2 + j, turn)
                    unit_softmax(u, u.step(2), u.step(-2))
            for c in range(14, NU):
                unit_softmax(Unit(c), None, Unit(c - 2))
            for c in range(14, NU):
                unit_output(Unit(c))

            for g in range(2):
                v.wait_ge(S["ossq"], g + 1)
                inv_rms(mr[g], ps[g][:, 0:NT], W)
                for c in range(PC):
                    k = g * PC + c
                    stt(oT[:, k, :], oT[:, k, :], parT[:, 64 + k:65 + k], mr[g], ALU.mult, ALU.mult
                        ).then_inc(S["on_done"], 1)
            gate = modT[:, MOD_GATE1 * KC:(MOD_GATE1 + 1) * KC, :]
            so = region(17408, NS)
            for k in range(KC):
                v.wait_ge(S["wo_mm"], k + 1)
                bank = ps[2 + k % 4]
                link(tt(so.rearrange("p (b i) -> p b i", b=NB), bank[:, NP:NT].rearrange("p (b i) -> p b i", b=NB),
                        gate[:, k, 1:].unsqueeze(2).broadcast_to([P, NB, NQ]), ALU.mult))
                link(tt(xT[:, k, NP:], xT[:, k, NP:], so, ALU.add))
                stt(xT[:, k, 0:NP], bank[:, 0:NP], gate[:, k, 0:1], xT[:, k, 0:NP], ALU.mult, ALU.add
                    ).then_inc(S["wo_done"], 1)
            v.wait_ge(S["ssq2"], 1)
            inv_rms(rstd[:], ps[0][:, 0:NT], D)
            link(normed(hT, xT))
            modulate(hT, MOD_SCALE2, MOD_SHIFT2, S["h2_done"])
            v.wait_ge(S["r_mm"], 1)
            nc.vector.memset(rt[:, 0:72], NEG)
            link(nc.vector.memset(lg, 0.0))
            br = brow[:].unsqueeze(1)
            link(tt(lg[:, 0:2, :], ps[1][:, 0:72].rearrange("p (t n) -> p t n", t=2), br.broadcast_to([P, 2, 36]),
                    ALU.add))
            link(tt(lg[0:NS, 2, :], ps[1][0:NS, 72:108], brow[0:NS, :], ALU.add))
            link(nc.vector.tensor_copy(g8[:, :, 0:NG], lg[:, :, 0:NG]))
            for t in range(3):
                link(nc.vector.max(gm8[:, t, :], g8[:, t, :]))
                link(nc.vector.max_index(gi8[:, t, :], gm8[:, t, :], g8[:, t, :]))
            link(nc.vector.tensor_copy(gidf, gi8[:]))
            tt(gex, lg[:, :, 0:NG], gm8[:, :, 0:1].broadcast_to([P, 3, NG]), ALU.subtract).then_inc(S["lg_ready"], 1)
            link(tt(goh, const("iota32")[:, 0:NG].unsqueeze(1).broadcast_to([P, 3, NG]),
                    gidf[:, :, 0:1].broadcast_to([P, 3, NG]), ALU.is_equal))
            for t in range(3):
                link(tt(sel_e[:, t, :].rearrange("p (g e) -> p g e", g=NG),
                        lg[:, t, NG:].rearrange("p (g e) -> p g e", g=NG),
                        goh[:, t, :].unsqueeze(2).broadcast_to([P, NG, EPG]), ALU.mult))
            link(nc.vector.tensor_reduce(e8, sel_e.rearrange("p t (g e) -> p t e g", g=NG), AX.X, ALU.add))
            for t in range(3):
                link(nc.vector.max(em8[:, t, :], e8[:, t, :]))
                link(nc.vector.max_index(ei8[:, t, :], em8[:, t, :], e8[:, t, :]))
            link(nc.vector.tensor_copy(eidf, ei8[:]))
            tt(tex.unsqueeze(2), em8[:, :, 1:2], em8[:, :, 0:1], ALU.subtract).then_inc(S["lg_ready"], 1)
            for a in range(2):
                link(stt(ids[:, a, :].unsqueeze(2), gidf[:, :, 0:1], float(EPG), eidf[:, :, a:a + 1],
                         ALU.mult, ALU.add))
                link(tt(A[:, a], const("iota32").unsqueeze(1).broadcast_to([P, 3, NE]),
                        ids[:, a, :].unsqueeze(2).broadcast_to([P, 3, NE]), ALU.is_equal))
            link(nc.vector.memset(A[NS:, :, 2, :], 0.0))
            tt(Asum, A[:, 0], A[:, 1], ALU.add).then_inc(S["sel_rdy"], 1)
            v.wait_ge(S["r_a"], 2)
            link(nc.vector.reduce_sum(gsum, gex, AX.X))
            link(ts(wt[:, 1, :], tex, 1.0, None, ALU.add))
            link(tt(wt[:, 1, :], wt[:, 1, :], gsum, ALU.mult))
            link(nc.vector.reciprocal(wt[:, 0, :], wt[:, 1, :]))
            link(tt(wt[:, 1, :], wt[:, 0, :], tex, ALU.mult))
            for r in range(1, 12, 2):
                v.wait_ge(S["htok_tp"], r + 1)
                dst, src = tok_evac(r)
                nc.vector.tensor_copy(dst, src).then_inc(S["v_moe"], 1)
            link(nc.vector.memset(ones32, 1.0))
            v.wait_ge(S["rank_mm"], 1)
            link(nc.vector.tensor_copy(rank, ps[2][:, 0:96].rearrange("p (t n) -> p t n", t=3)))
            link(nc.vector.tensor_copy(cnt, ps[2][:, 96:128]))
            link(nc.vector.tensor_tensor_scan(start, ones32, cnt, 0.0, ALU.mult, ALU.add))
            link(tt(start, start, cnt, ALU.subtract))
            link(ts(extra, cnt, float(BLK), None, ALU.is_gt))
            for m in range(2, NT // BLK):
                link(stt(extra, cnt, float(BLK * m), extra, ALU.is_gt, ALU.add))
            link(nc.vector.tensor_tensor_scan(ovb, ones32, extra, 0.0, ALU.mult, ALU.add))
            link(nc.vector.tensor_copy(ov_hi, ovb[0:1, :]))
            link(tt(ovb, ovb, extra, ALU.subtract))
            link(tt(place_m, rank, start.unsqueeze(1).broadcast_to([P, 3, NE]), ALU.add))
            for a in range(2):
                link(tt(tmp3, A[:, a], place_m, ALU.mult))
                link(nc.vector.tensor_reduce(slots[:, a, :], tmp3, AX.X, ALU.add))
            link(ts(base64, const("iota32"), float(BLK), None, ALU.mult))
            link(ts(ov_off, ovb, float(BLK), float(BLK * (NE - 1)), ALU.mult, ALU.add))
            link(tt(ov_off, ov_off, base64, ALU.subtract))
            link(ts(tmp3, rank, float(BLK), None, ALU.is_ge))
            link(tt(tmp3, tmp3, ov_off.unsqueeze(1).broadcast_to([P, 3, NE]), ALU.mult))
            link(tt(place_m, tmp3, rank, ALU.add))
            link(tt(place_m, place_m, base64.unsqueeze(1).broadcast_to([P, 3, NE]), ALU.add))
            for a in range(2):
                link(tt(tmp3, A[:, a], place_m, ALU.mult))
                link(nc.vector.tensor_reduce(poss[:, a, :], tmp3, AX.X, ALU.add))
            link(nc.vector.tensor_copy(posu[:].rearrange("p (a t) -> p a t", a=2), poss))
            link(nc.vector.tensor_copy(start_i[:], start[0:1, :]))
            jb = const("iota_ov", 1).unsqueeze(2).broadcast_to([1, MAXOV, NE])
            link(tt(ov_a, ovb[0:1, :].unsqueeze(1).broadcast_to([1, MAXOV, NE]), jb, ALU.is_le))
            link(tt(ov_b, ov_hi.unsqueeze(1).broadcast_to([1, MAXOV, NE]), jb, ALU.is_gt))
            link(tt(ov_a, ov_a, ov_b, ALU.mult))
            link(tt(ov_b, ov_a, const("iota32", 1).unsqueeze(1).broadcast_to([1, MAXOV, NE]), ALU.mult))
            link(nc.vector.tensor_reduce(ov_tab[:, 1, :], ov_b, AX.X, ALU.add))
            link(tt(ov_b, jb, ovb[0:1, :].unsqueeze(1).broadcast_to([1, MAXOV, NE]), ALU.subtract))
            link(ts(ov_b, ov_b, float(BLK), float(BLK), ALU.mult, ALU.add))
            link(tt(ov_b, ov_b, start[0:1, :].unsqueeze(1).broadcast_to([1, MAXOV, NE]), ALU.add))
            link(tt(ov_b, ov_b, ov_a, ALU.mult))
            link(nc.vector.tensor_reduce(ov_tab[:, 0, :], ov_b, AX.X, ALU.add))
            link(nc.vector.tensor_copy(ov_i[:], ov_tab.rearrange("p a n -> p (a n)")))
            nc.vector.tensor_copy(nov_i[:], ov_hi[:, NE - 1:NE]).then_inc(S["tabs"], 1)
            v.wait_ge(S["iota_done"], 1)
            for t, (_, n) in enumerate(TILES):
                ts(place1[0:n, t, :], iota_s[0:n, :], slots[0:n, 0, t:t + 1], None, ALU.is_equal
                   ).then_inc(S["onehot"], 1)
                v.wait_ge(S["onehot"], 2 * t + 1)
                stt(place1[0:n, t, :], iota_s[0:n, :], slots[0:n, 1, t:t + 1], place1[0:n, t, :], ALU.is_equal,
                    ALU.add).then_inc(S["onehot"], 1)
            nc.vector.memset(hid[BLK:, :, :], 0.0)
            nc.vector.memset(h_sort[:, :, ASSIGN:], 0.0).then_inc(S["pad_done"], 1)
            for k in range(KC):
                v.wait_ge(S["sort_mm"], k + 1)
                nc.vector.tensor_copy(h_sort[:, k, 512:ASSIGN], ps[2 * (k % 2) + 1][:, 0:ASSIGN - 512]
                                      ).then_inc(S["sort_v"], 1)
            v.wait_ge(S["g2_tp"], 1)
            nc.vector.tensor_copy(g2_row[:, 0:512], ps[6][0:NSEQ, :])
            nc.vector.tensor_copy(g2_row[:, 512:], ps[7][0:NSEQ, :]).then_inc(S["g2_ev"], 1)

            def hidden(e, par, bank, exp_sig, hid_sig):
                v.wait_ge(exp_sig, e + 1)
                a, b, s = ps[bank][0:BLK, 0:DE], ps[bank][0:BLK, DE:2 * DE], e_sig[:, par, :]
                steps = [lambda: ts(s, s, 1.0, None, ALU.add), lambda: nc.vector.reciprocal(s, s),
                         lambda: tt(s, s, a, ALU.mult), lambda: tt(hid[0:BLK, par, :], s, b, ALU.mult)]
                for i, st in enumerate(steps):
                    if i:
                        v.wait_ge(hid_sig, e * 4 + i)
                    st().then_inc(hid_sig, 1)

            def block_y(e, par, before, k, used):
                v.wait_ge(exp_free[k], used)
                if before is not None:
                    v.wait_ge(S[f"y_dma{par}"], before * 16)
                nc.vector.tensor_copy(y_st[0:BLK, par, 512:], ps[3 + 2 * par][0:BLK, :]).then_inc(S["y_ev_v"], 1)

            for e in range(4):
                hidden(e, e % 2, e % 2, S["h_exp"], S["hid"])
                if e >= 1:
                    block_y(e - 1, (e - 1) % 2, 1 if e == 3 else None, e - 1, 1)
            with v.Fori(0, NE // ES - 1) as turn:
                for k in range(ES):
                    e = turn * ES + ES + k
                    hidden(e, k % 2, k % 2, S["h_exp"], S["hid"])
                    block_y(e - 1, (k - 1) % 2, turn * 2 + (k + 3) // 2, (k - 1) % ES, turn + (1 if k == 0 else 2))
            block_y(NE - 1, 1, NE // 2 - 1, ES - 1, NE // ES)
            nov = v.value_load(nov_i[0:1, 0:1], min_val=0, max_val=MAXOV)
            with v.If(nov > 0):
                with v.Fori(0, nov) as i:
                    v.wait_ge(S["ov_h"], i + 1)
                    hidden(i, 0, 0, S["ov_exp"], S["ov_hid"])
                    v.wait_ge(exp_free[0], i + NE // ES + 1)
                    v.wait_ge(S["y_dma0"], i * 16 + 16 * (NE // 2))
                    nc.vector.tensor_copy(y_st[0:BLK, 0, 512:], ps[3][0:BLK, :]).then_inc(S["y_ev_v"], 1)
            v.wait_ge(S["gather_a"], 48)
            v.wait_ge(S["gather_b"], 48)
            v.wait_ge(S["gt_ev"], 6)
            v.wait_ge(S["gf_in"], 16)
            for t, (_, n) in enumerate(TILES):
                a, b, x = y_a[0:n, t, :], y_b3[t][0:n, :], x_tok2[0:n, t, :]
                link(ts(a, a, wt[0:n, 0, t:t + 1], None, ALU.mult))
                link(stt(a, b, wt[0:n, 1, t:t + 1], a, ALU.mult, ALU.add))
                link(tt(a, a, g_tok[0:n, t, :], ALU.mult))
                link(tt(x, x, a, ALU.add))
                nc.vector.tensor_tensor_reduce(a, x, x, 1.0, 0.0, ALU.mult, ALU.add, ss_f[0:n, t:t + 1]
                                               ).then_inc(S["fin_sq"], 1)
                v.wait_ge(S["fin_sq"], 2 * t + 1)
                ts(ss_f[0:n, t:t + 1], ss_f[0:n, t:t + 1], 1.0 / D, EPS, ALU.mult, ALU.add).then_inc(S["fin_sq"], 1)
                v.wait_ge(S["fin_sqrt"], t + 1)
                nc.vector.reciprocal(ss_f[0:n, t:t + 1], ss_f[0:n, t:t + 1]).then_inc(S["fin_v"], 1)
                v.wait_ge(S["fin_v"], 2 * t + 1)
                stt(x, x, ss_f[0:n, t:t + 1], gfin[0:n, :], ALU.mult, ALU.mult).then_inc(S["fin_v"], 1)

        @block.tensor
        def _(pe):
            mm, tp = nc.tensor.matmul, nc.tensor.transpose

            pe.wait_ge(cst_in, 16)
            pe.wait_ge(S["c_silu"], 1)
            for k in range(KC):
                last = tp(ps[4][:, k * NSEQ:(k + 1) * NSEQ], c_row[:, k * P:(k + 1) * P], const("ident", NSEQ)[:, 0:NSEQ])
            last.then_inc(S["head_tp"], 1)
            pe.wait_ge(par_in, 16 * 5)
            tp(ps[5][:, 0:72], par_row, const("ident", 72)[:, 0:72]).then_inc(S["head_tp"], 1)
            pe.wait_ge(x_in, 32)
            for k in range(KC):
                if k >= 4:
                    pe.wait_ge(S["x_ev_a" if k % 2 == 0 else "x_ev_v"], (k - 4) // 2 + 1)
                for t, (t0, n) in enumerate(TILES):
                    last = tp(ps[k % 4][:, t0:t0 + n], x_tok[0:n, t, k * P:(k + 1) * P], const("ident", n)[:, 0:n])
                last.then_inc(S["x_tp"], 1)

            def sum_squares(bank, src, chunks, sig, base, done, freed=None):
                for j, k in enumerate(chunks):
                    pe.wait_ge(sig, base + k + 1)
                    last = mm(ps[bank][:, 0:NT], ones, src[:, k, :], start=(j == 0), stop=(j == len(chunks) - 1))
                    if j == 0 and freed is not None:
                        last.then_inc(freed, 1)
                last.then_inc(done, 1)

            def ada_mm(r):
                m, hf = r // 2, r % 2
                n = ADA_AT[m]
                if r == 0:
                    pe.wait_ge(S["ada_half"], 16)
                else:
                    pe.wait_ge(ring_in[n % RS], 16 * (1 if r < 4 else WLOADS[n % RS] - (n == 5)))
                if r >= 2:
                    pe.wait_ge(S["ada_row"], r - 1)
                wv = slot[n % RS].rearrange("p (k e) -> p k e", k=KC)
                for k in range(KC):
                    last = mm(ps[6 + r % 2][0:NSEQ, :], silu_cT[:, k, :], wv[:, k, 512 * hf:512 * hf + 512],
                              start=(k == 0), stop=(k == KC - 1))
                last.then_inc(ada_full(r)[0], 1)

            def ada_tp(r):
                pe.wait_ge(S["ada_row"], r + 1)
                if r >= 1:
                    pe.wait_ge(S["mod_ev"], r)
                for c in range(4):
                    last = tp(ps[4][:, c * NSEQ:(c + 1) * NSEQ],
                              ada_row[r // 4 > 0][:, r % 2, c * P:(c + 1) * P], const("ident", NSEQ)[:, 0:NSEQ])
                last.then_inc(S["mod_tp"], 1)

            pe.wait_ge(S["head_ev"], 2)
            ada_mm(0)
            sum_squares(5, sq1, range(KC), S["sq_done"], 0, S["ssq_done"])
            for r in range(1, 4):
                ada_mm(r)
                ada_tp(r - 1)
            ada_tp(3)
            pe.wait_ge(S["mod_ev"], 4)
            pe.wait_ge(small_in, 16 * 10)
            mm(ps[5][0:H, 0:REV + FWD], t5[:], dist_oh, start=True, stop=True).then_inc(S["t5_mm"], 1)
            for k in range(KC):
                pe.wait_ge(S["h_done"], k + 1)
                last = mm(ps[4][0:H, 0:NT], wfg[:, k, :], hT[:, k, :], start=(k == 0), stop=(k == KC - 1))
            last.then_inc(S["fg_mm"], 1)
            for r, (transposed, item, col, d) in enumerate(PROJ):
                if r in (0, 8, 15):
                    pe.wait_ge(ring_in[item % RS], 16 * {2: 1, 3: 3, 4: 2}[item])
                if r >= 4:
                    pe.wait_ge(S["proj_a" if r % 2 == 0 else "proj_v"], (r - 4) // 2 + 1)
                wv = slot[item % RS].rearrange("p (k e) -> p k e", k=KC)
                for k in range(KC):
                    if transposed:
                        last = mm(ps[r % 4][:, 0:NT], wv[:, k, col:col + P], hT[:, k, :],
                                  start=(k == 0), stop=(k == KC - 1))
                    else:
                        t0, n = TILES[d[1]]
                        last = mm(ps[r % 4][0:n, :], hT[:, k, t0:t0 + n], wv[:, k, col:col + W],
                                  start=(k == 0), stop=(k == KC - 1))
                    if r in (8, 15) and k == 0:
                        last.then_inc(ring_free[(item - 1) % RS], 1)
                last.then_inc(S["proj_mm"], 1)
            pe.wait_ge(S["f_ready"], 2)
            for t, (t0, n) in enumerate(TILES):
                last = tp(ps[6][0:n, t * H:(t + 1) * H], lfT[:, t0:t0 + n], const("ident", H)[:, 0:H])
                if t == 0:
                    last.then_inc(ring_free[4 % RS], 1)
            last.then_inc(S["lf_tp"], 1)
            pe.wait_ge(S["proj_a"], 11)
            pe.wait_ge(S["proj_v"], 11)
            for r in range(6):
                g, t = r // 3, r % 3
                t0, n = TILES[t]
                if r == 1:
                    pe.wait_ge(S["t5_ev"], 3)
                if r >= 2:
                    pe.wait_ge(S["ktok_ev"], r - 1)
                for c in range(PC):
                    last = tp(ps[4 + r % 2][0:n, c * P:(c + 1) * P], qkT[:, 8 * g + 4 + c, t0:t0 + n], ident)
                last.then_inc(S["ktok_tp"], 1)
            pe.wait_ge(S["lf_ev"], 1)
            mm(ps[0][0:NS, 256:256 + H], const("neg_prefix", NS), lft[0:NS, 2, :], start=True, stop=True
               ).then_inc(S["own_mm"], 1)
            for g in range(2):
                for h in range(H):
                    rows = slice(64 * (h % 2), 64 * (h % 2) + 64)
                    last = mm(ps[2 * g + h % 2][0:NS, h // 2 * NS:(h // 2 + 1) * NS], qkT[rows, 8 * g + 4 + h // 2, NP:],
                              qkT[rows, 8 * g + h // 2, NP:], start=True, stop=True)
                last.then_inc(S["own_mm"], 1)
            pe.wait_ge(S["ktok_ev"], 6)
            pe.wait_ge(S["logf_pre"], 1)
            tsum = small[:, 0:128].rearrange("p (c h) -> p c h", c=16)
            later = small[:, 128:256].rearrange("p (c h) -> p c h", c=16)
            bank = ps[5][:, :].rearrange("p (c t h) -> p c t h", c=16, t=4)
            mm(ps[5][:, :], const("suf_lo"), logf_raw, start=True, stop=False)
            mm(ps[5][:, :], const("suf_same"), logf_tb, start=False, stop=False)
            mm(bank, const("suf_page"), tsum.unsqueeze(2).broadcast_to([P, 16, 4, H]), start=False, stop=False)
            mm(bank, ones, later.unsqueeze(2).broadcast_to([P, 16, 4, H]), start=False, stop=True
               ).then_inc(S["suf_mm"], 1)
            for r in range(4, 12):
                ada_mm(r)
                if r > 4:
                    ada_tp(r - 1)
            ada_tp(11)

            def head_rows(n):
                return slice(64 * (n % 2), 64 * (n % 2) + 64), 8 * (n // H) + n % H // 2

            def prompt_scores(n):
                rows, c = head_rows(n)
                if n >= 2:
                    pe.wait_ge(S["pr_max"], 3 * (n - 2) + 2)
                else:
                    pe.wait_ge(S["own_done"], 2)
                q, k = qkT[rows, c, :], qkT[rows, c + 4, :]
                mm(ps[n % 2][:, 0:P], q[:, 0:P], k[:, 0:P], start=True, stop=True)
                mm(ps[n % 2][:, P:3 * P], q[:, P:NP], k[:, 0:NP], start=True, stop=True).then_inc(S["pr_smm"], 1)

            def prompt_transpose(n):
                pe.wait_ge(S["pr_norm"], n + 1)
                if n >= 2:
                    pe.wait_ge(S["pr_pt"], n - 1)
                for j in range(3):
                    last = tp(ps[2 + n % 2][:, j * P:(j + 1) * P], pr_s[:, n % 2, j * P:(j + 1) * P], ident)
                last.then_inc(S["pr_tp"], 1)

            def prompt_pv(n):
                rows, _ = head_rows(n)
                pe.wait_ge(S["pr_pt"], n + 1)
                if n >= 2:
                    pe.wait_ge(S["pr_out"], n - 1)
                elif n == 0:
                    pe.wait_ge(S["mod_ev"], 12)
                else:
                    pe.wait_ge(S["suf_done"], 1)
                cols = slice(n % H * HD, (n % H + 1) * HD)
                o = ps[4 + n % 2]
                mm(o[rows, 0:P], v_tok[:, n // H, 0, cols], pr_pt[:, n % 2, 0:P], start=True, stop=True)
                mm(o[rows, P:NP], v_tok[:, n // H, 0, cols], pr_pt[:, n % 2, P:NP], start=True, stop=False)
                mm(o[rows, P:NP], v_tok[:, n // H, 1, cols], pr_pt[:, n % 2, NP:3 * P], start=False, stop=True
                   ).then_inc(S["pr_pv"], 1)

            for n in range(16 + 2):
                if n < 16:
                    prompt_scores(n)
                if 1 <= n < 17:
                    prompt_transpose(n - 1)
                if n >= 2:
                    prompt_pv(n - 2)

            def unit_scores(u, quarter):
                if quarter == 0:
                    pe.wait_ge(S["qcur"], u.times(1, 1))
                    pe.wait_ge(S["kt_ready"], u.times(2, 2))
                ktv = kt[u.par].rearrange("p q (c n) -> p q c n", c=16)
                for h in (2 * quarter, 2 * quarter + 1):
                    rows = slice(32 * (h % 4), 32 * (h % 4) + 32)
                    o = ps[0][rows, h // 4 * 256:h // 4 * 256 + 256].rearrange("p (q n) -> p q n", q=2)
                    for e in range(2):
                        last = mm(o, q_cur[:, u.g, 2 * h + e, :], ktv[:, :, 2 * h + e, :], start=(e == 0),
                                  stop=(e == 1))
                if quarter == 3:
                    last.then_inc(S["scores"], 1)

            def turn_scores(u):
                pe.wait_ge(S["s_copied"], u.times(1, 1))
                if u.c >= 1:
                    pe.wait_ge(S["s_added"], u.times(1))
                for half in range(2):
                    for q in range(2):
                        at = (q * 2 + half) * P
                        last = tp(ps[1][:, at:at + P], s_nat[:, (half * 2 + q) * P:(half * 2 + q + 1) * P], ident)
                last.then_inc(S["s_turned"], 1)

            def unit_gate(u):
                pe.wait_ge(S["gt_ready"], u.count(0, 1) + 1)
                mm(ps[2][:, 0:P], const("half0"), gt_sum, start=True, stop=True)
                mm(ps[2][:, P:2 * P], const("half1"), gt_sum, start=True, stop=True).then_inc(S["gate_mm"], 1)

            def unit_max(u):
                pe.wait_ge(S["max_part"], u.times(1, 1))
                tp(ps[3][:, 0:P], mx_b[:], ident).then_inc(S["max_t"], 1)

            def unit_bcast(u):
                pe.wait_ge(S["diag"], u.times(1, 1))
                mm(ps[4][:, 0:64], const("ones", 64), mx_diag[:], start=True, stop=True).then_inc(S["max_bc"], 1)

            def unit_sum(u):
                pe.wait_ge(S["p_add"], u.times(1, 1))
                if u.c >= 1:
                    pe.wait_ge(S["o_done"], u.times(2))
                mm(ps[5][:, 0:64], ones, l_part[:, u.par, :], start=True, stop=True).then_inc(S["lsum"], 1)

            def unit_pv(u, c):
                if c == 0:
                    pe.wait_ge(S["p_exp"], u.times(1, 1))
                    pe.wait_ge(pages_v_in[u.slot], u.in_slot(1) * (16 * PAGES))
                    if u.c >= 1:
                        pe.wait_ge(S["o_copied"], u.times(1))
                vv = slot[u.slot][:, 4096:].rearrange("p (g n) -> p g n", g=8)
                o = ps[6][32 * c:32 * c + 16, 0:P]
                for j in range(8):
                    last = mm(o, p_tile[:, u.par, 64 * j + 16 * c:64 * j + 16 * c + 16], vv[:, j, c * P:(c + 1) * P],
                              start=(j == 0), stop=False)
                if c == PC - 1:
                    last.then_inc(ring_free[u.slot], 1)
                last = mm(o, p_tile[0:NS, u.par, 512 + 16 * c:528 + 16 * c], v_tok[0:NS, u.g, 2, c * P:(c + 1) * P],
                          start=False, stop=True)
                if c == PC - 1:
                    last.then_inc(S["pv"], 1)

            def turn_output(u):
                pe.wait_ge(S["o_copied"], u.times(1, 1))
                tp(ps[7][:, 0:P], o_nat, ident).then_inc(S["o_turned"], 1)

            def unit_step(u, nxt, prev, old):
                turn_scores(u)
                if nxt is not None:
                    unit_scores(nxt, 0)
                if old is not None:
                    turn_output(old)
                if u.g == 1:
                    unit_gate(u)
                if nxt is not None:
                    unit_scores(nxt, 1)
                    unit_scores(nxt, 2)
                unit_max(u)
                if nxt is not None:
                    unit_scores(nxt, 3)
                if prev is not None:
                    unit_pv(prev, 0)
                unit_bcast(u)
                if prev is not None:
                    for c in range(1, PC):
                        unit_pv(prev, c)
                    unit_sum(prev)

            pe.wait_ge(S["pr_out"], 16)
            pe.wait_ge(S["o_init"], 1)
            for quarter in range(4):
                unit_scores(Unit(0), quarter)
            for c in range(2):
                unit_step(Unit(c), Unit(c + 1), Unit(c - 1) if c else None, None)
            with pe.Fori(0, 2) as turn:
                for j in range(6):
                    u = Unit(2 + j, turn)
                    unit_step(u, u.step(1), u.step(-1), u.step(-2))
            for c in range(14, NU):
                unit_step(Unit(c), Unit(c + 1) if c + 1 < NU else None, Unit(c - 1), Unit(c - 2))
            turn_output(Unit(14))
            for c in range(PC):
                unit_pv(Unit(15), c)
            unit_sum(Unit(15))
            turn_output(Unit(15))

            for g in range(2):
                sum_squares(g, sq, range(g * PC, (g + 1) * PC), S["osq"], 0, S["ossq"])
            pe.wait_ge(S["on_done"], KC)
            pe.wait_ge(ring_in[1], 16 * (WLOADS[1] + PAGES * 5 + 1))
            wv = slot[1].rearrange("p (k e) -> p k e", k=KC)
            for m in range(KC):
                if m >= 4:
                    pe.wait_ge(S["wo_done"], m - 3)
                for k in range(KC):
                    last = mm(ps[2 + m % 4][:, 0:NT], wv[:, k, m * P:(m + 1) * P], oT[:, k, :],
                              start=(k == 0), stop=(k == KC - 1))
                last.then_inc(S["wo_mm"], 1)
            sum_squares(0, sq, range(KC), S["sq2"], 0, S["ssq2"], ring_free[1])
            pe.wait_ge(S["h2_done"], KC)
            for t, (t0, n) in enumerate(TILES):
                for k in range(KC):
                    last = mm(ps[1][0:n, 36 * t:36 * t + 36], hT[:, k, t0:t0 + n], wr[:, k, :],
                              start=(k == 0), stop=(k == KC - 1))
            last.then_inc(S["r_mm"], 1)
            for r in range(12):
                src = (xT, hT)[r // 6]
                t, hf = r % 6 // 2, r % 2
                t0, n = TILES[t]
                if r == 0:
                    pe.wait_ge(S["wo_done"], KC)
                if r >= 4:
                    pe.wait_ge(S["htok_ev" if r % 2 == 0 else "v_moe"], (r - 4) // 2 + 1)
                for c in range(4):
                    last = tp(ps[4 + r % 4][0:n, c * P:(c + 1) * P], src[:, 4 * hf + c, t0:t0 + n], ident)
                last.then_inc(S["htok_tp"], 1)
            pe.wait_ge(S["sel_rdy"], 1)
            for t in range(3):
                for j in range(t):
                    mm(ps[2][:, 32 * t:32 * t + 32], ones, Asum[:, j, :], start=(j == 0), stop=False)
                mm(ps[2][:, 32 * t:32 * t + 32], const("before"), Asum[:, t, :], start=(t == 0), stop=True)
            for t in range(3):
                last = mm(ps[2][:, 96:128], ones, Asum[:, t, :], start=(t == 0), stop=(t == 2))
            last.then_inc(S["rank_mm"], 1)
            pe.wait_ge(S["tabs"], 1)
            pe.wait_ge(S["htok_ev"], 6)
            pe.wait_ge(S["v_moe"], 6)
            for k in range(KC):
                if k >= 2:
                    pe.wait_ge(S["sort_a"], k - 1)
                    pe.wait_ge(S["sort_v"], k - 1)
                for lo, hi, bank in ((0, 512, 2 * (k % 2)), (512, ASSIGN, 2 * (k % 2) + 1)):
                    for t, (_, n) in enumerate(TILES):
                        if k == 0 and lo == 0:
                            pe.wait_ge(S["onehot"], 2 * t + 2)
                        last = mm(ps[bank][:, 0:hi - lo], h_tok[0:n, t, k * P:(k + 1) * P], place1[0:n, t, lo:hi],
                                  start=(t == 0), stop=(t == 2))
                last.then_inc(S["sort_mm"], 1)
            gate2 = modT[:, MOD_GATE2 * KC:(MOD_GATE2 + 1) * KC, :]
            for k in range(KC):
                last = tp(ps[6 + k // 4][0:NSEQ, k % 4 * P:(k % 4 + 1) * P], gate2[:, k, :], ident)
            last.then_inc(S["g2_tp"], 1)
            pe.wait_ge(S["g2_ev"], 1)
            pe.wait_ge(S["seq_in"], 16)
            for r in range(6):
                t, hf = r // 2, r % 2
                t0, n = TILES[t]
                if r >= 2:
                    pe.wait_ge(S["gt_ev"], r - 1)
                mm(ps[4 + r % 2][0:n, :], seq_oh[:, t0:t0 + n], g2_row[:, 512 * hf:512 * hf + 512],
                   start=True, stop=True).then_inc(S["gt_mm"], 1)
            pe.wait_ge(S["gt_ev"], 6)

            def block_hidden(k, par, done):
                for c in range(KC):
                    last = mm(ps[par][0:BLK, :], h_cur[:, par, c, :], w13_of[k][:, c, :],
                              start=(c == 0), stop=(c == KC - 1))
                last.then_inc(done, 1)

            def block_turn(par):
                for f in range(FC):
                    last = tp(ps[6][:, f * P:(f + 1) * P], hid[:, par, f * P:(f + 1) * P], ident)
                last.then_inc(S["hid_tp"], 1)

            def block_out(k, par, done, freed):
                for hf in range(2):
                    for f in range(FC):
                        last = mm(ps[2 + 2 * par + hf][0:BLK, :], hid_t[:, par, f, :],
                                  w2_of[k][:, f, 512 * hf:512 * hf + 512], start=(f == 0), stop=(f == FC - 1))
                    if hf == 0:
                        last.then_inc(done, 1)
                last.then_inc(freed, 1)

            def step_hidden(e, k, turn):
                pe.wait_ge(exp_in[k], turn * 48 + 48)
                pe.wait_ge(S["hx"], e + 1)
                if not (isinstance(e, int) and e < 2):
                    pe.wait_ge(S["hid"], e * 4 - 4)
                block_hidden(k, k % 2, S["h_mm"])

            def step_out(e, k):
                pe.wait_ge(S["hid_t"], e + 1)
                if not (isinstance(e, int) and e < 2):
                    pe.wait_ge(S["y_ev_a"], e - 1)
                    pe.wait_ge(S["y_ev_v"], e - 1)
                block_out(k, k % 2, S["y_mm"], exp_free[k])

            def step_turn(e, k):
                pe.wait_ge(S["hid"], e * 4 + 4)
                if not (isinstance(e, int) and e < 1):
                    pe.wait_ge(S["hid_t"], e)
                block_turn(k % 2)

            for e in range(4):
                step_hidden(e, e, 0)
                if e >= 1:
                    step_out(e - 1, e - 1)
                step_turn(e, e)
            with pe.Fori(0, NE // ES - 1) as turn:
                for k in range(ES):
                    e = turn * ES + ES + k
                    step_hidden(e, k, turn + 1)
                    step_out(e - 1, (k - 1) % ES)
                    step_turn(e, k)
            step_out(NE - 1, ES - 1)
            pe.wait_ge(S["y_ev_a"], NE)
            pe.wait_ge(S["y_ev_v"], NE)
            nov = pe.value_load(nov_i[0:1, 0:1], min_val=0, max_val=MAXOV)
            with pe.If(nov > 0):
                with pe.Fori(0, nov) as i:
                    pe.wait_ge(S["ov_in"], i * 48 + 48)
                    pe.wait_ge(S["ov_hx"], i + 1)
                    block_hidden(0, 0, S["ov_h"])
                    pe.wait_ge(S["ov_hid"], i * 4 + 4)
                    block_turn(0)
                    pe.wait_ge(S["hid_t"], i + NE + 1)
                    pe.wait_ge(S["y_ev_a"], i + NE)
                    pe.wait_ge(S["y_ev_v"], i + NE)
                    block_out(0, 0, S["ov_y"], exp_free[0])


_INS = ['x_prompt', 'x_sample', 'cache_fox_k', 'cache_fox_v', 'cache_fox_logf', 'cache_moba_k', 'cache_moba_v',
        'page_table', 'c_prompt', 'c_sample', 'w_ada', 'b_ada', 'g_attn', 'w_in', 'b_forget', 'g_out_fox',
        'g_out_moba', 't5_bias', 'w_out', 'g_ffn', 'w_router_group', 'b_router_group', 'w_router_expert',
        'b_router_expert', 'w1', 'w3', 'w2', 'g_final']
_CONSTS = [('consts', make_constants), ('dist_onehot', make_distance_onehot), ('seq_onehot', make_sequence_onehot)]
_OUTS = [(1, NP, D), (NB, NQ, D),
         (1, 1, NP, H, HD), (1, 1, NP, H, HD), (1, 1, NP, H), (1, 1, NP, H, HD), (1, 1, NP, H, HD),
         (1, NB, NQ, H, HD), (1, NB, NQ, H, HD), (1, NB, NQ, H), (1, NB, NQ, H, HD), (1, NB, NQ, H, HD)]


def kernel(**inputs):
    import concourse.bacc as bacc
    from concourse.bass_utils import run_bass_kernel_spmd

    arrays = {n: np.ascontiguousarray(inputs[n]) for n in _INS}
    arrays.update({n: make() for n, make in _CONSTS})
    nc = bacc.Bacc("TRN2", target_bir_lowering=False, num_devices=1)
    ins = [nc.dram_tensor(n, a.shape, mybir.dt.from_np(a.dtype), kind="ExternalInput").ap()
           for n, a in arrays.items()]
    outs = [nc.dram_tensor(f"out_{i}", s, F32, kind="ExternalOutput").ap() for i, s in enumerate(_OUTS)]
    trunk_kernel(nc, ins, outs)
    r = run_bass_kernel_spmd(nc, [arrays], core_ids=[0])
    return tuple(r.results[0][f"out_{i}"] for i in range(len(_OUTS)))
```

```python
from contextlib import ExitStack

import numpy as np

import concourse.bass as bass
from concourse import mybir

F32 = mybir.dt.float32
I32 = mybir.dt.int32
U32 = mybir.dt.uint32
ALU = mybir.AluOpType
ACT = mybir.ActivationFunctionType
AX = mybir.AxisListType

P = 128
D = 1024
KC = D // P
NP = 256
NB = 8
NQ = 8
NS = NB * NQ
NT = NP + NS
TILES = [(0, P), (P, P), (2 * P, NS)]
H = 8
HD = 64
W = H * HD
PC = W // P
PAGES = 8
PAGE = 128
NSEQ = NB + 1
NEG = -1.0e30
EPS = 1e-6
NG, EPG = 4, 8
NE = NG * EPG
DE = 256
FC = DE // P
BLK = 64
ASSIGN = 2 * NT
SORTED = ASSIGN + BLK
MAXOV = (ASSIGN - 1) // BLK
BUCKETS = 32
MOD_SHIFT1, MOD_SCALE1, MOD_GATE1, MOD_SHIFT2, MOD_SCALE2, MOD_GATE2 = range(6)

CONST = {}
_at = 0
for _n, _w in [("ident", P), ("ones", P), ("half0", P), ("half1", P), ("causal", 2 * P), ("before", P),
               ("block_id", 2), ("block_no", 4), ("iota32", NE), ("iota_ov", MAXOV),
               ("suf_lo", P), ("suf_same", P), ("suf_page", P), ("own_mask", NS), ("neg_prefix", NS)]:
    if _n == "suf_lo":
        NCONST = _at
    CONST[_n] = (_at, _at + _w)
    _at += _w
NEARLY = _at - NCONST
REV = 256
FWD = 144
WROW = 384 + NQ + FWD


def make_constants():
    c = np.zeros((P, NCONST + NEARLY), np.float32)
    k, m = np.arange(P)[:, None], np.arange(P)[None, :]

    def put(name, v):
        a, b = CONST[name]
        c[:, a:b] = v

    put("ident", k == m)
    put("ones", 1.0)
    put("suf_lo", (k // 32 == m // 32) & (k > m))
    put("suf_same", k // 32 == m // 32)
    put("suf_page", k // 32 > m // 32)
    put("half0", (k < 64) & (m >= 0))
    put("half1", (k >= 64) & (m >= 0))
    put("causal", np.where(np.arange(2 * P)[None, :] <= P + k, 0.0, NEG))
    j, q = np.arange(P)[:, None], np.arange(NS)[None, :]
    put("own_mask", np.where((j // NQ == q // NQ) & (j <= q), 0.0, NEG))
    put("neg_prefix", np.where((j // NQ == q // NQ) & (j <= q), -1.0, 0.0))
    put("before", k < m)
    put("block_id", 2 * np.arange(2)[None, :] + k // 64 + 1)
    put("block_no", np.array([[1, 3, 2, 4]]))
    put("iota32", np.arange(NE)[None, :])
    put("iota_ov", np.arange(MAXOV)[None, :])
    return c


def make_distance_onehot():
    dist = np.concatenate([REV - 1 - np.arange(REV), np.arange(FWD)])
    half = BUCKETS // 2
    large = half + (np.log(np.maximum(dist, 1).astype(np.float32) / half) / np.float32(np.log(P / half))
                    * half).astype(np.int32)
    bucket = np.where(dist < half, dist, np.minimum(large, BUCKETS - 1))
    return (np.arange(BUCKETS)[:, None] == bucket[None, :]).astype(np.float32)


def make_sequence_onehot():
    seq = np.concatenate([np.zeros(NP, int), 1 + np.arange(NS) // NQ])
    return (np.arange(NSEQ)[:, None] == seq[None, :]).astype(np.float32)


def trunk_kernel(nc, ins, outs):
    (x_prompt, x_sample, cache_fox_k, cache_fox_v, cache_fox_logf, cache_moba_k, cache_moba_v, page_table,
     c_prompt, c_sample, w_ada, b_ada, g_attn, w_in, b_forget, g_out_fox, g_out_moba, t5_bias, w_out, g_ffn,
     w_rg, b_rg, w_re, b_re, w1, w3, w2, g_final, consts, dist_onehot, seq_onehot) = ins
    (y_prompt, y_sample, o_fk_p, o_fv_p, o_fl_p, o_mk_p, o_mv_p, o_fk_s, o_fv_s, o_fl_s, o_mk_s, o_mv_s) = outs
    n_phys = cache_fox_k.shape[1]
    cache_k, cache_v = [cache_fox_k, cache_moba_k], [cache_fox_v, cache_moba_v]

    scr_f = nc.dram_tensor("scr_f", (H, NP), F32).ap()
    scr_w = nc.dram_tensor("scr_w", (H, P, WROW), F32).ap()
    scr_y = nc.dram_tensor("scr_y", ((NE + MAXOV) * BLK, D), F32).ap()

    with ExitStack() as ctx:
        def sb(name, shape, dt=F32):
            return ctx.enter_context(nc.sbuf_tensor(name, shape, dt))

        def sem(name):
            return ctx.enter_context(nc.semaphore(name))

        RS = 3
        SLOT = 8 * D
        ES = 4
        ESLOT = 2 * KC * DE + FC * D
        ring = sb("ring", [P, RS * SLOT])
        slot = [ring[:, i * SLOT:(i + 1) * SLOT] for i in range(RS)]
        eplace = [0, 3, 1, 2]
        eslot = [ring[:, i * ESLOT:(i + 1) * ESLOT] for i in eplace]
        w13_of = [s[:, 0:2 * KC * DE].rearrange("p (k n) -> p k n", k=KC) for s in eslot]
        w2_of = [s[:, 2 * KC * DE:].rearrange("p (k n) -> p k n", k=FC) for s in eslot]

        work = sb("work", [P, 19456])
        early = work[:, 13824:13824 + NEARLY]
        xh = sb("xh", [P, 2 * KC * NT])
        xT = xh[:, 0:KC * NT].rearrange("p (k t) -> p k t", k=KC)
        hT = xh[:, KC * NT:].rearrange("p (k t) -> p k t", k=KC)
        oT = hT
        cst = sb("cst", [P, NCONST])

        def const(name, rows=P):
            a, b = CONST[name]
            return cst[0:rows, a:b] if a < NCONST else early[0:rows, a - NCONST:b - NCONST]

        ident, ones = const("ident"), const("ones")
        modT = sb("modT", [P, 6 * KC, NSEQ])
        parT = sb("parT", [P, 72])
        wfg = sb("wfg", [P, KC, H])
        wr = sb("wr", [P, KC, NG + NE])
        brow = sb("brow", [P, NG + NE])
        bfg = sb("bfg", [H, 1])
        t5 = sb("t5", [BUCKETS, H])
        t5_far = sb("t5_far", [P, H])
        rstd = sb("rstd", [P, NT])
        lfT = sb("lfT", [H, NT])
        lft = sb("lft", [P, 3, H])
        table = sb("table", [1, NB * PAGES], I32)
        page_no = sb("page_no", [P, 1], I32)

        def region(a, n):
            return work[:, a:a + n]

        qkT = region(0, 16 * NT).rearrange("p (c t) -> p c t", c=16)
        v_tok = region(5120, 6 * W).rearrange("p (g t n) -> p g t n", g=2, t=3)
        q_rep = region(8192, 2 * D).rearrange("p (g b h e i) -> p g b h e i", g=2, b=NB, h=H, e=2)
        kt = [region(at, 4096).rearrange("p (q n) -> p q n", q=2) for at in (10240, 1024)]
        s_nat = region(0, 512)
        o_nat = region(512, P)
        k_out = region(10240, 6 * W).rearrange("p (g t n) -> p g t n", g=2, t=3)
        fox_tab = region(10240, H * NP).rearrange("p (h t) -> p h t", h=H)
        pr_s = region(12288, 2 * 384).rearrange("p (a n) -> p a n", a=2)
        pr_pt = region(13056, 2 * 384).rearrange("p (a n) -> p a n", a=2)
        moba_tab = region(14336, H * NP).rearrange("p (h t) -> p h t", h=H)
        s_tile = region(14336, 512)
        p_tile = region(14912, 2 * 576).rearrange("p (a n) -> p a n", a=2)
        q_cur = region(16384, 2 * 512).rearrange("p (g c n) -> p g c n", g=2, c=16)
        fox_tab0 = region(16384, H * P).rearrange("p (h t) -> p h t", h=H)
        logf_raw = region(16384, 512)
        logf_tb = region(16896, 512)
        logf_pages = region(5120, PAGE * H)
        logf_turned = region(5120 + PAGE * H, PAGE * H)
        suffix = region(17408, 512)
        far_tab = region(17920, 512)
        own = region(18432, 1024).rearrange("p (g h t) -> p g h t", g=2, h=H)
        x_tok = region(10240, 3 * D).rearrange("p (t d) -> p t d", t=3)
        ada_row = [work[0:NSEQ, 4096:4096 + D].rearrange("p (a n) -> p a n", a=2),
                   xh[0:NSEQ, KC * NT:KC * NT + D].rearrange("p (a n) -> p a n", a=2)]
        c_row = work[0:NSEQ, 0:D]
        par_row = work[0:72, 2 * D:2 * D + P]
        dist_oh = work[0:BUCKETS, 3 * D:3 * D + REV + FWD]
        sq1 = region(0, KC * NT).rearrange("p (k t) -> p k t", k=KC)
        sq = region(14336, KC * NT).rearrange("p (k t) -> p k t", k=KC)
        h_sort = region(0, KC * SORTED).rearrange("p (k t) -> p k t", k=KC)
        h_tok = region(5632, 3 * D).rearrange("p (t d) -> p t d", t=3)
        place1 = region(8704, 3 * ASSIGN).rearrange("p (t n) -> p t n", t=3)
        iota_s = region(10624, ASSIGN)
        x_tok2 = region(11264, 3 * D).rearrange("p (t d) -> p t d", t=3)
        y_st = region(14336, 2 * D).rearrange("p (a d) -> p a d", a=2)
        h_cur = region(16384, 2 * KC * BLK).rearrange("p (a k t) -> p a k t", a=2, k=KC)
        g_tok = xh[:, 0:3 * D].rearrange("p (t d) -> p t d", t=3)
        g2_row = work[0:NSEQ, 17408:17408 + D]
        seq_oh = work[0:NSEQ, 18432:18432 + NT]
        gfin = region(8704, D)
        y_a = region(0, 3 * D).rearrange("p (t d) -> p t d", t=3)
        y_b3 = [region(3072, D), region(4096, D), region(17408, D)]

        small = sb("small", [P, 640])
        c_sig = small[:, 480:480 + KC * NSEQ]
        silu_cT = small[:, 560:560 + KC * NSEQ].rearrange("p (k s) -> p k s", k=KC)
        gt_sum = small[:, 0:128]
        eq4 = small[:, 128:384]
        mx_a = region(16064, 256)
        mx_b = sb("mx_b", [P, P])
        mx_col = sb("mx_col", [64, 1])
        mx_diag = work[0:64, 14848:14912]
        drop = small[:, 384:448]
        pen = small[:, 448:576].rearrange("p (q n) -> p q n", q=2)
        rsum = small[:, 576:640]
        p_half = sb("p_half", [P, 256])
        l_part = p_half[:, 0:128].rearrange("p (a n) -> p a n", a=2)
        pr_m = sb("pr_m", [P, 3, 2])
        pr_l = sb("pr_l", [P, 3, 2])
        pr_p = [pr_s[:, 0], pr_s[:, 1], small[:, 256:640]]

        lg = small[:, 0:108].rearrange("p (t n) -> p t n", t=3)
        rt = sb("rt", [P, 280])
        g8 = rt[:, 0:24].rearrange("p (t n) -> p t n", t=3)
        gm8 = rt[:, 24:48].rearrange("p (t n) -> p t n", t=3)
        e8 = rt[:, 48:72].rearrange("p (t n) -> p t n", t=3)
        em8 = rt[:, 72:96].rearrange("p (t n) -> p t n", t=3)
        gidf = rt[:, 96:120].rearrange("p (t n) -> p t n", t=3)
        eidf = rt[:, 120:144].rearrange("p (t n) -> p t n", t=3)
        goh = rt[:, 144:156].rearrange("p (t n) -> p t n", t=3)
        gex = rt[:, 156:168].rearrange("p (t n) -> p t n", t=3)
        gsum = rt[:, 168:171]
        tex = rt[:, 171:174]
        wt = rt[:, 174:180].rearrange("p (a t) -> p a t", a=2)
        ids = rt[:, 180:186].rearrange("p (a t) -> p a t", a=2)
        slots = rt[:, 186:192].rearrange("p (a t) -> p a t", a=2)
        poss = rt[:, 192:198].rearrange("p (a t) -> p a t", a=2)
        ss_f = rt[:, 198:201]
        gi8 = sb("gi8", [P, 3, 8], U32)
        ei8 = sb("ei8", [P, 3, 8], U32)
        posu = sb("posu", [P, 6], U32)
        sel_e = small[:, 108:204].rearrange("p (t n) -> p t n", t=3)
        A = mx_a[:, 0:192].rearrange("p (a t n) -> p a t n", a=2, t=3)
        Asum = small[:, 204:300].rearrange("p (t n) -> p t n", t=3)
        rank = small[:, 300:396].rearrange("p (t n) -> p t n", t=3)
        tmp3 = small[:, 396:492].rearrange("p (t n) -> p t n", t=3)
        place_m = small[:, 492:588].rearrange("p (t n) -> p t n", t=3)
        cnt = p_half[:, 0:32]
        start = p_half[:, 32:64]
        extra = p_half[:, 64:96]
        ovb = p_half[:, 96:128]
        base64 = p_half[:, 128:160]
        ov_off = p_half[:, 160:192]
        ones32 = p_half[:, 192:224]
        ov_hi = rt[0:1, 202:234]
        ov_tab = rt[0:1, 234:252].rearrange("p (a n) -> p a n", a=2)
        ov_a = work[0:1, 14336:14336 + MAXOV * NE].rearrange("p (j n) -> p j n", j=MAXOV)
        ov_b = work[0:1, 14336 + MAXOV * NE:14336 + 2 * MAXOV * NE].rearrange("p (j n) -> p j n", j=MAXOV)
        mr = [rstd[:], region(16896, NT)]
        e_sig = work[0:BLK, 17408:17408 + 2 * DE].rearrange("p (a n) -> p a n", a=2)
        hid = region(17408 + 2 * DE, 2 * DE).rearrange("p (a n) -> p a n", a=2)
        hid_t = region(18752, 2 * FC * BLK).rearrange("p (a f t) -> p a f t", a=2, f=FC)
        eps_col = rt[:, 253:254]
        start_i = sb("start_i", [1, NE], I32)
        ov_i = sb("ov_i", [1, 2 * MAXOV], I32)
        nov_i = sb("nov_i", [1, 1], I32)
        assert MAXOV == 9

        ps = [ctx.enter_context(nc.psum_tensor(f"ps{i}", [P, 512], F32)) for i in range(8)]

        ring_in = [sem(f"ring_in{i}") for i in range(RS)]
        pages_v_in = [sem(f"pages_v_in{i}") for i in range(RS)]
        ring_free = [sem(f"ring_free{i}") for i in range(RS)]
        exp_in = [sem(f"exp_in{i}") for i in range(ES)]
        exp_free = [sem(f"exp_free{i}") for i in range(ES)]
        table_in, cst_in, c_in, par_in, x_in, small_in = [sem(n) for n in (
            "table_in", "cst_in", "c_in", "par_in", "x_in", "small_in")]
        y_in = [sem(f"y_in{t}") for t in range(3)]
        names = """fin_x fin_scaled page_no page_in c_exp ada_half ada_mm ada_row mod_tp head_tp head_ev x_tp
            x_ev_a x_ev_v sq_done ssq_done var_done sqrt_done mod_ev h_done fg_mm fg_v fg_a proj_mm proj_a
            proj_v ktok_tp ktok_ev out_dma lf_tp lf_ev f_ready f_dma t5_mm t5_ev w_dma tab_dma own_init
            own_dma own_mm own_done logf_in logf_pre suf_mm suf_done pr_smm pr_max pr_exp pr_norm pr_tp
            pr_pt pr_pv pr_out qrep_a qrep_p qcur_init qcur scores kt_ready s_added s_copied s_turned
            o_copied o_turned o_init gt_ready gate_mm max_part max_t diag max_bc p_sub p_exp p_add lsum pv
            o_done vl vlc vlp hx osq ossq on_done wo_mm wo_done sq2 ssq2 h2_normed h2_prompt r_mm
            lg_ready sel_rdy rank_mm tabs onehot iota_done htok_tp htok_ev g2_tp g2_ev gt_mm gt_ev sort_mm
            sorted h_mm h_exp hid hid_tp hid_t y_mm y_ev_a y_ev_v y_dma0 y_dma1 ov_in ov_hx ov_h ov_exp
            ov_hid ov_y gf_in zero_set zero_dma fin_sq fin_sqrt fin_v fin_out seq_in pad_done r_a""".split()
        S = {n: sem(n) for n in names}

        block = ctx.enter_context(nc.Block())

        class Unit:

            def __init__(self, c, turn=None):
                self.c, self.turn = c, turn
                self.u = c if turn is None else turn * 6 + c
                self.b = c // 2 if turn is None else turn * 3 + c // 2
                self.g = self.par = c % 2
                self.slot = c % RS

            def step(self, n):
                return Unit(self.c + n, self.turn)

            def count(self, fox, moba):
                v = (self.c // 2) * (fox + moba) + (self.c % 2) * fox
                return v if self.turn is None else self.turn * 3 * (fox + moba) + v

            def times(self, n, more=0):
                return self.u * n + more

            def in_slot(self, more):
                n = self.c // RS + more
                return n if self.turn is None else self.turn * 2 + n

        NU = 2 * NB

        PROJ = ([(True, 2, j * P, j) for j in range(8)]
                + [(False, 3, 0, (0, t)) for t in range(3)] + [(True, 3, W + j * P, 8 + j) for j in range(4)]
                + [(True, 4, j * P, 12 + j) for j in range(4)] + [(False, 4, W, (1, t)) for t in range(3)])

        def proj_evac(r):
            transposed, _, _, d = PROJ[r]
            if transposed:
                return qkT[:, d, :], ps[r % 4][:, 0:NT], HD ** -0.5 if d // 4 % 2 == 0 else 1.0
            g, t = d
            n = TILES[t][1]
            return v_tok[0:n, g, t, :], ps[r % 4][0:n, :], 1.0

        def tok_evac(r):
            t, hf = r % 6 // 2, r % 2
            n = TILES[t][1]
            return (x_tok2, h_tok)[r // 6][0:n, t, 512 * hf:512 * hf + 512], ps[4 + r % 4][0:n, :]

        ADA_AT = [0, 1, 5, 6, 7, 8]
        WIN_AT = {2: [(0, 1024)], 3: [(1024, 512), (1544, 512)], 4: [(2056, 1024)]}
        WLOADS = [4, 3, 3]

        def key_loads(u):
            n = 16 * (WLOADS[u.slot] + PAGES * (u.c // RS + 1))
            return n if u.turn is None else u.turn * (2 * 16 * PAGES) + n

        def ada_full(r):
            n = ADA_AT[r // 2]
            return (S["ada_mm"], r // 2 + 1) if r % 2 == 0 else (ring_free[n % RS], n // RS + 1)

        @block.sync
        def _(sp):
            sp.dma_start(c_row[0:1, :], c_prompt).then_inc(c_in, 16)
            sp.dma_start(c_row[1:NSEQ, :], c_sample).then_inc(c_in, 16)
            sp.dma_start(cst[:], consts[:, 0:NCONST]).then_inc(cst_in, 16)
            ada = w_ada[0].rearrange("(k p) e -> p k e", p=P)
            win = w_in[0].rearrange("(k p) e -> p k e", p=P)
            for n in range(9):
                if n >= RS:
                    sp.wait_ge(ring_free[n % RS], n // RS)
                sv = slot[n % RS].rearrange("p (k e) -> p k e", k=KC)
                if n in WIN_AT:
                    at = 0
                    for c0, w in WIN_AT[n]:
                        sp.dma_start(sv[:, :, at:at + w], win[:, :, c0:c0 + w]).then_inc(ring_in[n % RS], 16)
                        at += w
                elif n == 0:
                    sp.dma_start(sv[:, :, 0:512], ada[:, :, 0:512]).then_inc(S["ada_half"], 16)
                    sp.wait_ge(x_in, 32)
                    sp.wait_ge(par_in, 16 * 5)
                    sp.dma_start(sv[:, :, 512:], ada[:, :, 512:D]).then_inc(ring_in[0], 16)
                else:
                    m = ADA_AT.index(n)
                    sp.dma_start(sv, ada[:, :, m * D:(m + 1) * D]).then_inc(ring_in[n % RS], 16)
            sp.wait_ge(table_in, 16)

            def pages_of(u):
                return [sp.value_load(table[0:1, bass.ds(u.b * PAGES + a, 1)], min_val=0, max_val=n_phys - 1)
                        for a in range(PAGES)]

            def load_keys(u, first, pages):
                kd = slot[u.slot][:, 0:4096].rearrange("p (a n) -> p a n", a=PAGES)
                if first:
                    sp.wait_ge(ring_free[u.slot], 3)
                else:
                    sp.wait_ge(S["kt_ready"], u.times(2, -4))
                for a, page in enumerate(pages):
                    sp.dma_start(kd[:, a, :], cache_k[u.g][0, bass.ds(page, 1)].rearrange("r t h d -> (r t) (h d)")
                                 ).then_inc(ring_in[u.slot], 16)

            def load_values(u, pages):
                vd = slot[u.slot][:, 4096:].rearrange("p (q t n) -> p q t n", q=2, t=4)
                sp.wait_ge(ring_free[u.slot], u.in_slot(3))
                for a, page in enumerate(pages):
                    sp.dma_start(vd[32 * (a % 4):32 * (a % 4) + 32, a // 4, :, :],
                                 cache_v[u.g][0, bass.ds(page, 1)].rearrange("r (t l) h d -> (r l) t (h d)", t=4)
                                 ).then_inc(pages_v_in[u.slot], 16)

            pages = pages_of(Unit(0))
            load_keys(Unit(0), True, pages)
            load_keys(Unit(1), True, pages)
            load_values(Unit(0), pages)
            load_keys(Unit(2), True, pages_of(Unit(2)))
            load_values(Unit(1), pages)
            with sp.Fori(0, 2) as turn:
                pages = pages_of(Unit(2, turn))
                for j in range(0, 6, 2):
                    u = Unit(2 + j, turn)
                    load_keys(u.step(1), False, pages)
                    later = pages_of(u.step(2))
                    load_values(u, pages)
                    load_keys(u.step(2), False, later)
                    load_values(u.step(1), pages)
                    pages = later
            pages = pages_of(Unit(14))
            load_keys(Unit(15), False, pages)
            load_values(Unit(14), pages)
            load_values(Unit(15), pages)
            sp.wait_ge(ring_free[1], 8)
            sp.dma_start(slot[1].rearrange("p (k e) -> p k e", k=KC),
                         w_out[0].rearrange("(k p) e -> p k e", p=P)).then_inc(ring_in[1], 16)

            def load_expert(e, k, inc):
                sp.dma_start(w13_of[k][:, :, 0:DE], w1[0, e].rearrange("(k p) n -> p k n", p=P)).then_inc(inc, 16)
                sp.dma_start(w13_of[k][:, :, DE:], w3[0, e].rearrange("(k p) n -> p k n", p=P)).then_inc(inc, 16)
                sp.dma_start(w2_of[k], w2[0, e].rearrange("(k p) n -> p k n", p=P)).then_inc(inc, 16)

            for e, need in ((0, [(0, 9)]), (1, [(2, 8)]), (2, [(0, 9), (1, 9)]), (3, [(1, 9), (2, 8)])):
                for s, n in need:
                    sp.wait_ge(ring_free[s], n)
                load_expert(e, e, exp_in[e])

            def expert_at(w, e, pat):
                return w[0, bass.ds(e, 1)].rearrange(pat, p=P)

            def load_expert_dyn(e, k, inc):
                sp.dma_start(w13_of[k][:, :, 0:DE], expert_at(w1, e, "o (k p) n -> p (o k) n")).then_inc(inc, 16)
                sp.dma_start(w13_of[k][:, :, DE:], expert_at(w3, e, "o (k p) n -> p (o k) n")).then_inc(inc, 16)
                sp.dma_start(w2_of[k], expert_at(w2, e, "o (k p) n -> p (o k) n")).then_inc(inc, 16)

            with sp.Fori(0, NE // ES - 1) as turn:
                for k in range(ES):
                    sp.wait_ge(exp_free[k], turn + 1)
                    load_expert_dyn(turn * ES + ES + k, k, exp_in[k])
            sp.wait_ge(S["tabs"], 1)
            nov = sp.value_load(nov_i[0:1, 0:1], min_val=0, max_val=MAXOV)
            with sp.If(nov > 0):
                with sp.Fori(0, nov) as i:
                    e = sp.value_load(ov_i[0:1, bass.ds(i + MAXOV, 1)], min_val=0, max_val=NE - 1)
                    sp.wait_ge(exp_free[0], i + NE // ES)
                    load_expert_dyn(e, 0, S["ov_in"])
            sp.wait_ge(S["out_dma"], 16 * 14)
            sp.wait_ge(S["fin_out"], 16 * 3)

        @block.gpsimd
        def _(pool):
            pool.dma_start(table[:], page_table.rearrange("(o b) p -> o (b p)", o=1)).then_inc(table_in, 16)
            nc.gpsimd.memset(page_no[:], 0).then_inc(S["page_no"], 1)
            pool.wait_ge(S["page_no"], 1)
            by_group = page_table.rearrange("b (q a) -> (b q) a", q=2)
            with nc.allow_non_contiguous_dma(reason="sixteen page numbers each"):
                for a in range(4):
                    pool.dma_start(page_no[32 * a:32 * a + 2 * NB, :], by_group[:, a:a + 1]
                                   ).then_inc(S["page_in"], 16)
            pool.wait_ge(S["page_in"], 16 * 4)
            pool.indirect_dma_start(logf_pages, None, cache_fox_logf[0].rearrange("r t h -> r (t h)"),
                                    bass.IndirectOffsetOnAxis(page_no[:, 0:1], 0)).then_inc(S["logf_in"], 16)
            zeros = work[0:BLK, 10240:10240 + D]
            pool.wait_ge(S["x_tp"], KC)
            nc.gpsimd.memset(zeros, 0.0).then_inc(S["zero_set"], 1)
            pool.wait_ge(S["zero_set"], 1)
            pool.dma_start(scr_y[NE * BLK:, :].rearrange("(j p) d -> p j d", p=BLK),
                           zeros.unsqueeze(1).broadcast_to([BLK, MAXOV, D])).then_inc(S["zero_dma"], 16)
            pool.wait_ge(S["proj_a"], 11)
            pool.wait_ge(S["proj_v"], 11)

            n = 0
            for r in range(2):
                for e in range(2):
                    src = qkT[64 * r + 32 * e:64 * r + 32 * e + 32, 8:12, NP:NT] \
                        .rearrange("p c (b i) -> p b c i", b=NB)
                    for tb in range(4):
                        nc.gpsimd.tensor_copy(q_rep[32 * tb:32 * tb + 32, 1, :, r::2, e, :], src
                                              ).then_inc(S["qrep_p"], 1)
                        n += 1
                        pool.wait_ge(S["qrep_p"], n)
            pool.wait_ge(S["pr_max"], 3 * H)
            nc.gpsimd.memset(q_cur, 0.0).then_inc(S["qcur_init"], 1)
            pool.wait_ge(S["qcur_init"], 1)
            pool.wait_ge(S["qrep_a"], 1)

            qr = q_rep.rearrange("p g b h e i -> p g b (h e) i")

            def unit_query(u):
                if u.c >= 2:
                    pool.wait_ge(S["scores"], u.times(1, -1))
                for tb in range(4):
                    last = nc.gpsimd.tensor_copy(
                        q_cur[32 * tb:32 * tb + 32, u.g, :, 8 * tb:8 * tb + 8],
                        qr[32 * tb:32 * tb + 32, u.g, bass.ds(u.b, 1), :, :].rearrange("p o c i -> p (o c) i"))
                last.then_inc(S["qcur"], 1)

            for c in range(2):
                unit_query(Unit(c))
            with pool.Fori(0, 2) as turn:
                for j in range(6):
                    unit_query(Unit(2 + j, turn))
            for c in range(14, NU):
                unit_query(Unit(c))

            pool.wait_ge(S["wo_done"], 1)
            nc.gpsimd.iota(iota_s, pattern=[[1, ASSIGN]], base=0, channel_multiplier=0,
                           allow_small_or_imprecise_dtypes=True).then_inc(S["iota_done"], 1)
            pool.wait_ge(S["sorted"], KC)
            pool.wait_ge(S["pad_done"], 1)
            pool.wait_ge(S["tabs"], 1)

            def block_columns(e, par, first=False):
                r = pool.value_load(start_i[0:1, bass.ds(e, 1)], min_val=0, max_val=ASSIGN)
                if not first:
                    pool.wait_ge(S["h_mm"], e - 1)
                nc.gpsimd.tensor_copy(h_cur[:, par], h_sort[:, :, bass.ds(r, BLK)]).then_inc(S["hx"], 1)

            for e in range(4):
                block_columns(e, e % 2, e < 2)
            with pool.Fori(0, NE // ES - 1) as turn:
                for k in range(ES):
                    block_columns(turn * ES + ES + k, k % 2)
            for par in range(2):
                pool.wait_ge(S[f"y_dma{par}"], 16 * NE // 2)
            nov = pool.value_load(nov_i[0:1, 0:1], min_val=0, max_val=MAXOV)
            with pool.If(nov > 0):
                with pool.Fori(0, nov) as i:
                    r = pool.value_load(ov_i[0:1, bass.ds(i, 1)], min_val=0, max_val=ASSIGN)
                    nc.gpsimd.tensor_copy(h_cur[:, 0], h_sort[:, :, bass.ds(r, BLK)]).then_inc(S["ov_hx"], 1)
                    pool.wait_ge(S["y_dma0"], i * 16 + 16 * (NE // 2 + 1))
            for t, (_, n) in enumerate(TILES):
                for a, y in enumerate((y_a[0:n, t, :], y_b3[t][0:n, :])):
                    pool.indirect_dma_start(y, None, scr_y,
                                            bass.IndirectOffsetOnAxis(posu[0:n, 3 * a + t:3 * a + t + 1], 0)
                                            ).then_inc(y_in[t], 16)

        @block.scalar
        def _(act):
            act.dma_start(x_tok[:, 0:2, :], x_prompt[0].rearrange("(t p) d -> p t d", p=P)).then_inc(x_in, 16)
            act.dma_start(x_tok[0:NS, 2, :], x_sample.rearrange("b i d -> (b i) d")).then_inc(x_in, 16)
            at = 0
            for v, n in ((b_ada, 48), (g_attn, 8), (g_ffn, 8), (g_out_fox, 4), (g_out_moba, 4)):
                act.dma_start(par_row[at:at + n, :], v[0].rearrange("(a p) -> a p", p=P)).then_inc(par_in, 16)
                at += n
            act.wait_ge(S["head_tp"], 1)
            nc.scalar.activation(c_sig, ps[4][:, 0:KC * NSEQ], ACT.Exp, scale=-1.0).then_inc(S["c_exp"], 1)
            act.dma_start(wfg[:], w_in[0].rearrange("(k p) e -> p k e", p=P)[:, :, 3 * W:3 * W + H]
                          ).then_inc(small_in, 16)
            act.dma_start(wr[:, :, 0:NG], w_rg[0].rearrange("(k p) e -> p k e", p=P)).then_inc(small_in, 16)
            act.dma_start(wr[:, :, NG:], w_re[0].rearrange("(k p) e -> p k e", p=P)).then_inc(small_in, 16)
            act.dma_start(brow[:, 0:NG], b_rg.partition_broadcast(P).rearrange("p o n -> p (o n)")
                          ).then_inc(small_in, 16)
            act.dma_start(brow[:, NG:], b_re.partition_broadcast(P).rearrange("p o n -> p (o n)")
                          ).then_inc(small_in, 16)
            act.dma_start(bfg[:], b_forget.rearrange("o h -> h o")).then_inc(small_in, 16)
            act.dma_start(t5[:], t5_bias).then_inc(small_in, 16)
            act.dma_start(t5_far[:], t5_bias[BUCKETS - 1:BUCKETS, :].partition_broadcast(P)
                          .rearrange("p o n -> p (o n)")).then_inc(small_in, 16)
            act.dma_start(dist_oh, dist_onehot).then_inc(small_in, 16)
            act.dma_start(early, consts[:, NCONST:]).then_inc(small_in, 16)
            for k in range(0, KC, 2):
                act.wait_ge(S["x_tp"], k + 1)
                nc.scalar.copy(xT[:, k, :], ps[k % 4][:, 0:NT]).then_inc(S["x_ev_a"], 1)
            for k in range(KC):
                act.wait_ge(*((S["x_ev_a"], k // 2 + 1) if k % 2 == 0 else (S["x_ev_v"], k // 2 + 1)))
                if k == 0:
                    act.wait_ge(S["head_ev"], 2)
                nc.scalar.activation(sq1[:, k, :], xT[:, k, :], ACT.Square).then_inc(S["sq_done"], 1)
            def ada_evac(r):
                act.wait_ge(*ada_full(r))
                nc.scalar.copy(ada_row[r // 4 > 0][:, r % 2, :], ps[6 + r % 2][0:NSEQ, :]).then_inc(S["ada_row"], 1)

            ada_evac(0)
            act.wait_ge(S["var_done"], 1)
            nc.scalar.activation(rstd[:], rstd[:], ACT.Sqrt).then_inc(S["sqrt_done"], 1)
            for r in range(1, 4):
                ada_evac(r)
            act.wait_ge(S["fg_v"], 2)
            nc.scalar.activation(work[0:H, 16000:16000 + NT], work[0:H, 15500:15500 + NT], ACT.Exp, scale=-1.0
                                 ).then_inc(S["fg_a"], 1)
            act.wait_ge(S["fg_v"], 3)
            nc.scalar.activation(work[0:H, 16000:16000 + NT], work[0:H, 16000:16000 + NT], ACT.Ln
                                 ).then_inc(S["fg_a"], 1)
            for r in range(0, 22, 2):
                act.wait_ge(S["proj_mm"], r + 1)
                dst, src, scale = proj_evac(r)
                nc.scalar.activation(dst, src, ACT.Copy, scale=scale).then_inc(S["proj_a"], 1)
            act.wait_ge(S["proj_a"], 11)
            act.wait_ge(S["proj_v"], 11)
            for r in range(2):
                for e in range(2):
                    src = qkT[64 * r + 32 * e:64 * r + 32 * e + 32, 0:4, NP:NT] \
                        .rearrange("p c (b i) -> p b c i", b=NB)
                    for tb in range(4):
                        last = nc.scalar.copy(q_rep[32 * tb:32 * tb + 32, 0, :, r::2, e, :], src)
            last.then_inc(S["qrep_a"], 1)
            for g, (kp, ks_, vp, vs) in enumerate(((o_fk_p, o_fk_s, o_fv_p, o_fv_s),
                                                   (o_mk_p, o_mk_s, o_mv_p, o_mv_s))):
                kpv = kp[0, 0].rearrange("(t p) h d -> p t (h d)", p=P)
                vpv = vp[0, 0].rearrange("(t p) h d -> p t (h d)", p=P)
                for t in range(2):
                    act.dma_start(vpv[:, t, :], v_tok[:, g, t, :]).then_inc(S["out_dma"], 16)
                act.dma_start(vs[0].rearrange("b i h d -> (b i) (h d)"), v_tok[0:NS, g, 2, :]
                              ).then_inc(S["out_dma"], 16)
                for t in range(2):
                    act.wait_ge(S["ktok_ev"], 3 * g + t + 1)
                    act.dma_start(kpv[:, t, :], k_out[:, g, t, :]).then_inc(S["out_dma"], 16)
                act.wait_ge(S["ktok_ev"], 3 * g + 3)
                act.dma_start(ks_[0].rearrange("b i h d -> (b i) (h d)"), k_out[0:NS, g, 2, :]
                              ).then_inc(S["out_dma"], 16)
            act.wait_ge(S["lf_ev"], 1)
            act.dma_start(o_fl_p[0, 0].rearrange("(t p) h -> p t h", p=P), lft[:, 0:2, :]).then_inc(S["out_dma"], 16)
            act.dma_start(o_fl_s[0].rearrange("b i h -> (b i) h"), lft[0:NS, 2, :]).then_inc(S["out_dma"], 16)
            act.wait_ge(S["f_ready"], 2)
            act.dma_start(scr_f, work[0:H, 15500:15500 + NP]).then_inc(S["f_dma"], 16)
            act.wait_ge(S["t5_ev"], 3)
            act.dma_start(scr_w, work[0:H, 17408:17408 + WROW].unsqueeze(1).broadcast_to([H, P, WROW])
                          ).then_inc(S["w_dma"], 16)
            for r in range(4, 8):
                ada_evac(r)
            act.wait_ge(S["f_dma"], 16)
            act.wait_ge(S["out_dma"], 16 * 14)
            act.dma_start(fox_tab, scr_f.partition_broadcast(P)).then_inc(S["tab_dma"], 16)
            act.wait_ge(S["w_dma"], 16)

            def shifted(offset, n, width):
                return bass.AP(scr_w.tensor, offset, [[WROW - 1, n], [P * WROW, H], [1, width]])

            act.dma_start(moba_tab, shifted(P - 1, P, NP)
                          ).then_inc(S["w_dma"], 16)
            act.wait_ge(S["own_init"], 2)
            ft = far_tab.rearrange("p (q h t i) -> p q h t i", q=2, h=H, t=4)
            for t in range(4):
                act.dma_start(ft[96:128, 1, :, t, :], shifted(384 + NQ + P - 32 * t, 32, NQ)
                              ).then_inc(S["own_dma"], 16)
            for b in range(NB):
                act.dma_start(own[NQ * b:NQ * b + NQ, 1, :, NQ * b:NQ * b + NQ],
                              shifted(384 + NQ, NQ, NQ)
                              ).then_inc(S["own_dma"], 16)
            for r in range(8, 12):
                ada_evac(r)
            def prompt_turned(n):
                act.wait_ge(S["pr_tp"], n + 1)
                nc.scalar.copy(pr_pt[:, n % 2, :], ps[2 + n % 2][:, 0:384]).then_inc(S["pr_pt"], 1)

            for n in range(16):
                act.wait_ge(S["pr_max"], 3 * (n + 1))
                for j in range(2):
                    a, b = (0, P) if j == 0 else (P, 3 * P)
                    nc.scalar.activation(pr_p[n % 3][:, a:b], pr_p[n % 3][:, a:b], ACT.Exp,
                                         bias=pr_m[:, n % 3, j:j + 1], accum_out=pr_l[:, n % 3, j:j + 1]
                                         ).then_inc(S["pr_exp"], 1)
                if n >= 2:
                    prompt_turned(n - 2)
            for n in (14, 15):
                prompt_turned(n)

            def copy_scores(u):
                act.wait_ge(S["scores"], u.times(1, 1))
                nc.scalar.copy(s_nat, ps[0][:, :]).then_inc(S["s_copied"], 1)

            def unit_exp(u):
                act.wait_ge(S["p_sub"], u.times(3, 3))
                nc.scalar.activation(p_tile[:, u.par, :], p_tile[:, u.par, :], ACT.Exp).then_inc(S["p_exp"], 1)

            def copy_output(u):
                act.wait_ge(S["pv"], u.times(1, 1))
                nc.scalar.copy(o_nat, ps[6][:, 0:P]).then_inc(S["o_copied"], 1)

            copy_scores(Unit(0))
            for c in range(2):
                copy_scores(Unit(c + 1))
                unit_exp(Unit(c))
                if c:
                    copy_output(Unit(0))
            with act.Fori(0, 2) as turn:
                for j in range(6):
                    u = Unit(2 + j, turn)
                    copy_scores(u.step(1))
                    unit_exp(u)
                    copy_output(u.step(-1))
            for c in range(14, NU):
                if c + 1 < NU:
                    copy_scores(Unit(c + 1))
                unit_exp(Unit(c))
                copy_output(Unit(c - 1))
            copy_output(Unit(NU - 1))
            act.wait_ge(S["o_done"], 2 * NU)
            act.wait_ge(S["pr_out"], 16)
            for k in range(KC):
                nc.scalar.activation(sq[:, k, :], oT[:, k, :], ACT.Square).then_inc(S["osq"], 1)
            for g in range(2):
                act.wait_ge(S["var_done"], 2 + g)
                nc.scalar.activation(mr[g], mr[g], ACT.Sqrt).then_inc(S["sqrt_done"], 1)
            for k in range(KC):
                act.wait_ge(S["wo_done"], k + 1)
                nc.scalar.activation(sq[:, k, :], xT[:, k, :], ACT.Square).then_inc(S["sq2"], 1)
            act.wait_ge(S["var_done"], 4)
            nc.scalar.activation(rstd[:], rstd[:], ACT.Sqrt).then_inc(S["sqrt_done"], 1)
            act.dma_start(seq_oh, seq_onehot).then_inc(S["seq_in"], 16)
            for k in range(KC):
                act.wait_ge(S["h2_normed"], k + 1)
                a, b = [modT[:, m * KC + k, 0:1] for m in (MOD_SCALE2, MOD_SHIFT2)]
                nc.scalar.activation(hT[:, k, 0:NP], hT[:, k, 0:NP], ACT.Identity, scale=a, bias=b
                                     ).then_inc(S["h2_prompt"], 1)
            for r in range(12):
                act.wait_ge(S["htok_tp"], r + 1)
                dst, src = tok_evac(r)
                nc.scalar.copy(dst, src).then_inc(S["htok_ev"], 1)
            act.wait_ge(S["lg_ready"], 1)
            nc.scalar.activation(gex, gex, ACT.Exp).then_inc(S["r_a"], 1)
            act.wait_ge(S["lg_ready"], 2)
            nc.scalar.activation(tex, tex, ACT.Exp).then_inc(S["r_a"], 1)
            act.wait_ge(S["g2_tp"], 1)
            for hf in range(2):
                nc.scalar.copy(g2_row[:, 512 * hf:512 * hf + 512], ps[6 + hf][0:NSEQ, :]).then_inc(S["g2_ev"], 1)

            def gate_rows(r):
                act.wait_ge(S["gt_mm"], r + 1)
                t, hf = r // 2, r % 2
                n = TILES[t][1]
                nc.scalar.copy(g_tok[0:n, t, 512 * hf:512 * hf + 512], ps[4 + r % 2][0:n, :]).then_inc(S["gt_ev"], 1)
            for r in range(3):
                gate_rows(r)
            for k in range(KC):
                act.wait_ge(S["sort_mm"], k + 1)
                nc.scalar.copy(h_sort[:, k, 0:512], ps[2 * (k % 2)][:, 0:512])
                nc.scalar.copy(h_sort[:, k, 512:ASSIGN], ps[2 * (k % 2) + 1][:, 0:ASSIGN - 512]
                               ).then_inc(S["sorted"], 1)
            for r in range(3, 6):
                gate_rows(r)
            act.wait_ge(S["onehot"], 6)
            act.wait_ge(S["sort_mm"], KC)
            act.dma_start(gfin, g_final.rearrange("(o d) -> o d", o=1).partition_broadcast(P)
                          .rearrange("p o n -> p (o n)")).then_inc(S["gf_in"], 16)

            def block_exp(e, par, hidden_full, done):
                act.wait_ge(hidden_full, e + 1)
                nc.scalar.activation(e_sig[:, par, :], ps[par][0:BLK, 0:DE], ACT.Exp, scale=-1.0).then_inc(done, 1)

            def block_turned(e, par):
                act.wait_ge(S["hid_tp"], e + 1)
                nc.scalar.copy(hid_t[:, par, :, :], ps[6][:, 0:FC * P].rearrange("p (f t) -> p f t", f=FC)[:, :, 0:BLK]
                               ).then_inc(S["hid_t"], 1)

            def block_y_act(e, par, before):
                act.wait_ge(S["y_mm"], e + 1)
                if before is not None:
                    act.wait_ge(S[f"y_dma{par}"], before * 16)
                nc.scalar.copy(y_st[0:BLK, par, 0:512], ps[2 + 2 * par][0:BLK, :]).then_inc(S["y_ev_a"], 1)

            def store_block(e, par):
                act.wait_ge(S["y_ev_a"], e + 1)
                act.wait_ge(S["y_ev_v"], e + 1)
                act.dma_start(scr_y[bass.ds(e * BLK, BLK), :], y_st[0:BLK, par, :]).then_inc(S[f"y_dma{par}"], 16)

            block_exp(0, 0, S["h_mm"], S["h_exp"])
            for e in range(1, 4):
                block_exp(e, e % 2, S["h_mm"], S["h_exp"])
                if e == 1:
                    block_turned(0, 0)
                block_y_act(e - 1, (e - 1) % 2, 1 if e == 3 else None)
                block_turned(e, e % 2)
                store_block(e - 1, (e - 1) % 2)
            with act.Fori(0, NE // ES - 1) as turn:
                for k in range(ES):
                    e = turn * ES + ES + k
                    block_exp(e, k % 2, S["h_mm"], S["h_exp"])
                    block_y_act(e - 1, (k - 1) % 2, turn * 2 + (k + 3) // 2)
                    block_turned(e, k % 2)
                    store_block(e - 1, (k - 1) % 2)
            block_y_act(NE - 1, 1, NE // 2 - 1)
            store_block(NE - 1, 1)
            nov = act.value_load(nov_i[0:1, 0:1], min_val=0, max_val=MAXOV)
            with act.If(nov > 0):
                with act.Fori(0, nov) as i:
                    block_exp(i, 0, S["ov_h"], S["ov_exp"])
                    block_turned(i + NE, 0)
                    act.wait_ge(S["y_dma0"], i * 16 + 16 * (NE // 2))
                    act.wait_ge(S["ov_y"], i + 1)
                    nc.scalar.copy(y_st[0:BLK, 0, 0:512], ps[2][0:BLK, :]).then_inc(S["y_ev_a"], 1)
                    store_block(i + NE, 0)
            def final_scale(t):
                n = TILES[t][1]
                act.wait_ge(y_in[t], 32)
                nc.scalar.activation(y_a[0:n, t, :], y_a[0:n, t, :], ACT.Copy, scale=wt[0:n, 0, t:t + 1]
                                     ).then_inc(S["fin_scaled"], 1)

            def final_root(t):
                n = TILES[t][1]
                ss = ss_f[0:n, t:t + 1]
                act.wait_ge(S["fin_x"], t + 1)
                nc.scalar.activation(y_b3[t][0:n, :], x_tok2[0:n, t, :], ACT.Square, accum_out=ss
                                     ).then_inc(S["fin_sq"], 1)
                act.wait_ge(S["fin_sq"], t + 1)
                nc.scalar.activation(ss, ss, ACT.Sqrt, scale=1.0 / D, bias=eps_col[0:n, :]).then_inc(S["fin_sqrt"], 1)

            for t in range(3):
                final_scale(t)
                if t:
                    final_root(t - 1)
            final_root(2)
            act.wait_ge(S["fin_v"], 2)
            act.dma_start(y_prompt[0].rearrange("(t p) d -> p t d", p=P)[:, 0], x_tok2[:, 0, :]
                          ).then_inc(S["fin_out"], 16)
            act.wait_ge(S["fin_v"], 4)
            act.dma_start(y_prompt[0].rearrange("(t p) d -> p t d", p=P)[:, 1], x_tok2[:, 1, :]
                          ).then_inc(S["fin_out"], 16)
            act.wait_ge(S["fin_v"], 6)
            act.dma_start(y_sample.rearrange("b i d -> (b i) d"), x_tok2[0:NS, 2, :]).then_inc(S["fin_out"], 16)

        @block.vector
        def _(v):
            chain = [0]

            def link(ins):
                chain[0] += 1
                ins.then_inc(S["vl"], 1)
                v.wait_ge(S["vl"], chain[0])

            tt, ts, stt = nc.vector.tensor_tensor, nc.vector.tensor_scalar, nc.vector.scalar_tensor_tensor

            nc.vector.memset(mx_b[:], 0.0)
            v.wait_ge(S["c_exp"], 1)
            link(ts(c_sig, c_sig, 1.0, None, ALU.add))
            link(nc.vector.reciprocal(c_sig, c_sig))
            tt(silu_cT, ps[4][:, 0:KC * NSEQ].rearrange("p (k s) -> p k s", k=KC),
               c_sig.rearrange("p (k s) -> p k s", k=KC), ALU.mult).then_inc(S["head_ev"], 1)
            bias_rows = work[0:H, 17408:17408 + WROW]
            nc.vector.memset(bias_rows, NEG).then_inc(S["t5_ev"], 1)
            for k in range(1, KC, 2):
                v.wait_ge(S["x_tp"], k + 1)
                nc.vector.tensor_copy(xT[:, k, :], ps[k % 4][:, 0:NT]).then_inc(S["x_ev_v"], 1)

            v.wait_ge(S["head_tp"], 2)
            nc.vector.tensor_copy(parT[:], ps[5][:, 0:72]).then_inc(S["head_ev"], 1)

            rms = [0]

            def inv_rms(dst, src, n):
                ts(dst, src, 1.0 / n, EPS, ALU.mult, ALU.add).then_inc(S["var_done"], 1)
                rms[0] += 1
                v.wait_ge(S["sqrt_done"], rms[0])
                link(nc.vector.reciprocal(dst, dst))

            def normed(dst, src):
                return tt(dst, src, rstd[:].unsqueeze(1).broadcast_to([P, KC, NT]), ALU.mult)

            def modulate_sample(x, m_scale, m_shift):
                sv = x[:, :, NP:].rearrange("p k (b i) -> p k b i", b=NB)
                a = modT[:, m_scale * KC:(m_scale + 1) * KC, :]
                s = modT[:, m_shift * KC:(m_shift + 1) * KC, :]
                link(tt(sv, sv, a[:, :, 1:].unsqueeze(3).broadcast_to([P, KC, NB, NQ]), ALU.mult))
                return tt(sv, sv, s[:, :, 1:].unsqueeze(3).broadcast_to([P, KC, NB, NQ]), ALU.add)

            v.wait_ge(S["logf_in"], 16)
            link(nc.vector.transpose(logf_turned.rearrange("p (t h c) -> p t h c", t=4, h=H),
                                     logf_pages.rearrange("p (t l h) -> p t h l", t=4, h=H)))
            link(nc.vector.tensor_copy(logf_raw.rearrange("p (c t h) -> p c t h", c=16, t=4),
                                       logf_turned.rearrange("p (t h c) -> p c t h", t=4, h=H)[:, 0:16]))

            v.wait_ge(S["ssq_done"], 1)
            inv_rms(rstd[:], ps[5][:, 0:NT], D)
            v.wait_ge(S["x_ev_a"], 4)
            link(normed(hT, xT))
            def mod_add(r):
                v.wait_ge(S["mod_tp"], r + 1)
                tt(modT[:, 4 * r:4 * r + 4, :],
                   ps[4][:, 0:4 * NSEQ].rearrange("p (k s) -> p k s", k=4),
                   parT[:, 4 * r:4 * r + 4].unsqueeze(2).broadcast_to([P, 4, NSEQ]), ALU.add).then_inc(S["mod_ev"], 1)

            def mod_gain(m, at):
                a = modT[:, m * KC:(m + 1) * KC, :]
                link(stt(a, a, 1.0, parT[:, at:at + KC].unsqueeze(2).broadcast_to([P, KC, NSEQ]), ALU.add, ALU.mult))

            for r in range(4):
                mod_add(r)
            v.wait_ge(S["mod_ev"], 4)
            mod_gain(MOD_SCALE1, 48)
            modulate_sample(hT, MOD_SCALE1, MOD_SHIFT1)
            for k in range(KC):
                a, b = [modT[:, m * KC + k, 0:1] for m in (MOD_SCALE1, MOD_SHIFT1)]
                ts(hT[:, k, 0:NP], hT[:, k, 0:NP], a, b, ALU.mult, ALU.add).then_inc(S["h_done"], 1)
            az, ez = work[0:H, 15500:15500 + NT], work[0:H, 16000:16000 + NT]
            v.wait_ge(S["fg_mm"], 1)
            ts(lfT[:], ps[4][0:H, 0:NT], bfg[:, 0:1], None, ALU.add).then_inc(S["fg_v"], 1)
            v.wait_ge(S["fg_v"], 1)
            stt(az, lfT[:], -1.0, lfT[:], ALU.mult, ALU.max).then_inc(S["fg_v"], 1)

            def proj_round(r):
                v.wait_ge(S["proj_mm"], r + 1)
                dst, src, scale = proj_evac(r)
                ts(dst, src, scale, None, ALU.mult).then_inc(S["proj_v"], 1)

            proj_round(1)
            v.wait_ge(S["fg_a"], 1)
            ts(ez, ez, 1.0, None, ALU.add).then_inc(S["fg_v"], 1)
            proj_round(3)
            v.wait_ge(S["fg_a"], 2)
            link(stt(lfT[:], lfT[:], 0.0, ez, ALU.min, ALU.subtract))
            f_cum = work[0:H, 15500:15500 + NP]
            nc.vector.tensor_tensor_scan(f_cum[:, 0:P], const("ones", H), lfT[:, 0:P], 0.0, ALU.mult, ALU.add
                                         ).then_inc(S["f_ready"], 1)
            v.wait_ge(S["f_ready"], 1)
            nc.vector.tensor_tensor_scan(f_cum[:, P:NP], const("ones", H), lfT[:, P:NP], f_cum[:, P - 1:P],
                                         ALU.mult, ALU.add).then_inc(S["f_ready"], 1)
            nc.vector.memset(own, NEG).then_inc(S["own_init"], 1)
            v.wait_ge(S["t5_mm"], 1)
            v.wait_ge(S["t5_ev"], 1)
            nc.vector.tensor_copy(bias_rows[:, 0:REV], ps[5][0:H, 0:REV]).then_inc(S["t5_ev"], 1)
            nc.vector.tensor_copy(bias_rows[:, 384 + NQ:], ps[5][0:H, REV:REV + FWD]).then_inc(S["t5_ev"], 1)
            for r in range(5, 22, 2):
                proj_round(r)
            v.wait_ge(S["lf_tp"], 1)
            nc.vector.tensor_copy(lft[:, 0:2, :], ps[6][:, 0:2 * H].rearrange("p (t h) -> p t h", t=2))
            nc.vector.tensor_copy(lft[0:NS, 2, :], ps[6][0:NS, 2 * H:3 * H]).then_inc(S["lf_ev"], 1)
            v.wait_ge(S["zero_dma"], 16)
            for r in range(6):
                g, t = r // 3, r % 3
                n = TILES[t][1]
                v.wait_ge(S["ktok_tp"], r + 1)
                nc.vector.tensor_copy(k_out[0:n, g, t, :], ps[4 + r % 2][0:n, :]).then_inc(S["ktok_ev"], 1)
            lv = logf_raw.rearrange("p (c t h) -> p c t h", c=16, t=4)
            uv = logf_tb.rearrange("p (c t h) -> p c t h", c=16, t=4)
            tv = small[:, 0:128].rearrange("p (c h) -> p c h", c=16)
            nc.vector.memset(uv[:, :, 3, :], 0.0)
            link(nc.vector.tensor_copy(uv[:, :, 2, :], lv[:, :, 3, :]))
            link(tt(uv[:, :, 1, :], uv[:, :, 2, :], lv[:, :, 2, :], ALU.add))
            link(tt(uv[:, :, 0, :], uv[:, :, 1, :], lv[:, :, 1, :], ALU.add))
            link(nc.vector.memset(small[:, 128:256], 0.0))
            link(tt(tv, uv[:, :, 0, :], lv[:, :, 0, :], ALU.add))
            nc.vector.tensor_copy(small[:, 128:256].rearrange("p (b q h) -> p b q h", b=NB, q=2)[:, :, 0],
                                  tv.rearrange("p (b q) h -> p b q h", b=NB)[:, :, 1]).then_inc(S["logf_pre"], 1)
            v.wait_ge(S["w_dma"], 16)
            nc.vector.tensor_copy(far_tab.rearrange("p (q h n) -> p q h n", q=2, h=H),
                                  t5_far[:].unsqueeze(1).unsqueeze(3).broadcast_to([P, 2, H, 32])
                                  ).then_inc(S["own_init"], 1)
            v.wait_ge(S["suf_mm"], 1)
            nc.vector.tensor_copy(suffix.rearrange("p (c h t) -> p c t h", c=16, h=H),
                                  ps[5][:, :].rearrange("p (c t h) -> p c t h", c=16, t=4)
                                  ).then_inc(S["suf_done"], 1)
            v.wait_ge(S["own_mm"], 3)
            om = const("own_mask", NS).unsqueeze(1).broadcast_to([NS, H, NS])
            link(tt(own[0:NS, 0], ps[0][0:NS, 256:256 + H].unsqueeze(2).broadcast_to([NS, H, NS]), om, ALU.add))

            def own_add(g):
                for r in range(2):
                    o = own[0:NS, g, r::2, :]
                    last = tt(o, o, ps[2 * g + r][0:NS, 0:4 * NS].rearrange("p (h t) -> p h t", h=4), ALU.add)
                last.then_inc(S["own_done"], 1)

            own_add(0)
            for r in range(4, 8):
                mod_add(r)
            v.wait_ge(S["own_dma"], 16 * (NB + 4))
            own_add(1)
            v.wait_ge(S["tab_dma"], 16)
            link(tt(fox_tab0, const("causal")[:, P:].unsqueeze(1).broadcast_to([P, H, P]), fox_tab[:, :, 0:P],
                    ALU.subtract))
            link(tt(fox_tab, const("causal").unsqueeze(1).broadcast_to([P, H, NP]), fox_tab, ALU.subtract))
            for r in range(8, 12):
                mod_add(r)
            v.wait_ge(S["mod_ev"], 12)
            mod_gain(MOD_SCALE2, 56)
            v.wait_ge(S["w_dma"], 32)

            def prompt_max(n):
                tab = (fox_tab, moba_tab)[n // H][:, n % H, :]
                tab0 = fox_tab0[:, n, :] if n < H else tab[:, P:]
                v.wait_ge(S["pr_smm"], n + 1)
                if n >= 3:
                    v.wait_ge(S["pr_tp"], n - 2)
                for j, (a, b, bias) in enumerate(((0, P, tab0), (P, 3 * P, tab))):
                    nc.vector.tensor_tensor_reduce(pr_p[n % 3][:, a:b], ps[n % 2][:, a:b], bias, 1.0, NEG,
                                                   ALU.add, ALU.max, pr_m[:, n % 3, j:j + 1]
                                                   ).then_inc(S["pr_max"], 1)
                v.wait_ge(S["pr_max"], 3 * n + 2)
                ts(pr_m[:, n % 3, :], pr_m[:, n % 3, :], -1.0, None, ALU.mult).then_inc(S["pr_max"], 1)

            def prompt_norm(n):
                v.wait_ge(S["pr_exp"], 2 * n + 2)
                link(nc.vector.reciprocal(pr_l[:, n % 3, :], pr_l[:, n % 3, :]))
                ts(pr_p[n % 3][:, 0:P], pr_p[n % 3][:, 0:P], pr_l[:, n % 3, 0:1], None, ALU.mult)
                ts(pr_p[n % 3][:, P:3 * P], pr_p[n % 3][:, P:3 * P], pr_l[:, n % 3, 1:2], None, ALU.mult
                   ).then_inc(S["pr_norm"], 1)

            def prompt_out(n):
                v.wait_ge(S["pr_pv"], n + 1)
                rows = slice(64 * (n % 2), 64 * (n % 2) + 64)
                nc.vector.tensor_copy(oT[rows, n // 2, 0:NP], ps[4 + n % 2][rows, 0:NP]).then_inc(S["pr_out"], 1)

            for n in range(16 + 3):
                if n < 16:
                    prompt_max(n)
                if 1 <= n < 17:
                    prompt_norm(n - 1)
                if n >= 3:
                    prompt_out(n - 3)

            LINKS = (2, 9)
            sv = s_tile.rearrange("p (q h t i) -> p q h t i", q=2, h=H, t=4)

            def transpose_keys(u, q):
                if q == 0:
                    v.wait_ge(ring_in[u.slot], key_loads(u))
                    if u.c >= 2:
                        v.wait_ge(S["scores"], u.times(1, -1))
                nc.vector.transpose(kt[u.par][:, q, :].rearrange("p (c a l) -> p a c l", c=16, a=4),
                                    slot[u.slot][:, 2048 * q:2048 * q + 2048]
                                    .rearrange("p (a c l) -> p a c l", c=16, a=4)).then_inc(S["kt_ready"], 1)

            def unit_softmax(u, later, prev, old):
                moba = u.g == 1
                did = [0]

                def ulink(ins):
                    did[0] += 1
                    ins.then_inc(S["vlc"], 1)
                    v.wait_ge(S["vlc"], u.count(*LINKS) + did[0])

                bank = ps[1]
                v.wait_ge(S["s_turned"], u.times(1, 1))
                if u.c >= 1:
                    v.wait_ge(S["p_sub"], u.times(3))
                if moba:
                    nc.vector.tensor_reduce(gt_sum.rearrange("p (c i) -> p c i", c=16),
                                            bank[:, :].rearrange("p (c t i) -> p c i t", c=16, t=4),
                                            AX.X, ALU.add).then_inc(S["gt_ready"], 1)
                    tt(s_tile, bank[:, :], far_tab, ALU.add).then_inc(S["s_added"], 1)
                else:
                    d = suffix.rearrange("p (b c) -> p b c", b=NB)[:, bass.ds(u.b, 1), :] \
                        .rearrange("p o c -> p (o c)").unsqueeze(2).broadcast_to([P, 64, NQ])
                    tt(s_tile.rearrange("p (c i) -> p c i", c=64), bank[:, :].rearrange("p (c i) -> p c i", c=64),
                       d, ALU.add).then_inc(S["s_added"], 1)
                v.wait_ge(S["s_added"], u.times(1, 1))
                if moba:
                    v.wait_ge(S["gate_mm"], u.count(0, 1) + 1)
                    g4 = ps[2][:, 0:256].rearrange("p (n c) -> p n c", n=4)
                    e4 = eq4.rearrange("p (n c) -> p n c", n=4)
                    ulink(nc.vector.tensor_reduce(drop, ps[2][:, 0:256].rearrange("p (n c) -> p c n", n=4), AX.X,
                                                  ALU.min))
                    ulink(tt(e4, g4, drop.unsqueeze(1).broadcast_to([P, 4, 64]), ALU.is_le))
                    ulink(tt(e4, e4, const("block_no").unsqueeze(2).broadcast_to([P, 4, 64]), ALU.mult))
                    ulink(nc.vector.tensor_reduce(drop, eq4.rearrange("p (n c) -> p c n", n=4), AX.X, ALU.max))
                    ulink(tt(pen, drop.unsqueeze(1).broadcast_to([P, 2, 64]),
                             const("block_id").unsqueeze(2).broadcast_to([P, 2, 64]), ALU.is_equal))
                    left_out = pen.rearrange("p q (h i) -> p (q h) i", h=H).unsqueeze(2).broadcast_to([P, 2 * H, 4, NQ])
                    sa = s_tile.rearrange("p (c t i) -> p c t i", c=2 * H, t=4)
                    ulink(ts(pen, pen, NEG, None, ALU.mult))
                    ulink(tt(sa, sa, left_out, ALU.add))
                own_u = own[:, u.g, :, bass.ds(u.b * NQ, NQ)]
                mb = mx_b[:, 0:64].rearrange("p (h i) -> p h i", h=H)
                ulink(nc.vector.tensor_reduce(mb, s_tile.rearrange("p (q h t i) -> p h i q t", q=2, h=H, t=4),
                                              AX.XY, ALU.max))
                tt(mb, mb, own_u, ALU.max).then_inc(S["max_part"], 1)
                v.wait_ge(S["max_t"], u.times(1, 1))
                ulink(nc.vector.reduce_max(mx_col[:], ps[3][0:64, 0:P], AX.X))
                assert did[0] == LINKS[u.g]
                ts(mx_diag[:], const("ident", 64)[:, 0:64], mx_col[:, 0:1], None, ALU.mult).then_inc(S["diag"], 1)
                if prev is not None:
                    unit_part_sums(prev)
                if old is not None:
                    unit_output(old)
                v.wait_ge(S["max_bc"], u.times(1, 1))
                m = ps[4][:, 0:64].rearrange("p (h i) -> p h i", h=H)
                pt = p_tile[:, u.par, :]
                for q in range(2):
                    tt(pt[:, 256 * q:256 * q + 256].rearrange("p (t h i) -> p h t i", h=H, t=4), sv[:, q],
                       m.unsqueeze(2).broadcast_to([P, H, 4, NQ]), ALU.subtract).then_inc(S["p_sub"], 1)
                tt(pt[:, 512:576].rearrange("p (h i) -> p h i", h=H), own_u, m, ALU.subtract).then_inc(S["p_sub"], 1)
                if later is not None:
                    for q in range(2):
                        transpose_keys(later, q)

            def unit_part_sums(u):
                v.wait_ge(S["p_exp"], u.times(1, 1))
                nc.vector.tensor_reduce(l_part[:, u.par, :],
                                        p_tile[:, u.par, :].rearrange("p (s n) -> p n s", s=9), AX.X, ALU.add
                                        ).then_inc(S["p_add"], 1)

            def unit_output(u):
                v.wait_ge(S["lsum"], u.times(1, 1))
                nc.vector.reciprocal(rsum, ps[5][:, 0:64]).then_inc(S["vlp"], 1)
                v.wait_ge(S["vlp"], u.times(1, 1))
                v.wait_ge(S["o_turned"], u.times(1, 1))
                o = ps[7][:, 0:P].rearrange("p (c r i) -> p c r i", c=4, r=4)
                for r in range(2):
                    rows = slice(64 * r, 64 * r + 64)
                    tt(oT[rows, 4 * u.g:4 * u.g + 4, bass.ds(u.b * NQ + NP, NQ)], o[rows, :, r, :],
                       rsum[rows, :].rearrange("p (c r i) -> p c r i", c=4, r=2)[:, :, r, :], ALU.mult
                       ).then_inc(S["o_done"], 1)

            nc.vector.memset(ps[6][:, 0:P], 0.0).then_inc(S["o_init"], 1)
            v.wait_ge(S["pr_pv"], 16)
            v.wait_ge(S["qcur"], 1)
            for c in range(2):
                for q in range(2):
                    transpose_keys(Unit(c), q)
            for c in range(2):
                unit_softmax(Unit(c), Unit(c + 2), Unit(c - 1) if c else None, None)
            with v.Fori(0, 2) as turn:
                for j in range(6):
                    u = Unit(2 + j, turn)
                    unit_softmax(u, u.step(2), u.step(-1), u.step(-2))
            for c in range(14, NU):
                unit_softmax(Unit(c), None, Unit(c - 1), Unit(c - 2))
            unit_part_sums(Unit(15))
            for c in range(14, NU):
                unit_output(Unit(c))

            def group_variance(g):
                v.wait_ge(S["ossq"], g + 1)
                ts(mr[g], ps[g][:, 0:NT], 1.0 / W, EPS, ALU.mult, ALU.add).then_inc(S["var_done"], 1)

            group_variance(0)
            for g in range(2):
                rms[0] += 1
                v.wait_ge(S["sqrt_done"], rms[0])
                link(nc.vector.reciprocal(mr[g], mr[g]))
                if g == 0:
                    group_variance(1)
                for k in range(g * PC, (g + 1) * PC):
                    stt(oT[:, k, :], oT[:, k, :], parT[:, 64 + k:65 + k], mr[g], ALU.mult, ALU.mult
                        ).then_inc(S["on_done"], 1)
            gate = modT[:, MOD_GATE1 * KC:(MOD_GATE1 + 1) * KC, :]
            so = region(17408, NS)
            for k in range(KC):
                v.wait_ge(S["wo_mm"], k + 1)
                bank = ps[2 + k % 4]
                link(tt(so.rearrange("p (b i) -> p b i", b=NB), bank[:, NP:NT].rearrange("p (b i) -> p b i", b=NB),
                        gate[:, k, 1:].unsqueeze(2).broadcast_to([P, NB, NQ]), ALU.mult))
                link(tt(xT[:, k, NP:], xT[:, k, NP:], so, ALU.add))
                stt(xT[:, k, 0:NP], bank[:, 0:NP], gate[:, k, 0:1], xT[:, k, 0:NP], ALU.mult, ALU.add
                    ).then_inc(S["wo_done"], 1)
            v.wait_ge(S["ssq2"], 1)
            inv_rms(rstd[:], ps[0][:, 0:NT], D)
            for k in range(KC):
                tt(hT[:, k, :], xT[:, k, :], rstd[:], ALU.mult).then_inc(S["h2_normed"], 1)
            v.wait_ge(S["h2_normed"], KC)
            modulate_sample(hT, MOD_SCALE2, MOD_SHIFT2).then_inc(S["h2_normed"], 1)
            v.wait_ge(S["r_mm"], 1)
            nc.vector.memset(rt[:, 0:72], NEG)
            link(nc.vector.memset(lg, 0.0))
            br = brow[:].unsqueeze(1)
            link(tt(lg[:, 0:2, :], ps[1][:, 0:72].rearrange("p (t n) -> p t n", t=2), br.broadcast_to([P, 2, 36]),
                    ALU.add))
            link(tt(lg[0:NS, 2, :], ps[1][0:NS, 72:108], brow[0:NS, :], ALU.add))
            link(nc.vector.tensor_copy(g8[:, :, 0:NG], lg[:, :, 0:NG]))
            for t in range(3):
                link(nc.vector.max(gm8[:, t, :], g8[:, t, :]))
                link(nc.vector.max_index(gi8[:, t, :], gm8[:, t, :], g8[:, t, :]))
            link(nc.vector.tensor_copy(gidf, gi8[:]))
            tt(gex, lg[:, :, 0:NG], gm8[:, :, 0:1].broadcast_to([P, 3, NG]), ALU.subtract).then_inc(S["lg_ready"], 1)
            link(tt(goh, const("iota32")[:, 0:NG].unsqueeze(1).broadcast_to([P, 3, NG]),
                    gidf[:, :, 0:1].broadcast_to([P, 3, NG]), ALU.is_equal))
            for t in range(3):
                link(tt(sel_e[:, t, :].rearrange("p (g e) -> p g e", g=NG),
                        lg[:, t, NG:].rearrange("p (g e) -> p g e", g=NG),
                        goh[:, t, :].unsqueeze(2).broadcast_to([P, NG, EPG]), ALU.mult))
            link(nc.vector.tensor_reduce(e8, sel_e.rearrange("p t (g e) -> p t e g", g=NG), AX.X, ALU.add))
            for t in range(3):
                link(nc.vector.max(em8[:, t, :], e8[:, t, :]))
                link(nc.vector.max_index(ei8[:, t, :], em8[:, t, :], e8[:, t, :]))
            link(nc.vector.tensor_copy(eidf, ei8[:]))
            tt(tex.unsqueeze(2), em8[:, :, 1:2], em8[:, :, 0:1], ALU.subtract).then_inc(S["lg_ready"], 1)
            for a in range(2):
                link(stt(ids[:, a, :].unsqueeze(2), gidf[:, :, 0:1], float(EPG), eidf[:, :, a:a + 1],
                         ALU.mult, ALU.add))
                link(tt(A[:, a], const("iota32").unsqueeze(1).broadcast_to([P, 3, NE]),
                        ids[:, a, :].unsqueeze(2).broadcast_to([P, 3, NE]), ALU.is_equal))
            link(nc.vector.memset(A[NS:, :, 2, :], 0.0))
            tt(Asum, A[:, 0], A[:, 1], ALU.add).then_inc(S["sel_rdy"], 1)
            link(nc.vector.memset(ones32, 1.0))
            nc.vector.memset(eps_col, EPS)
            v.wait_ge(S["rank_mm"], 1)
            link(nc.vector.tensor_copy(rank, ps[2][:, 0:96].rearrange("p (t n) -> p t n", t=3)))
            link(nc.vector.tensor_copy(cnt, ps[2][:, 96:128]))
            link(nc.vector.tensor_tensor_scan(start, ones32, cnt, 0.0, ALU.mult, ALU.add))
            link(tt(start, start, cnt, ALU.subtract))
            link(tt(place_m, rank, start.unsqueeze(1).broadcast_to([P, 3, NE]), ALU.add))
            for a in range(2):
                link(tt(tmp3, A[:, a], place_m, ALU.mult))
                link(nc.vector.tensor_reduce(slots[:, a, :], tmp3, AX.X, ALU.add))
            v.wait_ge(S["iota_done"], 1)
            for t, (_, n) in enumerate(TILES):
                ts(place1[0:n, t, :], iota_s[0:n, :], slots[0:n, 0, t:t + 1], None, ALU.is_equal
                   ).then_inc(S["onehot"], 1)
                v.wait_ge(S["onehot"], 2 * t + 1)
                stt(place1[0:n, t, :], iota_s[0:n, :], slots[0:n, 1, t:t + 1], place1[0:n, t, :], ALU.is_equal,
                    ALU.add).then_inc(S["onehot"], 1)
            link(ts(extra, cnt, float(BLK), None, ALU.is_gt))
            for m in range(2, NT // BLK):
                link(stt(extra, cnt, float(BLK * m), extra, ALU.is_gt, ALU.add))
            link(nc.vector.tensor_tensor_scan(ovb, ones32, extra, 0.0, ALU.mult, ALU.add))
            link(nc.vector.tensor_copy(ov_hi, ovb[0:1, :]))
            link(tt(ovb, ovb, extra, ALU.subtract))
            link(ts(base64, const("iota32"), float(BLK), None, ALU.mult))
            link(ts(ov_off, ovb, float(BLK), float(BLK * (NE - 1)), ALU.mult, ALU.add))
            link(tt(ov_off, ov_off, base64, ALU.subtract))
            link(ts(tmp3, rank, float(BLK), None, ALU.is_ge))
            link(tt(tmp3, tmp3, ov_off.unsqueeze(1).broadcast_to([P, 3, NE]), ALU.mult))
            link(tt(place_m, tmp3, rank, ALU.add))
            link(tt(place_m, place_m, base64.unsqueeze(1).broadcast_to([P, 3, NE]), ALU.add))
            for a in range(2):
                link(tt(tmp3, A[:, a], place_m, ALU.mult))
                link(nc.vector.tensor_reduce(poss[:, a, :], tmp3, AX.X, ALU.add))
            link(nc.vector.tensor_copy(posu[:].rearrange("p (a t) -> p a t", a=2), poss))
            link(nc.vector.tensor_copy(start_i[:], start[0:1, :]))
            jb = const("iota_ov", 1).unsqueeze(2).broadcast_to([1, MAXOV, NE])
            link(tt(ov_a, ovb[0:1, :].unsqueeze(1).broadcast_to([1, MAXOV, NE]), jb, ALU.is_le))
            link(tt(ov_b, ov_hi.unsqueeze(1).broadcast_to([1, MAXOV, NE]), jb, ALU.is_gt))
            link(tt(ov_a, ov_a, ov_b, ALU.mult))
            link(tt(ov_b, ov_a, const("iota32", 1).unsqueeze(1).broadcast_to([1, MAXOV, NE]), ALU.mult))
            link(nc.vector.tensor_reduce(ov_tab[:, 1, :], ov_b, AX.X, ALU.add))
            link(tt(ov_b, jb, ovb[0:1, :].unsqueeze(1).broadcast_to([1, MAXOV, NE]), ALU.subtract))
            link(ts(ov_b, ov_b, float(BLK), float(BLK), ALU.mult, ALU.add))
            link(tt(ov_b, ov_b, start[0:1, :].unsqueeze(1).broadcast_to([1, MAXOV, NE]), ALU.add))
            link(tt(ov_b, ov_b, ov_a, ALU.mult))
            link(nc.vector.tensor_reduce(ov_tab[:, 0, :], ov_b, AX.X, ALU.add))
            link(nc.vector.tensor_copy(ov_i[:], ov_tab.rearrange("p a n -> p (a n)")))
            nc.vector.tensor_copy(nov_i[:], ov_hi[:, NE - 1:NE]).then_inc(S["tabs"], 1)
            v.wait_ge(S["r_a"], 2)
            link(nc.vector.reduce_sum(gsum, gex, AX.X))
            link(ts(wt[:, 1, :], tex, 1.0, None, ALU.add))
            link(tt(wt[:, 1, :], wt[:, 1, :], gsum, ALU.mult))
            link(nc.vector.reciprocal(wt[:, 0, :], wt[:, 1, :]))
            link(tt(wt[:, 1, :], wt[:, 0, :], tex, ALU.mult))
            nc.vector.memset(hid[BLK:, :, :], 0.0)
            nc.vector.memset(h_sort[:, :, ASSIGN:], 0.0).then_inc(S["pad_done"], 1)

            def hidden(e, par, exp_sig, hid_sig):
                v.wait_ge(exp_sig, e + 1)
                a, b, s = ps[par][0:BLK, 0:DE], ps[par][0:BLK, DE:2 * DE], e_sig[:, par, :]
                steps = [lambda: ts(s, s, 1.0, None, ALU.add), lambda: nc.vector.reciprocal(s, s),
                         lambda: tt(s, s, a, ALU.mult), lambda: tt(hid[0:BLK, par, :], s, b, ALU.mult)]
                for i, st in enumerate(steps):
                    if i:
                        v.wait_ge(hid_sig, e * 4 + i)
                    st().then_inc(hid_sig, 1)

            def block_y(e, par, before, k, used):
                v.wait_ge(exp_free[k], used)
                if before is not None:
                    v.wait_ge(S[f"y_dma{par}"], before * 16)
                nc.vector.tensor_copy(y_st[0:BLK, par, 512:], ps[3 + 2 * par][0:BLK, :]).then_inc(S["y_ev_v"], 1)

            for e in range(4):
                hidden(e, e % 2, S["h_exp"], S["hid"])
                if e >= 1:
                    block_y(e - 1, (e - 1) % 2, 1 if e == 3 else None, e - 1, 1)
            with v.Fori(0, NE // ES - 1) as turn:
                for k in range(ES):
                    e = turn * ES + ES + k
                    hidden(e, k % 2, S["h_exp"], S["hid"])
                    block_y(e - 1, (k - 1) % 2, turn * 2 + (k + 3) // 2, (k - 1) % ES, turn + (1 if k == 0 else 2))
            block_y(NE - 1, 1, NE // 2 - 1, ES - 1, NE // ES)
            nov = v.value_load(nov_i[0:1, 0:1], min_val=0, max_val=MAXOV)
            with v.If(nov > 0):
                with v.Fori(0, nov) as i:
                    v.wait_ge(S["ov_h"], i + 1)
                    hidden(i, 0, S["ov_exp"], S["ov_hid"])
                    v.wait_ge(exp_free[0], i + NE // ES + 1)
                    v.wait_ge(S["y_dma0"], i * 16 + 16 * (NE // 2))
                    nc.vector.tensor_copy(y_st[0:BLK, 0, 512:], ps[3][0:BLK, :]).then_inc(S["y_ev_v"], 1)
            v.wait_ge(S["gt_ev"], 6)
            v.wait_ge(S["gf_in"], 16)

            def final_sum(t):
                n = TILES[t][1]
                a, b, x = y_a[0:n, t, :], y_b3[t][0:n, :], x_tok2[0:n, t, :]
                v.wait_ge(S["fin_scaled"], t + 1)
                link(stt(a, b, wt[0:n, 1, t:t + 1], a, ALU.mult, ALU.add))
                link(tt(a, a, g_tok[0:n, t, :], ALU.mult))
                tt(x, x, a, ALU.add).then_inc(S["fin_x"], 1)

            def final_norm(t):
                n = TILES[t][1]
                x = x_tok2[0:n, t, :]
                v.wait_ge(S["fin_sqrt"], t + 1)
                nc.vector.reciprocal(ss_f[0:n, t:t + 1], ss_f[0:n, t:t + 1]).then_inc(S["fin_v"], 1)
                v.wait_ge(S["fin_v"], 2 * t + 1)
                stt(x, x, ss_f[0:n, t:t + 1], gfin[0:n, :], ALU.mult, ALU.mult).then_inc(S["fin_v"], 1)

            for t in range(3):
                final_sum(t)
                if t:
                    final_norm(t - 1)
            final_norm(2)

        @block.tensor
        def _(pe):
            mm, tp = nc.tensor.matmul, nc.tensor.transpose

            pe.wait_ge(cst_in, 16)
            pe.wait_ge(c_in, 32)
            for k in range(KC):
                last = tp(ps[4][:, k * NSEQ:(k + 1) * NSEQ], c_row[:, k * P:(k + 1) * P],
                          const("ident", NSEQ)[:, 0:NSEQ])
            last.then_inc(S["head_tp"], 1)
            pe.wait_ge(x_in, 32)
            for k in range(KC):
                if k >= 4:
                    pe.wait_ge(S["x_ev_a" if k % 2 == 0 else "x_ev_v"], (k - 4) // 2 + 1)
                for t, (t0, n) in enumerate(TILES):
                    last = tp(ps[k % 4][:, t0:t0 + n], x_tok[0:n, t, k * P:(k + 1) * P], const("ident", n)[:, 0:n])
                last.then_inc(S["x_tp"], 1)

            def sum_squares(bank, src, chunks, sig, base, done, freed=None):
                for j, k in enumerate(chunks):
                    pe.wait_ge(sig, base + k + 1)
                    last = mm(ps[bank][:, 0:NT], ones, src[:, k, :], start=(j == 0), stop=(j == len(chunks) - 1))
                    if j == 0 and freed is not None:
                        last.then_inc(freed, 1)
                last.then_inc(done, 1)

            def ada_mm(r):
                m, hf = r // 2, r % 2
                n = ADA_AT[m]
                if r == 0:
                    pe.wait_ge(S["ada_half"], 16)
                else:
                    pe.wait_ge(ring_in[n % RS], 16 * (1 if r < 4 else WLOADS[n % RS] - (n == 5)))
                if r >= 2:
                    pe.wait_ge(S["ada_row"], r - 1)
                wv = slot[n % RS].rearrange("p (k e) -> p k e", k=KC)
                for k in range(KC):
                    last = mm(ps[6 + r % 2][0:NSEQ, :], silu_cT[:, k, :], wv[:, k, 512 * hf:512 * hf + 512],
                              start=(k == 0), stop=(k == KC - 1))
                last.then_inc(ada_full(r)[0], 1)

            def ada_tp(r):
                pe.wait_ge(S["ada_row"], r + 1)
                if r >= 1:
                    pe.wait_ge(S["mod_ev"], r)
                for c in range(4):
                    last = tp(ps[4][:, c * NSEQ:(c + 1) * NSEQ],
                              ada_row[r // 4 > 0][:, r % 2, c * P:(c + 1) * P], const("ident", NSEQ)[:, 0:NSEQ])
                last.then_inc(S["mod_tp"], 1)

            pe.wait_ge(S["head_ev"], 1)
            ada_mm(0)
            pe.wait_ge(par_in, 16 * 5)
            tp(ps[5][:, 0:72], par_row, const("ident", 72)[:, 0:72]).then_inc(S["head_tp"], 1)
            pe.wait_ge(S["head_ev"], 2)
            sum_squares(5, sq1, range(KC), S["sq_done"], 0, S["ssq_done"])
            for r in range(1, 4):
                ada_mm(r)
                ada_tp(r - 1)
            ada_tp(3)
            pe.wait_ge(S["mod_ev"], 4)
            pe.wait_ge(small_in, 16 * 10)
            mm(ps[5][0:H, 0:REV + FWD], t5[:], dist_oh, start=True, stop=True).then_inc(S["t5_mm"], 1)
            for k in range(KC):
                pe.wait_ge(S["h_done"], k + 1)
                last = mm(ps[4][0:H, 0:NT], wfg[:, k, :], hT[:, k, :], start=(k == 0), stop=(k == KC - 1))
            last.then_inc(S["fg_mm"], 1)
            for r, (transposed, item, col, d) in enumerate(PROJ):
                if r in (0, 8, 15):
                    pe.wait_ge(ring_in[item % RS], 16 * {2: 1, 3: 3, 4: 2}[item])
                if r >= 4:
                    pe.wait_ge(S["proj_a" if r % 2 == 0 else "proj_v"], (r - 4) // 2 + 1)
                wv = slot[item % RS].rearrange("p (k e) -> p k e", k=KC)
                for k in range(KC):
                    if transposed:
                        last = mm(ps[r % 4][:, 0:NT], wv[:, k, col:col + P], hT[:, k, :],
                                  start=(k == 0), stop=(k == KC - 1))
                    else:
                        t0, n = TILES[d[1]]
                        last = mm(ps[r % 4][0:n, :], hT[:, k, t0:t0 + n], wv[:, k, col:col + W],
                                  start=(k == 0), stop=(k == KC - 1))
                    if r in (8, 15) and k == 0:
                        last.then_inc(ring_free[(item - 1) % RS], 1)
                last.then_inc(S["proj_mm"], 1)
            pe.wait_ge(S["f_ready"], 2)
            for t, (t0, n) in enumerate(TILES):
                last = tp(ps[6][0:n, t * H:(t + 1) * H], lfT[:, t0:t0 + n], const("ident", H)[:, 0:H])
                if t == 0:
                    last.then_inc(ring_free[4 % RS], 1)
            last.then_inc(S["lf_tp"], 1)
            pe.wait_ge(S["proj_a"], 11)
            pe.wait_ge(S["proj_v"], 11)
            for r in range(6):
                g, t = r // 3, r % 3
                t0, n = TILES[t]
                if r == 1:
                    pe.wait_ge(S["t5_ev"], 3)
                if r >= 2:
                    pe.wait_ge(S["ktok_ev"], r - 1)
                for c in range(PC):
                    last = tp(ps[4 + r % 2][0:n, c * P:(c + 1) * P], qkT[:, 8 * g + 4 + c, t0:t0 + n], ident)
                last.then_inc(S["ktok_tp"], 1)
            pe.wait_ge(S["lf_ev"], 1)
            mm(ps[0][0:NS, 256:256 + H], const("neg_prefix", NS), lft[0:NS, 2, :], start=True, stop=True
               ).then_inc(S["own_mm"], 1)
            for g in range(2):
                for h in range(H):
                    rows = slice(64 * (h % 2), 64 * (h % 2) + 64)
                    last = mm(ps[2 * g + h % 2][0:NS, h // 2 * NS:(h // 2 + 1) * NS],
                              qkT[rows, 8 * g + 4 + h // 2, NP:],
                              qkT[rows, 8 * g + h // 2, NP:], start=True, stop=True)
                last.then_inc(S["own_mm"], 1)
            pe.wait_ge(S["ktok_ev"], 6)
            pe.wait_ge(S["logf_pre"], 1)
            tsum = small[:, 0:128].rearrange("p (c h) -> p c h", c=16)
            later = small[:, 128:256].rearrange("p (c h) -> p c h", c=16)
            bank = ps[5][:, :].rearrange("p (c t h) -> p c t h", c=16, t=4)
            mm(ps[5][:, :], const("suf_lo"), logf_raw, start=True, stop=False)
            mm(ps[5][:, :], const("suf_same"), logf_tb, start=False, stop=False)
            mm(bank, const("suf_page"), tsum.unsqueeze(2).broadcast_to([P, 16, 4, H]), start=False, stop=False)
            mm(bank, ones, later.unsqueeze(2).broadcast_to([P, 16, 4, H]), start=False, stop=True
               ).then_inc(S["suf_mm"], 1)
            for r in range(4, 12):
                ada_mm(r)
                if r > 4:
                    ada_tp(r - 1)
            ada_tp(11)

            def head_rows(n):
                return slice(64 * (n % 2), 64 * (n % 2) + 64), 8 * (n // H) + n % H // 2

            def prompt_scores(n):
                rows, c = head_rows(n)
                if n >= 2:
                    pe.wait_ge(S["pr_max"], 3 * (n - 2) + 2)
                else:
                    pe.wait_ge(S["own_done"], 2)
                q, k = qkT[rows, c, :], qkT[rows, c + 4, :]
                mm(ps[n % 2][:, 0:P], q[:, 0:P], k[:, 0:P], start=True, stop=True)
                mm(ps[n % 2][:, P:3 * P], q[:, P:NP], k[:, 0:NP], start=True, stop=True).then_inc(S["pr_smm"], 1)

            def prompt_transpose(n):
                pe.wait_ge(S["pr_norm"], n + 1)
                if n >= 2:
                    pe.wait_ge(S["pr_pt"], n - 1)
                for j in range(3):
                    last = tp(ps[2 + n % 2][:, j * P:(j + 1) * P], pr_p[n % 3][:, j * P:(j + 1) * P], ident)
                last.then_inc(S["pr_tp"], 1)

            def prompt_pv(n):
                rows, _ = head_rows(n)
                pe.wait_ge(S["pr_pt"], n + 1)
                if n >= 2:
                    pe.wait_ge(S["pr_out"], n - 1)
                elif n == 0:
                    pe.wait_ge(S["mod_ev"], 12)
                else:
                    pe.wait_ge(S["suf_done"], 1)
                cols = slice(n % H * HD, (n % H + 1) * HD)
                o = ps[4 + n % 2]
                mm(o[rows, 0:P], v_tok[:, n // H, 0, cols], pr_pt[:, n % 2, 0:P], start=True, stop=True)
                mm(o[rows, P:NP], v_tok[:, n // H, 0, cols], pr_pt[:, n % 2, P:NP], start=True, stop=False)
                mm(o[rows, P:NP], v_tok[:, n // H, 1, cols], pr_pt[:, n % 2, NP:3 * P], start=False, stop=True
                   ).then_inc(S["pr_pv"], 1)

            for n in range(16 + 3):
                if n < 16:
                    prompt_scores(n)
                if 2 <= n < 18:
                    prompt_transpose(n - 2)
                if n >= 3:
                    prompt_pv(n - 3)

            def unit_scores(u, quarter):
                if quarter == 0:
                    pe.wait_ge(S["qcur"], u.times(1, 1))
                    pe.wait_ge(S["kt_ready"], u.times(2, 2))
                ktv = kt[u.par].rearrange("p q (c n) -> p q c n", c=16)
                for h in (2 * quarter, 2 * quarter + 1):
                    rows = slice(32 * (h % 4), 32 * (h % 4) + 32)
                    o = ps[0][rows, h // 4 * 256:h // 4 * 256 + 256].rearrange("p (q n) -> p q n", q=2)
                    for e in range(2):
                        last = mm(o, q_cur[:, u.g, 2 * h + e, :], ktv[:, :, 2 * h + e, :], start=(e == 0),
                                  stop=(e == 1))
                if quarter == 3:
                    last.then_inc(S["scores"], 1)

            def turn_scores(u):
                pe.wait_ge(S["s_copied"], u.times(1, 1))
                if u.c >= 1:
                    pe.wait_ge(S["s_added"], u.times(1))
                for half in range(2):
                    for q in range(2):
                        at = (q * 2 + half) * P
                        last = tp(ps[1][:, at:at + P], s_nat[:, (half * 2 + q) * P:(half * 2 + q + 1) * P], ident)
                last.then_inc(S["s_turned"], 1)

            def unit_gate(u):
                pe.wait_ge(S["gt_ready"], u.count(0, 1) + 1)
                mm(ps[2][:, 0:P], const("half0"), gt_sum, start=True, stop=True)
                mm(ps[2][:, P:2 * P], const("half1"), gt_sum, start=True, stop=True).then_inc(S["gate_mm"], 1)

            def unit_max(u):
                pe.wait_ge(S["max_part"], u.times(1, 1))
                tp(ps[3][:, 0:P], mx_b[:], ident).then_inc(S["max_t"], 1)

            def unit_bcast(u):
                pe.wait_ge(S["diag"], u.times(1, 1))
                mm(ps[4][:, 0:64], const("ones", 64), mx_diag[:], start=True, stop=True).then_inc(S["max_bc"], 1)

            def unit_sum(u):
                pe.wait_ge(S["p_add"], u.times(1, 1))
                if u.c >= 1:
                    pe.wait_ge(S["o_done"], u.times(2))
                mm(ps[5][:, 0:64], ones, l_part[:, u.par, :], start=True, stop=True).then_inc(S["lsum"], 1)

            def unit_pv(u, c):
                if c == 0:
                    pe.wait_ge(S["p_exp"], u.times(1, 1))
                    pe.wait_ge(pages_v_in[u.slot], u.in_slot(1) * (16 * PAGES))
                    if u.c >= 1:
                        pe.wait_ge(S["o_copied"], u.times(1))
                vv = slot[u.slot][:, 4096:].rearrange("p (g n) -> p g n", g=8)
                o = ps[6][32 * c:32 * c + 16, 0:P]
                for j in range(8):
                    last = mm(o, p_tile[:, u.par, 64 * j + 16 * c:64 * j + 16 * c + 16], vv[:, j, c * P:(c + 1) * P],
                              start=(j == 0), stop=False)
                if c == PC - 1:
                    last.then_inc(ring_free[u.slot], 1)
                last = mm(o, p_tile[0:NS, u.par, 512 + 16 * c:528 + 16 * c], v_tok[0:NS, u.g, 2, c * P:(c + 1) * P],
                          start=False, stop=True)
                if c == PC - 1:
                    last.then_inc(S["pv"], 1)

            def turn_output(u):
                pe.wait_ge(S["o_copied"], u.times(1, 1))
                tp(ps[7][:, 0:P], o_nat, ident).then_inc(S["o_turned"], 1)

            def unit_step(u, nxt, prev, old):
                def scores(*quarters):
                    if nxt is not None:
                        for quarter in quarters:
                            unit_scores(nxt, quarter)

                def values(*pairs):
                    if prev is not None:
                        for c in pairs:
                            unit_pv(prev, c)

                turn_scores(u)
                scores(0)
                if old is not None:
                    turn_output(old)
                if u.g == 1:
                    unit_gate(u)
                    scores(1, 2, 3)
                    values(0)
                    unit_max(u)
                    values(1)
                    unit_bcast(u)
                    values(2, 3)
                else:
                    scores(1)
                    unit_max(u)
                    scores(2)
                    unit_bcast(u)
                    scores(3)
                    values(0, 1, 2, 3)
                if prev is not None:
                    unit_sum(prev)

            pe.wait_ge(S["pr_out"], 16)
            pe.wait_ge(S["o_init"], 1)
            for quarter in range(4):
                unit_scores(Unit(0), quarter)
            for c in range(2):
                unit_step(Unit(c), Unit(c + 1), Unit(c - 1) if c else None, None)
            with pe.Fori(0, 2) as turn:
                for j in range(6):
                    u = Unit(2 + j, turn)
                    unit_step(u, u.step(1), u.step(-1), u.step(-2))
            for c in range(14, NU):
                unit_step(Unit(c), Unit(c + 1) if c + 1 < NU else None, Unit(c - 1), Unit(c - 2))
            turn_output(Unit(14))
            for c in range(PC):
                unit_pv(Unit(15), c)
            unit_sum(Unit(15))
            turn_output(Unit(15))

            for g in range(2):
                sum_squares(g, sq, range(g * PC, (g + 1) * PC), S["osq"], 0, S["ossq"])
            pe.wait_ge(ring_in[1], 16 * (WLOADS[1] + PAGES * 5 + 1))
            wv = slot[1].rearrange("p (k e) -> p k e", k=KC)

            def project(m, g):
                for k in range(g * PC, (g + 1) * PC):
                    last = mm(ps[2 + m % 4][:, 0:NT], wv[:, k, m * P:(m + 1) * P], oT[:, k, :],
                              start=(k == 0), stop=(k == KC - 1))
                if g == 1:
                    last.then_inc(S["wo_mm"], 1)

            pe.wait_ge(S["on_done"], PC)
            for m in range(4):
                project(m, 0)
            pe.wait_ge(S["on_done"], KC)
            for m in range(4):
                project(m, 1)
            for m in range(4, KC):
                pe.wait_ge(S["wo_done"], m - 3)
                for g in range(2):
                    project(m, g)
            sum_squares(0, sq, range(KC), S["sq2"], 0, S["ssq2"], ring_free[1])
            def tok_turn(r):
                src = (xT, hT)[r // 6]
                t, hf = r % 6 // 2, r % 2
                t0, n = TILES[t]
                if r >= 4:
                    pe.wait_ge(S["htok_ev"], r - 3)
                for c in range(4):
                    last = tp(ps[4 + r % 4][0:n, c * P:(c + 1) * P], src[:, 4 * hf + c, t0:t0 + n], ident)
                last.then_inc(S["htok_tp"], 1)

            pe.wait_ge(S["wo_done"], KC)
            for r in range(4):
                tok_turn(r)
            pe.wait_ge(S["h2_prompt"], KC)
            pe.wait_ge(S["h2_normed"], KC + 1)
            for t, (t0, n) in enumerate(TILES):
                for k in range(KC):
                    last = mm(ps[1][0:n, 36 * t:36 * t + 36], hT[:, k, t0:t0 + n], wr[:, k, :],
                              start=(k == 0), stop=(k == KC - 1))
            last.then_inc(S["r_mm"], 1)
            for r in range(4, 12):
                tok_turn(r)
            pe.wait_ge(S["sel_rdy"], 1)
            for t in range(3):
                for j in range(t):
                    mm(ps[2][:, 32 * t:32 * t + 32], ones, Asum[:, j, :], start=(j == 0), stop=False)
                mm(ps[2][:, 32 * t:32 * t + 32], const("before"), Asum[:, t, :], start=(t == 0), stop=True)
            for t in range(3):
                last = mm(ps[2][:, 96:128], ones, Asum[:, t, :], start=(t == 0), stop=(t == 2))
            last.then_inc(S["rank_mm"], 1)
            gate2 = modT[:, MOD_GATE2 * KC:(MOD_GATE2 + 1) * KC, :]
            pe.wait_ge(S["htok_ev"], 12)
            for k in range(KC):
                last = tp(ps[6 + k // 4][0:NSEQ, k % 4 * P:(k % 4 + 1) * P], gate2[:, k, :], ident)
            last.then_inc(S["g2_tp"], 1)
            pe.wait_ge(S["g2_ev"], 2)
            pe.wait_ge(S["seq_in"], 16)

            def gate_rows(r):
                t, hf = r // 2, r % 2
                t0, n = TILES[t]
                if r >= 2:
                    pe.wait_ge(S["gt_ev"], r - 1)
                mm(ps[4 + r % 2][0:n, :], seq_oh[:, t0:t0 + n], g2_row[:, 512 * hf:512 * hf + 512],
                   start=True, stop=True).then_inc(S["gt_mm"], 1)
            for r in range(3):
                gate_rows(r)
            for k in range(KC):
                if k >= 2:
                    pe.wait_ge(S["sorted"], k - 1)
                for lo, hi, bank in ((0, 512, 2 * (k % 2)), (512, ASSIGN, 2 * (k % 2) + 1)):
                    for t, (_, n) in enumerate(TILES):
                        if k == 0 and lo == 0:
                            pe.wait_ge(S["onehot"], 2 * t + 2)
                        last = mm(ps[bank][:, 0:hi - lo], h_tok[0:n, t, k * P:(k + 1) * P], place1[0:n, t, lo:hi],
                                  start=(t == 0), stop=(t == 2))
                last.then_inc(S["sort_mm"], 1)
            for r in range(3, 6):
                gate_rows(r)
            pe.wait_ge(S["gt_ev"], 6)

            def block_hidden(k, par, done):
                for c in range(KC):
                    last = mm(ps[par][0:BLK, :], h_cur[:, par, c, :], w13_of[k][:, c, :],
                              start=(c == 0), stop=(c == KC - 1))
                last.then_inc(done, 1)

            def block_turn(par):
                for f in range(FC):
                    last = tp(ps[6][:, f * P:(f + 1) * P], hid[:, par, f * P:(f + 1) * P], ident)
                last.then_inc(S["hid_tp"], 1)

            def block_out(k, par, done, freed):
                for hf in range(2):
                    for f in range(FC):
                        last = mm(ps[2 + 2 * par + hf][0:BLK, :], hid_t[:, par, f, :],
                                  w2_of[k][:, f, 512 * hf:512 * hf + 512], start=(f == 0), stop=(f == FC - 1))
                    if hf == 0:
                        last.then_inc(done, 1)
                last.then_inc(freed, 1)

            def step_hidden(e, k, turn):
                pe.wait_ge(exp_in[k], turn * 48 + 48)
                pe.wait_ge(S["hx"], e + 1)
                if not (isinstance(e, int) and e < 2):
                    pe.wait_ge(S["hid"], e * 4 - 4)
                block_hidden(k, k % 2, S["h_mm"])

            def step_out(e, k):
                pe.wait_ge(S["hid_t"], e + 1)
                if not (isinstance(e, int) and e < 2):
                    pe.wait_ge(S["y_ev_a"], e - 1)
                    pe.wait_ge(S["y_ev_v"], e - 1)
                block_out(k, k % 2, S["y_mm"], exp_free[k])

            def step_turn(e, k):
                pe.wait_ge(S["hid"], e * 4 + 4)
                if not (isinstance(e, int) and e < 1):
                    pe.wait_ge(S["hid_t"], e)
                block_turn(k % 2)

            step_hidden(0, 0, 0)
            for e in range(1, 4):
                step_hidden(e, e, 0)
                if e == 1:
                    step_turn(0, 0)
                step_out(e - 1, e - 1)
                step_turn(e, e)
            with pe.Fori(0, NE // ES - 1) as turn:
                for k in range(ES):
                    e = turn * ES + ES + k
                    step_hidden(e, k, turn + 1)
                    step_out(e - 1, (k - 1) % ES)
                    step_turn(e, k)
            step_out(NE - 1, ES - 1)
            pe.wait_ge(S["y_ev_a"], NE)
            pe.wait_ge(S["y_ev_v"], NE)
            nov = pe.value_load(nov_i[0:1, 0:1], min_val=0, max_val=MAXOV)
            with pe.If(nov > 0):
                with pe.Fori(0, nov) as i:
                    pe.wait_ge(S["ov_in"], i * 48 + 48)
                    pe.wait_ge(S["ov_hx"], i + 1)
                    block_hidden(0, 0, S["ov_h"])
                    pe.wait_ge(S["ov_hid"], i * 4 + 4)
                    block_turn(0)
                    pe.wait_ge(S["hid_t"], i + NE + 1)
                    pe.wait_ge(S["y_ev_a"], i + NE)
                    pe.wait_ge(S["y_ev_v"], i + NE)
                    block_out(0, 0, S["ov_y"], exp_free[0])


_INS = ['x_prompt', 'x_sample', 'cache_fox_k', 'cache_fox_v', 'cache_fox_logf', 'cache_moba_k', 'cache_moba_v',
        'page_table', 'c_prompt', 'c_sample', 'w_ada', 'b_ada', 'g_attn', 'w_in', 'b_forget', 'g_out_fox',
        'g_out_moba', 't5_bias', 'w_out', 'g_ffn', 'w_router_group', 'b_router_group', 'w_router_expert',
        'b_router_expert', 'w1', 'w3', 'w2', 'g_final']
_CONSTS = [('consts', make_constants), ('dist_onehot', make_distance_onehot), ('seq_onehot', make_sequence_onehot)]
_OUTS = [(1, NP, D), (NB, NQ, D),
         (1, 1, NP, H, HD), (1, 1, NP, H, HD), (1, 1, NP, H), (1, 1, NP, H, HD), (1, 1, NP, H, HD),
         (1, NB, NQ, H, HD), (1, NB, NQ, H, HD), (1, NB, NQ, H), (1, NB, NQ, H, HD), (1, NB, NQ, H, HD)]


def kernel(**inputs):
    import concourse.bacc as bacc
    from concourse.bass_utils import run_bass_kernel_spmd

    arrays = {n: np.ascontiguousarray(inputs[n]) for n in _INS}
    arrays.update({n: make() for n, make in _CONSTS})
    nc = bacc.Bacc("TRN2", target_bir_lowering=False, num_devices=1)
    ins = [nc.dram_tensor(n, a.shape, mybir.dt.from_np(a.dtype), kind="ExternalInput").ap()
           for n, a in arrays.items()]
    outs = [nc.dram_tensor(f"out_{i}", s, F32, kind="ExternalOutput").ap() for i, s in enumerate(_OUTS)]
    trunk_kernel(nc, ins, outs)
    r = run_bass_kernel_spmd(nc, [arrays], core_ids=[0])
    return tuple(r.results[0][f"out_{i}"] for i in range(len(_OUTS)))
```
